# Optimizing a Trainium2 kernel written in Bass

```python
import math
import jax, jax.numpy as jnp
from jax import lax
import numpy as np

D_MODEL = 1024
BATCH = 1
SEQ = 256
DEPTH = 1
DEC_BATCH = 8
DEC_SEQ = 8
PAST_LEN = 2048
PAGE_SIZE = 128

HEAD_DIM = 64
N_ATTN_HEADS = 12
D_ATTN = N_ATTN_HEADS * HEAD_DIM
D_CONV = D_MODEL - D_ATTN
CONV_WIDTH = 3
BRANCHES = ((128, 1), (512, 4), (2048, 16))
W_MAX = 2048
Q_BLOCK = 128
NUM_BUCKETS = 32
MAX_DISTANCE = 2048
N_EXPERTS = 32
TOP_K = 4
D_FF = D_MODEL
SWIGLU_LIMIT = 7.0
SWIGLU_ALPHA = 1.702
EXPERT_BLOCK = 128
DEEPNORM_ALPHA = (2 * DEPTH) ** 0.25
DEEPNORM_BETA = (8 * DEPTH) ** -0.25
LN_EPS = 1e-5
RMS_EPS = 1e-6
NEG_INF = -1e30
D_IN = 3 * D_ATTN + 3 * D_CONV
SPLITS = [D_ATTN, 2 * D_ATTN, 3 * D_ATTN, 3 * D_ATTN + D_CONV, 3 * D_ATTN + 2 * D_CONV]

kernel_name = 'hymba_dilated_conv_moe_step'

def layer_norm(x, g, b):
    xf = x.astype(jnp.float32)
    mu = jnp.mean(xf, axis=-1, keepdims=True)
    var = jnp.mean(jnp.square(xf - mu), axis=-1, keepdims=True)
    y = (xf - mu) * lax.rsqrt(var + LN_EPS)
    return (y * g.astype(jnp.float32) + b.astype(jnp.float32)).astype(x.dtype)

def rms_norm(x, g):
    xf = x.astype(jnp.float32)
    y = xf * lax.rsqrt(jnp.mean(jnp.square(xf), axis=-1, keepdims=True) + RMS_EPS)
    return (y * g.astype(jnp.float32)).astype(x.dtype)

def t5_bucket(dist):
    max_exact = NUM_BUCKETS // 2
    df = jnp.maximum(dist, max_exact).astype(jnp.float32)
    large = max_exact + (jnp.log(df / max_exact) / math.log(MAX_DISTANCE / max_exact)
                         * (NUM_BUCKETS - max_exact)).astype(jnp.int32)
    return jnp.where(dist < max_exact, dist, jnp.minimum(large, NUM_BUCKETS - 1))

def softmax_stats(logits, valid):
    logits = jnp.where(valid, logits, NEG_INF)
    m = jnp.max(logits, axis=-1, keepdims=True)
    p = jnp.exp(logits - m)
    s = jnp.sum(p, axis=-1, keepdims=True)
    return p, s[..., 0], (m + jnp.log(s))[..., 0]

def merge_branches(outs, lses):
    w = jax.nn.softmax(jnp.stack(lses, axis=0), axis=0)
    return jnp.sum(w[..., None] * jnp.stack(outs, axis=0), axis=0)

def dilated_attention_prompt(q, k, v, rel_bias):
    bsz, seq = q.shape[:2]
    pad = ((0, 0), (W_MAX, 0), (0, 0), (0, 0))
    kp = jnp.pad(k, pad)
    vp = jnp.pad(v, pad)
    scale = HEAD_DIM ** -0.5

    def one_block(t0):
        qb = lax.dynamic_slice_in_dim(q, t0, Q_BLOCK, axis=1)
        outs, lses = [], []
        for w, d in BRANCHES:
            nq, nk, nj = Q_BLOCK // d, (w + Q_BLOCK) // d, w // d
            start = t0 + W_MAX - w
            ks = lax.dynamic_slice_in_dim(kp, start, w + Q_BLOCK, axis=1).reshape(bsz, nk, d, N_ATTN_HEADS, HEAD_DIM)
            vs = lax.dynamic_slice_in_dim(vp, start, w + Q_BLOCK, axis=1).reshape(bsz, nk, d, N_ATTN_HEADS, HEAD_DIM)
            qs = qb.reshape(bsz, nq, d, N_ATTN_HEADS, HEAD_DIM)
            step = nj + jnp.arange(nq)[:, None] - jnp.arange(nk)[None, :]
            key_pos = t0 - w + jnp.arange(nk)[None, :] * d + jnp.arange(d)[:, None]
            valid = ((step >= 0) & (step <= nj))[None, :, :] & (key_pos >= 0)[:, None, :]
            bias = rel_bias[t5_bucket(jnp.clip(step, 0, nj) * d)]
            logits = jnp.einsum('bqrhe,bkrhe->bhrqk', qs, ks).astype(jnp.float32) * scale
            logits = logits + jnp.transpose(bias, (2, 0, 1)).astype(jnp.float32)[None, :, None]
            p, s, lse = softmax_stats(logits, valid[None, None])
            o = jnp.einsum('bhrqk,bkrhe->bqrhe', p, vs.astype(jnp.float32))
            s = jnp.transpose(s, (0, 3, 2, 1))
            outs.append((o / s[..., None]).reshape(bsz, Q_BLOCK, N_ATTN_HEADS, HEAD_DIM))
            lses.append(jnp.transpose(lse, (0, 3, 2, 1)).reshape(bsz, Q_BLOCK, N_ATTN_HEADS))
        return merge_branches(outs, lses)

    starts = jnp.arange(seq // Q_BLOCK, dtype=jnp.int32) * Q_BLOCK
    o = lax.map(one_block, starts)
    return jnp.transpose(o, (1, 0, 2, 3, 4)).reshape(bsz, seq, N_ATTN_HEADS, HEAD_DIM).astype(q.dtype)

def dilated_attention_sample(q, k_new, v_new, cache_k, cache_v, rel_bias):
    n_past, n_new = cache_k.shape[1], q.shape[1]
    kc = jnp.concatenate([cache_k, k_new.astype(cache_k.dtype)], axis=1)
    vc = jnp.concatenate([cache_v, v_new.astype(cache_v.dtype)], axis=1)
    scale = HEAD_DIM ** -0.5
    outs, lses = [], []
    for w, d in BRANCHES:
        nj = w // d
        j = jnp.arange(nj + 1)
        idx = n_past + jnp.arange(n_new)[:, None] - j[None, :] * d
        valid = idx >= 0
        kg = kc[:, jnp.maximum(idx, 0)]
        vg = vc[:, jnp.maximum(idx, 0)]
        bias = rel_bias[t5_bucket(j * d)]
        logits = jnp.einsum('bthe,btjhe->bhtj', q, kg).astype(jnp.float32) * scale
        logits = logits + jnp.transpose(bias).astype(jnp.float32)[None, :, None, :]
        p, s, lse = softmax_stats(logits, valid[None, None])
        o = jnp.einsum('bhtj,btjhe->bthe', p, vg.astype(jnp.float32)) / jnp.transpose(s, (0, 2, 1))[..., None]
        outs.append(o)
        lses.append(jnp.transpose(lse, (0, 2, 1)))
    return merge_branches(outs, lses).astype(q.dtype)

def short_conv(z, z_past, conv_w):
    zp = jnp.concatenate([z_past.astype(z.dtype), z], axis=1)
    n = z.shape[1]
    y = conv_w[0] * zp[:, 0:n]
    for i in range(1, CONV_WIDTH):
        y = y + conv_w[i] * zp[:, i:i + n]
    return y, zp[:, -(CONV_WIDTH - 1):]

def moe(u, router_w, router_b, w_up, b_up, w_down, b_down):
    bsz, n, dm = u.shape
    n_tok = bsz * n
    xf = u.reshape(n_tok, dm)
    logits = (xf @ router_w + router_b).astype(jnp.float32)
    top_val, top_idx = lax.top_k(logits, TOP_K)
    gates = jax.nn.softmax(top_val, axis=-1)
    nk = n_tok * TOP_K
    flat_e = top_idx.reshape(-1)
    flat_tok = jnp.repeat(jnp.arange(n_tok, dtype=jnp.int32), TOP_K)
    flat_g = gates.reshape(-1)
    order = jnp.argsort(flat_e)
    sorted_e, sorted_tok, sorted_g = flat_e[order], flat_tok[order], flat_g[order]
    counts = jnp.zeros((N_EXPERTS,), jnp.int32).at[flat_e].add(1)
    padded = ((counts + EXPERT_BLOCK - 1) // EXPERT_BLOCK) * EXPERT_BLOCK
    starts = jnp.cumsum(counts) - counts
    pad_ends = jnp.cumsum(padded)
    pad_starts = pad_ends - padded
    dest = pad_starts[sorted_e] + jnp.arange(nk, dtype=jnp.int32) - starts[sorted_e]
    n_rows = (-(-nk // EXPERT_BLOCK) + N_EXPERTS) * EXPERT_BLOCK
    buf_tok = jnp.full((n_rows,), n_tok, jnp.int32).at[dest].set(sorted_tok)
    buf_g = jnp.zeros((n_rows,), jnp.float32).at[dest].set(sorted_g)
    n_blocks = n_rows // EXPERT_BLOCK
    blk_e = jnp.minimum(jnp.searchsorted(pad_ends, jnp.arange(n_blocks, dtype=jnp.int32) * EXPERT_BLOCK, side='right'),
                        N_EXPERTS - 1)
    x_pad = jnp.concatenate([xf, jnp.zeros((1, dm), xf.dtype)], axis=0)
    xb = x_pad[buf_tok].reshape(n_blocks, EXPERT_BLOCK, dm)

    def expert_block(args):
        xblk, e = args
        hcat = xblk @ w_up[e] + b_up[e]
        x_glu, x_lin = hcat[:, :D_FF], hcat[:, D_FF:]
        x_glu = jnp.minimum(x_glu, SWIGLU_LIMIT)
        x_lin = jnp.clip(x_lin, -SWIGLU_LIMIT, SWIGLU_LIMIT)
        a = x_glu * jax.nn.sigmoid(SWIGLU_ALPHA * x_glu) * (x_lin + 1)
        return a @ w_down[e] + b_down[e]

    yb = lax.map(expert_block, (xb, blk_e)).reshape(n_rows, dm)
    y = jnp.zeros((n_tok + 1, dm), jnp.float32).at[buf_tok].add(yb.astype(jnp.float32) * buf_g[:, None])[:n_tok]
    return y.astype(u.dtype).reshape(bsz, n, dm)

def hybrid_layer(x, c, conv_past, cache_k, cache_v, w_ada, b_ada, w_in, conv_w, norm_attn_g, norm_conv_g, w_o,
                 ln1_g, ln1_b, rel_bias, router_w, router_b, w_up, b_up, w_down, b_down, ln2_g, ln2_b):
    bsz, n = x.shape[:2]
    ada = jax.nn.silu(c) @ w_ada + b_ada
    shift1, scale1, gate1, shift2, scale2, gate2 = jnp.split(ada[:, None, :], 6, axis=-1)
    u = x * (1 + scale1) + shift1
    proj = u @ w_in
    q, k, v, gb, gc, h = jnp.split(proj, SPLITS, axis=-1)
    q = q.reshape(bsz, n, N_ATTN_HEADS, HEAD_DIM)
    k = k.reshape(bsz, n, N_ATTN_HEADS, HEAD_DIM)
    v = v.reshape(bsz, n, N_ATTN_HEADS, HEAD_DIM)
    if cache_k is None:
        o = dilated_attention_prompt(q, k, v, rel_bias)
    else:
        o = dilated_attention_sample(q, k, v, cache_k, cache_v, rel_bias)
    attn = rms_norm(o.reshape(bsz, n, D_ATTN), norm_attn_g)
    yc, conv_state = short_conv(gc * h, conv_past, conv_w)
    conv = rms_norm(gb * yc, norm_conv_g)
    mix = jnp.concatenate([attn, conv], axis=-1) @ w_o
    x = layer_norm(DEEPNORM_ALPHA * x + (1 + gate1) * mix, ln1_g, ln1_b)
    u2 = x * (1 + scale2) + shift2
    ffn = moe(u2, router_w, router_b, w_up, b_up, w_down, b_down)
    x = layer_norm(DEEPNORM_ALPHA * x + (1 + gate2) * ffn, ln2_g, ln2_b)
    return x, k, v, conv_state

def setup_inputs(seed: int = 0) -> dict:
    key = jax.random.key(seed)
    ks = jax.random.split(key, 32)
    f32 = jnp.float32

    def nrm(k, shape, s):
        return s * jax.random.normal(k, shape, f32)

    n_keep = min(W_MAX, PAST_LEN)
    dm = D_MODEL
    return {
        'x_prompt': nrm(ks[0], (BATCH, SEQ, dm), 1.0),
        'x_sample': nrm(ks[1], (DEC_BATCH, DEC_SEQ, dm), 1.0),
        'cache_k': nrm(ks[2], (DEPTH, DEC_BATCH, n_keep, N_ATTN_HEADS, HEAD_DIM), 1.0),
        'cache_v': nrm(ks[3], (DEPTH, DEC_BATCH, n_keep, N_ATTN_HEADS, HEAD_DIM), 1.0),
        'state_conv': nrm(ks[4], (DEPTH, DEC_BATCH, CONV_WIDTH - 1, D_CONV), 1.0),
        'c_prompt': nrm(ks[5], (BATCH, dm), 1.0),
        'c_sample': nrm(ks[6], (DEC_BATCH, dm), 1.0),
        'w_ada': nrm(ks[7], (DEPTH, dm, 6 * dm), 0.2 * dm ** -0.5),
        'b_ada': nrm(ks[8], (DEPTH, 6 * dm), 0.01),
        'w_in': nrm(ks[9], (DEPTH, dm, D_IN), dm ** -0.5),
        'conv_w': nrm(ks[10], (DEPTH, CONV_WIDTH, D_CONV), CONV_WIDTH ** -0.5),
        'norm_attn_g': 1.0 + nrm(ks[11], (DEPTH, D_ATTN), 0.1),
        'norm_conv_g': 1.0 + nrm(ks[12], (DEPTH, D_CONV), 0.1),
        'w_o': nrm(ks[13], (DEPTH, dm, dm), DEEPNORM_BETA * dm ** -0.5),
        'ln1_g': 1.0 + nrm(ks[14], (DEPTH, dm), 0.1),
        'ln1_b': nrm(ks[15], (DEPTH, dm), 0.01),
        'rel_bias': nrm(ks[16], (NUM_BUCKETS, N_ATTN_HEADS), 0.5),
        'router_w': nrm(ks[17], (DEPTH, dm, N_EXPERTS), dm ** -0.5),
        'router_b': nrm(ks[18], (DEPTH, N_EXPERTS), 0.01),
        'w_up': nrm(ks[19], (DEPTH, N_EXPERTS, dm, 2 * D_FF), dm ** -0.5),
        'b_up': nrm(ks[20], (DEPTH, N_EXPERTS, 2 * D_FF), 0.01),
        'w_down': nrm(ks[21], (DEPTH, N_EXPERTS, D_FF, dm), DEEPNORM_BETA * D_FF ** -0.5),
        'b_down': nrm(ks[22], (DEPTH, N_EXPERTS, dm), 0.01),
        'ln2_g': 1.0 + nrm(ks[23], (DEPTH, dm), 0.1),
        'ln2_b': nrm(ks[24], (DEPTH, dm), 0.01),
    }

def reference(x_prompt, x_sample, cache_k, cache_v, state_conv, c_prompt, c_sample, w_ada, b_ada, w_in, conv_w,
              norm_attn_g, norm_conv_g, w_o, ln1_g, ln1_b, rel_bias, router_w, router_b, w_up, b_up, w_down, b_down,
              ln2_g, ln2_b):
    xp, xs = x_prompt, x_sample
    n_keep = min(W_MAX, x_prompt.shape[1])
    kp_l, vp_l, cp_l, ks_l, vs_l, cs_l = [], [], [], [], [], []
    for l in range(DEPTH):
        weights = (w_ada[l], b_ada[l], w_in[l], conv_w[l], norm_attn_g[l], norm_conv_g[l], w_o[l], ln1_g[l], ln1_b[l],
                   rel_bias, router_w[l], router_b[l], w_up[l], b_up[l], w_down[l], b_down[l], ln2_g[l], ln2_b[l])
        conv0 = jnp.zeros((xp.shape[0], CONV_WIDTH - 1, D_CONV), xp.dtype)
        xp, k, v, cst = hybrid_layer(xp, c_prompt, conv0, None, None, *weights)
        kp_l.append(k[:, -n_keep:])
        vp_l.append(v[:, -n_keep:])
        cp_l.append(cst)
        xs, k, v, cst = hybrid_layer(xs, c_sample, state_conv[l], cache_k[l], cache_v[l], *weights)
        ks_l.append(k)
        vs_l.append(v)
        cs_l.append(cst)
    return (xp, xs, jnp.stack(kp_l), jnp.stack(vp_l), jnp.stack(cp_l), jnp.stack(ks_l), jnp.stack(vs_l), jnp.stack(cs_l))


_drawn_inputs = setup_inputs


def setup_inputs(seed=0):
    import zlib

    import numpy as np

    out = dict(_drawn_inputs(seed))
    spreads = {}
    factors = {'router_b': 2.753, 'b_up': 8.0, 'b_down': 8.0, 'ln2_b': 5.71}
    for name, (base, spread) in spreads.items():
        noise = np.random.default_rng([zlib.crc32(name.encode()), seed]).standard_normal(out[name].shape)
        drawn = base * np.exp(spread * noise) if base else spread * noise
        out[name] = __import__('jax').numpy.asarray(drawn.astype(out[name].dtype))
    for name, factor in factors.items():
        out[name] = (out[name] * factor).astype(out[name].dtype)
    return out
```

```python
import concourse.bass as bass
from concourse import mybir
from contextlib import ExitStack

D = 1024
KC = D // 128
NE = 32
FF = 1024
HEADS, HD = 12, 64
DA, DC = HEADS * HD, 256
AC, CC = DA // 128, DC // 128
SEQ, NB, NS = 256, 8, 8
NTOK = SEQ + NB * NS
PAST = 2048
REC, OLD = 512, 768
KB = (REC + OLD) // 128
NCACHE = REC + OLD
WIN = 2 * NB * NS - NS
SB = NCACHE + WIN
TILES = [(0, 128), (128, 128), (256, 64)]
ALPHA = 2.0 ** 0.25
LN_EPS, RMS_EPS = 1e-5, 1e-6
ROUNDS = 3
ITEMS = ROUNDS * NE
FAR = 1000.0

F32, I32, U32 = mybir.dt.float32, mybir.dt.int32, mybir.dt.uint32
ALU = mybir.AluOpType
ACT = mybir.ActivationFunctionType
AX = mybir.AxisListType

CONSTS = {}


def lay_consts():
    at = 0
    for name, n in (("ident", 128), ("tri", 128), ("iota", 128), ("ones", 128), ("rep_p", 128), ("rep_s", 64)):
        CONSTS[name] = (at, n)
        at += n
    return at


NCONST = lay_consts()


class Chain:

    def __init__(self, eng, sem):
        self.eng, self.sem, self.n, self.before, self.off = eng, sem, 0, 0, 0

    def __call__(self, ins):
        ins.then_inc(self.sem, 1)
        self.n += 1
        self.eng.wait_ge(self.sem, self.n + self.off)

    def enter(self, i, per):
        self.start, self.per = self.n, per
        self.off = i * per + self.before

    def leave(self, turns):
        assert self.n - self.start == self.per, (self.n - self.start, self.per)
        self.n = self.start
        self.before = turns * self.per + self.before
        self.off = self.before


def layer_kernel(nc, t, out, scratch):
    ctx = ExitStack()
    with ctx:
        def sem(name):
            return ctx.enter_context(nc.semaphore(name))

        TOTAL = 53200
        arena = ctx.enter_context(nc.sbuf_tensor("arena", [128, TOTAL], F32))
        ps = ctx.enter_context(nc.psum_tensor("ps", [128, 4096], F32))

        def view(at, *dims):
            n = 1
            for d in dims:
                n *= d
            assert at + n <= TOTAL, (at, n)
            v = arena[:, at:at + n]
            if len(dims) == 2:
                v = v.rearrange("p (a b) -> p a b", a=dims[0])
            elif len(dims) == 3:
                v = v.rearrange("p (a b c) -> p a b c", a=dims[0], b=dims[1])
            return v

        def bank(b, a=0, z=512):
            return ps[:, 512 * b + a:512 * b + z]

        W = 0
        up_w = view(W, KC, 2 * FF)
        dn_w = view(W + KC * 2 * FF, KC, D)
        ADA_SLOTS = 3
        ada_w = view(W, ADA_SLOTS, 6 * D)
        XW = W + ADA_SLOTS * 6 * D
        x_in = view(XW, 3, D)
        sig_c = view(XW + 3 * D, D)
        rows = view(XW + 4 * D, DC)
        g_rows = view(XW + 4 * D + DC, 128)
        win_w = view(W, KC, 3 * D)
        KX = W
        k_sb = view(KX, KB, DA)
        VX = KX + KB * DA
        v_sb = view(VX, KB, DA)
        KTX = VX + KB * DA
        kt_sb = view(KTX, AC, NCACHE)
        hot_s = view(KTX, 2, SB)
        log_s = view(KTX + 2 * SB, SB)
        MX = KTX + AC * NCACHE
        head_mask = view(MX, 256)
        query_sum = view(MX + 256, 3, 8)
        assert MX + 280 <= 24576

        P = 24576
        consts = view(P, NCONST)
        P += NCONST
        ada_sb = view(P, 3, 512)
        P += 1536
        rows_t = view(P, 2, 32); P += 64
        g_attn = view(P, 8); P += 8
        z_last = view(P, 2, 18); P += 36
        z_nat = view(P, DC); P += 256
        rw_sb = view(P, KC, NE); P += 256
        rb_sb = view(P, NE); P += 32
        relb = view(P, 12); P += 12
        bias_sel = view(P, 2, 96); P += 192
        log_sel = view(P, 96); P += 96
        rank_t = view(P, 3, ITEMS + 1); P += 3 * (ITEMS + 1)
        gate_t = view(P, 3, ITEMS + 1); P += 3 * (ITEMS + 1)
        mask_t = view(P, 3, NE); P += 96
        lg = view(P, NE); P += NE
        ex = view(P, NE); P += NE
        flag_f = z_nat[:, 0:ITEMS + 2]
        flag_i = view(P, ITEMS + 2).bitcast(I32); P += ITEMS + 2
        cnt = view(P, NE); P += NE
        st = view(P, 96); P += 96
        idx_u = view(P, 8).bitcast(U32); P += 8
        idx_f = view(P, 8); P += 8
        lead = view(P, 8); P += 8
        R1, R2 = P, P + 3072
        R3 = R2 + 3072
        R4 = R3 + 8192
        R5 = R4 + 6144
        R6 = R5 + 1316 + 640
        assert R6 + 1920 <= TOTAL, R6 + 1920

        ident = consts[:, 0:128]
        tri = consts[:, 128:256]
        iota = consts[:, 256:384]
        ones = consts[:, 384:512]
        rep_p = consts[:, 512:640]
        rep_s = consts[:, 640:704]

        hb = view(R1, HEADS, 256)
        s_bias = view(R1, SB)
        p_soft = view(R1 + SB, 2, 384)
        p_turn = view(R1 + SB + 768, 2, 384)
        prob = view(R1 + SB, NCACHE + 64)
        x1 = view(R1, 3, D)
        p_bias = view(R2, HEADS, 256)
        pt_sb = view(R2, KB + 1, 96)
        qbd = view(R2 + (KB + 1) * 96, AC, 32)
        o_mask = view(R2 + (KB + 1) * 96 + AC * 32, 256)
        u2 = view(R2, 3, D)
        u_t = view(R3, KC, NTOK)
        k_nat = view(R3 + 2560, 3, DA)
        b_rows = view(R3 + 4864, 3, 512)
        c_sb = view(R3 + 6400, D)
        ada_t = view(R3 + 7424, 4, 128)
        c_t = view(R3 + 7936, KC, 32)
        wo_sb = view(R3, KC, D)
        acc = view(R3, 3, D)
        act_g = view(R3 + 3072, 2, 512)
        act_s = view(R3 + 4096, 2, 512)
        act_l = view(R3 + 5120, 2, 512)
        b_up = view(R3 + 6144, 2 * FF)
        fin_t = view(R3 + 3072, D)
        fin_y = view(R3 + 4096, 3, D)
        q_t = view(R4, AC, NTOK)
        k_t = view(R4 + 1920, AC, NTOK)
        v_nat = view(R4 + 3840, 3, DA)
        mix = view(R4, D)
        u2_t = view(R4 + D, KC, 128)
        ln1 = view(R4 + 2 * D, 2, D)
        sq_c = view(R4 + 4 * D, CC, 128)
        xe_t = view(R4, KC, 128)
        a_t = view(R4 + 1024, 2, 512)
        y_sb = view(R4 + 2048, 2, 512)
        sel = view(R4 + 3072, 3, 128)
        sel_g = view(R4 + 3456, 3, 4, 64)
        sel_t = view(R4 + 4224, 2, 384)
        z_p = view(R5, 2, SEQ + 2)
        z_s = view(R5 + 516, 2, 80)
        c_gate = view(R5 + 676, 2, NTOK)
        y_c = view(R5 + 1316, 2, NTOK)
        sq_a = view(R5, AC, 128)
        o_t = view(R6, AC, NTOK)
        tab_hot = view(R6, 384)
        tab_log = view(R6 + 384, 384)
        tab_sb = view(R6 + 768, 384)
        anti = view(R6 + 1152, 128)
        ln2 = view(R5, 2, D)
        bd_sb = view(R5 + 2 * D, D)
        gt_sb = view(R5 + 3 * D, NTOK)

        wada_d = t["w_ada"][0].rearrange("(k p) n -> k p n", p=128)
        win_d = t["w_in"][0].rearrange("(k p) n -> k p n", p=128)
        wo_d = t["w_o"][0].rearrange("(k p) n -> p k n", p=128)
        wup_d = t["w_up"][0].rearrange("e (k p) n -> e k p n", p=128)
        wdn_d = t["w_down"][0].rearrange("e (m k p) n -> e m p k n", p=128, k=2)
        ck = t["cache_k"][0].rearrange("b s h e -> b s (h e)")
        cv = t["cache_v"][0].rearrange("b s h e -> b s (h e)")

        ada_in = [sem(f"ada_in{s}") for s in range(ADA_SLOTS)]
        ada_used, win_in, hot_in, k_rec_in, k_old_in, v_in, wo_in = map(
            sem, ("ada_used", "win_in", "hot_in", "k_rec_in", "k_old_in", "v_in", "wo_in"))
        up_in = [sem(f"up_in{k}") for k in range(KC)]
        dn_in = [sem(f"dn_in{m}") for m in range(KC // 2)]
        bup_in, bup_used, up_used, dn_used = map(sem, ("bup_in", "bup_used", "up_used", "dn_used"))
        const_in, c_in, rows_in, bada_in, x_ready, tabc_in = map(
            sem, ("const_in", "c_in", "rows_in", "bada_in", "x_ready", "tabc_in"))
        zeroed, sig_done, c_ready, ct_done, ct_ready, rows_done, rows_ready = map(
            sem, ("zeroed", "sig_done", "c_ready", "ct_done", "ct_ready", "rows_done", "rows_ready"))
        xt_done, xt_copied, ada_ready, adat_done, u_ready = map(
            sem, ("xt_done", "xt_copied", "ada_ready", "adat_done", "u_ready"))
        tab_done, tab_ready, scr_out, hb_in, pb_done, pb_ready = map(
            sem, ("tab_done", "tab_ready", "scr_out", "hb_in", "pb_done", "pb_ready"))
        proj_done, proj_act, proj_dve = map(sem, ("proj_done", "proj_act", "proj_dve"))
        kn_done, kn_dve, kn_act, zl_ready, zn_done, zn_ready = map(
            sem, ("kn_done", "kn_dve", "kn_act", "zl_ready", "zn_done", "zn_ready"))
        out_kv, out_y = sem("out_kv"), sem("out_y")
        sb_done, sb_ready, bsel_ready = sem("sb_done"), sem("sb_ready"), sem("bsel_ready")
        ps_done, pmax_ready, pexp_ready, pnorm_ready, pt_done, pt_copied, pv_done, po_copied = map(
            sem, ("ps_done", "pmax_ready", "pexp_ready", "pnorm_ready", "pt_done", "pt_copied", "pv_done", "po_copied"))
        qbd_ready, kt_done, kt_dve, kt_act, s_done, s_max, s_exp, st_done, st_act, st_dve = map(
            sem, ("qbd_ready", "kt_done", "kt_dve", "kt_act", "s_done", "s_max", "s_exp", "st_done", "st_act", "st_dve"))
        k_used, v_used, sv_done, om_ready, so_done, so_copied = map(
            sem, ("k_used", "v_used", "sv_done", "om_ready", "so_done", "so_copied"))
        tail_in, sq_ready, og_ready, ss_done, var_ready, sd_ready, wo_done, g1_done, c2_done = map(
            sem, ("tail_in", "sq_ready", "og_ready", "ss_done", "var_ready", "sd_ready", "wo_done", "g1_done", "c2_done"))
        mixed, gated, u2_ready, u2t_done, u2t_ready, lg_done, neg_ready, ex_ready, masks_ready = map(
            sem, ("mixed", "gated", "u2_ready", "u2t_done", "u2t_ready", "lg_done", "neg_ready", "ex_ready", "masks_ready"))
        rank_done, route_ready, gt_done, gt_ready, bd_done, acc_ready, late_in, ln2_in = map(
            sem, ("rank_done", "route_ready", "gt_done", "gt_ready", "bd_done", "acc_ready", "late_in", "ln2_in"))
        sel_ready, selg_ready, y_ready = sem("sel_ready"), sem("selg_ready"), sem("y_ready")
        g_ready, sig_ready, a_ready, at_done, at_ready = (
            [sem(f"{name}_{v}") for v in "ab"] for name in ("g_ready", "sig_ready", "a_ready", "at_done", "at_ready"))
        ga_done, xe_ready, xe_act, selt_done, selt_ready, sc_done, sc_added = map(
            sem, ("ga_done", "xe_ready", "xe_act", "selt_done", "selt_ready", "sc_done", "sc_added"))
        g2_done, fin_mixed, y_done = sem("g2_done"), sem("fin_mixed"), sem("y_done")
        ch_v, ch_end = sem("vector_chain"), sem("vector_chain_at_the_end")

        UNITS = [("q", c, 128 * c, "act") for c in range(AC)]
        UNITS += [("k", c, DA + 128 * c, "dve") for c in range(AC)]
        for c in range(CC):
            UNITS += [("C", c, 3 * DA + DC + 128 * c, "act"), ("h", c, 3 * DA + 2 * DC + 128 * c, "dve")]
        UNITS += [("B", c, 3 * DA + 128 * c, "act") for c in range(CC)]
        for tt in range(3):
            UNITS += [("v", (tt, 0), 2 * DA, "act"), ("v", (tt, 1), 2 * DA + 384, "dve")]
        PB = 6

        def copied(u):
            return sum(1 for w in UNITS[:u + 1] if w[3] == UNITS[u][3])

        block = ctx.enter_context(nc.Block())

        @block.sync
        def _(sp):
            for k in range(KC):
                if k >= ADA_SLOTS:
                    sp.wait_ge(ada_used, k - ADA_SLOTS + 1)
                sp.dma_start(ada_w[:, k % ADA_SLOTS, :], wada_d[k]).then_inc(ada_in[k % ADA_SLOTS], 16)
            for k, last in ((4, 6), (5, 6), (0, 7), (1, 7), (2, 8), (3, 8), (6, 8), (7, 8)):
                sp.wait_ge(ada_used, last)
                sp.dma_start(win_w[:, k, :], win_d[k]).then_inc(win_in, 16)
            sp.wait_ge(proj_done, len(UNITS))
            sp.dma_start(hot_s, t["hot_s"].rearrange("(a p) n -> p a n", p=128)).then_inc(hot_in, 16)
            sp.dma_start(log_s[0:8, :], t["log_s"]).then_inc(hot_in, 16)
            sp.dma_start(head_mask[0:96, :], t["head_mask"]).then_inc(hot_in, 16)
            sp.dma_start(query_sum[0:96], t["query_sum"].rearrange("p (a b) -> p a b", a=3)).then_inc(hot_in, 16)
            with sp.Fori(0, NB) as b:
                for c_d, sb, used, rec_in, old_in in ((ck, k_sb, k_used, k_rec_in, k_old_in),
                                                      (cv, v_sb, v_used, v_in, v_in)):
                    sp.wait_ge(used, b + 1)
                    row = c_d[bass.ds(b, 1)]
                    sp.dma_start(sb[:, 0:4, :], row[:, PAST - REC:PAST, :].rearrange("o (p r) d -> (o p) r d", r=4)
                                 ).then_inc(rec_in, 16)
                    old = row[:, 0:PAST - REC, :].rearrange("o (r g i) d -> i (o g) r d", r=6, g=16)
                    for i in range(8):
                        sp.dma_start(sb[16 * i:16 * i + 16, 4:KB, :], old[i]).then_inc(old_in, 16)
            sp.wait_ge(out_kv, 96)
            sp.dma_start(wo_sb, wo_d).then_inc(wo_in, 16)

            def load_expert(e, slot_free):
                if slot_free is not None:
                    sp.wait_ge(bup_used, slot_free)
                sp.dma_start(b_up[0:1, :], t["b_up"][0, bass.ds(e, 1), :]).then_inc(bup_in, 16)

            sp.wait_ge(v_used, NB + 1)
            sp.wait_ge(so_copied, NB)
            for k in range(KC):
                sp.dma_start(up_w[:, k, :], wup_d[0, k]).then_inc(up_in[k], 16)
            for m in range(KC // 2):
                sp.dma_start(dn_w[:, 2 * m:2 * m + 2, :], wdn_d[0, m]).then_inc(dn_in[m], 16)
            sp.wait_ge(route_ready, 1)
            load_expert(0, None)
            items = sp.value_load(flag_i[0:1, 0:1], min_val=NE, max_val=ITEMS)
            with sp.Fori(1, items) as i:
                e = i % NE
                load_expert(e, i)
                for k in range(KC):
                    sp.wait_ge(up_used, (i - 1) * KC + k + 1)
                    sp.dma_start(up_w[:, k, :], wup_d[bass.ds(e, 1), k].rearrange("o p n -> (o p) n")
                                 ).then_inc(up_in[k], 16)
                for m in range(KC // 2):
                    sp.wait_ge(dn_used, (i - 1) * (KC // 2) + m + 1)
                    sp.dma_start(dn_w[:, 2 * m:2 * m + 2, :], wdn_d[bass.ds(e, 1), m].rearrange(
                        "o p k n -> (o p) k n")).then_inc(dn_in[m], 16)
            sp.wait_ge(y_done, 2)
            sp.dma_start(out[0][0].rearrange("(a p) d -> p a d", p=128), fin_y[:, 0:2, :]).then_inc(out_y, 16)
            sp.wait_ge(y_done, 3)
            sp.dma_start(out[1].rearrange("b s d -> (b s) d"), fin_y[0:64, 2, :]).then_inc(out_y, 16)
            sp.wait_ge(out_y, 32)

        @block.gpsimd
        def _(pool):
            pool.wait_ge(tab_ready, 1)
            pool.dma_start(scratch, tab_sb[0:HEADS, :]).then_inc(scr_out, 16)
            pool.wait_ge(scr_out, 16)
            pool.dma_start(hb, bass.AP(scratch.tensor, 0, [[1, 128], [384, HEADS], [1, 256]])).then_inc(hb_in, 16)
            pool.wait_ge(kn_dve, 3)
            pool.wait_ge(kn_act, 3)
            pool.dma_start(out[2][0, 0].rearrange("(a p) h e -> p a (h e)", p=128), k_nat[:, 0:2, :]).then_inc(out_kv, 16)
            pool.dma_start(out[5][0].rearrange("b s h e -> (b s) (h e)"), k_nat[0:64, 2, :]).then_inc(out_kv, 16)
            pool.wait_ge(proj_act, copied(len(UNITS) - 2))
            pool.wait_ge(proj_dve, copied(len(UNITS) - 1))
            pool.dma_start(out[3][0, 0].rearrange("(a p) h e -> p a (h e)", p=128), v_nat[:, 0:2, :]).then_inc(out_kv, 16)
            pool.dma_start(out[6][0].rearrange("b s h e -> (b s) (h e)"), v_nat[0:64, 2, :]).then_inc(out_kv, 16)
            pool.wait_ge(zn_ready, 1)
            pool.dma_start(out[4][0, 0], z_nat[0:2, :]).then_inc(out_kv, 16)
            pool.dma_start(out[7][0].rearrange("b s c -> (b s) c"), z_nat[2:18, :]).then_inc(out_kv, 16)
            pool.wait_ge(out_kv, 96)
            pool.wait_ge(so_copied, NB)
            pool.dma_start(x1[:, 0:2, :], t["x_prompt"][0].rearrange("(a p) d -> p a d", p=128)).then_inc(tail_in, 16)
            pool.dma_start(x1[0:64, 2, :], t["x_sample"].rearrange("b s d -> (b s) d")).then_inc(tail_in, 16)
            for a, name in enumerate(("ln1_g", "ln1_b")):
                pool.dma_start(ln1[:, a, :], t[name][0:1, :].to_broadcast([128, D])).then_inc(tail_in, 16)
            pool.wait_ge(wo_done, 3)
            pool.wait_ge(mixed, 3)
            pool.dma_start(bd_sb[0:NE, :], t["b_down"][0]).then_inc(late_in, 16)
            for a, name in enumerate(("ln2_g", "ln2_b")):
                pool.dma_start(ln2[:, a, :], t[name][0:1, :].to_broadcast([128, D])).then_inc(ln2_in, 16)

        @block.scalar
        def _(act):
            act.dma_start(consts, t["consts"]).then_inc(const_in, 16)
            act.wait_ge(zeroed, 1)
            act.dma_start(c_sb[0:1, :], t["c_prompt"]).then_inc(c_in, 16)
            act.dma_start(c_sb[1:1 + NB, :], t["c_sample"]).then_inc(c_in, 16)
            act.dma_start(rows[0:16, :], t["state_conv"][0].rearrange("b i c -> (b i) c")).then_inc(rows_in, 16)
            act.dma_start(rows[16:19, :], t["conv_w"][0]).then_inc(rows_in, 16)
            act.dma_start(rows[19:20, :], t["norm_conv_g"]).then_inc(rows_in, 16)
            act.dma_start(g_rows[0:AC, :], t["norm_attn_g"].rearrange("o (c p) -> (o c) p", p=128)).then_inc(rows_in, 16)
            act.dma_start(x_in[:, 0:2, :], t["x_prompt"][0].rearrange("(a p) d -> p a d", p=128)).then_inc(x_ready, 16)
            act.dma_start(x_in[0:64, 2, :], t["x_sample"].rearrange("b s d -> (b s) d")).then_inc(x_ready, 16)
            for j in range(4):
                src = t["b_ada"].rearrange("o (m j c) -> j o m c", m=3, j=4)[j]
                act.dma_start(b_rows[32 * j:32 * j + 32], src.to_broadcast([32, 3, 512])).then_inc(bada_in, 16)
            act.dma_start(tab_hot[0:32, :], t["tab_hot"]).then_inc(tabc_in, 16)
            act.dma_start(tab_log[0:1, :], t["tab_log"]).then_inc(tabc_in, 16)
            for q in range(4):
                act.dma_start(relb[32 * q:32 * q + 32, :], t["rel_bias"]).then_inc(tabc_in, 16)
            act.dma_start(log_sel[0:8, :], t["log_sel"]).then_inc(tabc_in, 16)
            act.dma_start(anti, t["anti"]).then_inc(tabc_in, 16)
            act.dma_start(rw_sb, t["router_w"][0].rearrange("(k p) e -> p k e", p=128)).then_inc(tabc_in, 16)
            act.dma_start(rb_sb[0:1, :], t["router_b"]).then_inc(tabc_in, 16)
            act.wait_ge(c_in, 32)
            nc.scalar.activation(sig_c[0:32, :], c_sb[0:32, :], ACT.Sigmoid).then_inc(sig_done, 1)

            for u, (kind, c, _, eng) in enumerate(UNITS):
                if eng != "act":
                    continue
                act.wait_ge(proj_done, u + 1)
                src = bank(u % PB)
                if kind == "q":
                    ins = nc.scalar.mul(q_t[:, c, :], src[:, 0:NTOK], HD ** -0.5)
                elif kind == "C":
                    ins = nc.scalar.copy(c_gate[:, c, :], src[:, 0:NTOK])
                elif kind == "B":
                    ins = nc.scalar.copy(y_c[:, c, :], src[:, 0:NTOK])
                else:
                    n = TILES[c[0]][1]
                    ins = nc.scalar.copy(v_nat[0:n, c[0], 0:384], src[0:n, 0:384])
                ins.then_inc(proj_act, 1)
            for tt, (_, n) in enumerate(TILES):
                act.wait_ge(kn_done, tt + 1)
                nc.scalar.copy(k_nat[0:n, tt, 512:DA], bank(7)[0:n, 0:256]).then_inc(kn_act, 1)

            for s in range(HEADS + 2):
                if s < HEADS:
                    act.wait_ge(pmax_ready, s + 1)
                    for q, (a, z) in enumerate(((0, 128), (128, 384))):
                        ins = nc.scalar.activation(p_soft[:, s % 2, a:z], p_soft[:, s % 2, a:z], ACT.Exp,
                                                   bias=st[:, 4 * (s % 2) + 2 + q:4 * (s % 2) + 3 + q],
                                                   accum_out=st[:, 8 + 2 * (s % 2) + q:9 + 2 * (s % 2) + q])
                    ins.then_inc(pexp_ready, 1)
                if 1 <= s <= HEADS:
                    h = s - 1
                    act.wait_ge(pt_done, h + 1)
                    if h >= 2:
                        act.wait_ge(pv_done, h - 1)
                    nc.scalar.copy(p_turn[:, h % 2, :], bank(2 + h % 2, 0, 384)).then_inc(pt_copied, 1)
                if s >= 2 and s % 2 == 1:
                    c = (s - 3) // 2
                    act.wait_ge(pv_done, s - 1)
                    nc.scalar.copy(o_t[:, c, 0:SEQ], bank(4 + c % 2, 0, SEQ)).then_inc(po_copied, 1)

            act.sem_inc(kt_act, 1)
            with act.Fori(0, NB) as b:
                for kt in range(3):
                    for c in range(1, AC, 2):
                        n = kt * AC + c
                        w = 512 if kt < 2 else 256
                        act.wait_ge(kt_done, b * 18 + n + 1)
                        nc.scalar.copy(kt_sb[:, c, 512 * kt:512 * kt + w], bank(4, 0, w)).then_inc(kt_act, 1)
                act.wait_ge(s_max, b + 2)
                nc.scalar.activation(prob[0:96, :], prob[0:96, :], ACT.Exp, bias=st[0:96, 14:15],
                                     accum_out=st[0:96, 15:16]).then_inc(s_exp, 1)
                act.wait_ge(st_done, b * 3 + 1)
                nc.scalar.copy(pt_sb[:, 0:5, :], bank(5, 0, 480).rearrange("p (a b) -> p a b", a=5)).then_inc(st_act, 1)

            act.wait_ge(so_copied, NB)
            for tt, (a, n) in enumerate(TILES):
                act.wait_ge(var_ready, 2 * tt + 1)
                nc.scalar.activation(st[0:n, 18:20], st[0:n, 16:18], ACT.Sqrt).then_inc(sd_ready, 1)
                act.wait_ge(var_ready, 2 * tt + 2)
                nc.scalar.activation(st[0:n, 36:37], st[0:n, 35:36], ACT.Sqrt).then_inc(sd_ready, 1)
                act.wait_ge(u2t_done, 2 * tt + 1)
                nc.scalar.copy(u2_t[:, 0:4, 0:n], bank(4).rearrange("p (a b) -> p a b", a=4)[:, :, 0:n]).then_inc(u2t_ready, 1)
                act.wait_ge(u2t_done, 2 * tt + 2)
                nc.scalar.copy(u2_t[:, 4:8, 0:n], bank(5).rearrange("p (a b) -> p a b", a=4)[:, :, 0:n]).then_inc(u2t_ready, 1)
                act.wait_ge(neg_ready, tt + 1)
                nc.scalar.activation(ex[0:n, :], lg[0:n, :], ACT.Exp, bias=st[0:n, 40:41]).then_inc(ex_ready, 1)

            act.wait_ge(route_ready, 1)
            for counted_from_one in (xe_act, y_ready, selt_ready):
                act.sem_inc(counted_from_one, 1)
            items = act.value_load(flag_i[0:1, 0:1], min_val=NE, max_val=ITEMS)
            with act.Fori(0, items) as i:
                now_b = act.value_load(flag_i[0:1, bass.ds(i + 1, 1)], min_val=0, max_val=1)

                def sigmoid(v):
                    act.wait_ge(g_ready[v], i + 1)
                    nc.scalar.activation(act_s[:, v, :], act_g[:, v, :], ACT.Sigmoid, scale=1.702
                                         ).then_inc(sig_ready[v], 1)

                def turned(v):
                    act.wait_ge(at_done[v], i + 1)
                    nc.scalar.copy(a_t[:, v, :], bank(2 * v)).then_inc(at_ready[v], 1)

                sigmoid(0)
                turned(0)
                with act.If(now_b > 0):
                    sigmoid(1)
                    turned(1)
                with act.Else():
                    act.sem_inc(sig_ready[1], 1)
                    act.sem_inc(at_ready[1], 1)
                act.wait_ge(ga_done, i + 2)
                nc.scalar.copy(xe_t[:, 4:8, :], bank(5).rearrange("p (a b) -> p a b", a=4)).then_inc(xe_act, 1)
                with act.If(now_b > 0):
                    act.wait_ge(dn_used, i * (KC // 2) + KC // 2)
                    nc.scalar.copy(y_sb[:, 1, :], bank(2))
                    nc.scalar.copy(y_sb[:, 0, :], bank(3)).then_inc(y_ready, 1)
                with act.Else():
                    act.wait_ge(dn_used, i * (KC // 2) + KC // 2)
                    nc.scalar.copy(y_sb[:, 0, :], bank(3)).then_inc(y_ready, 1)
                act.wait_ge(selt_done, i + 2)
                for v in range(2):
                    ins = nc.scalar.copy(sel_t[:, v, 0:320], bank(6 + v, 0, 320))
                ins.then_inc(selt_ready, 1)
            for tt, (a, n) in enumerate(TILES):
                act.wait_ge(var_ready, 7 + tt)
                nc.scalar.activation(st[0:n, 36:37], st[0:n, 35:36], ACT.Sqrt).then_inc(sd_ready, 1)

        @block.vector
        def _(dve):
            V = Chain(dve, ch_v)
            v_ = nc.vector
            v_.memset(c_sb[0:32, :], 0.0)
            v_.memset(rows[0:32, :], 0.0)
            v_.memset(z_p[:, :, 0:2], 0.0)
            v_.memset(g_rows[0:8, :], 0.0).then_inc(zeroed, 1)
            dve.wait_ge(sig_done, 1)
            v_.tensor_tensor(c_sb[0:32, :], c_sb[0:32, :], sig_c[0:32, :], ALU.mult).then_inc(c_ready, 1)
            dve.wait_ge(ct_done, 1)
            v_.tensor_copy(c_t, bank(7, 0, 256).rearrange("p (a b) -> p a b", a=KC)).then_inc(ct_ready, 1)
            dve.wait_ge(rows_done, 1)
            v_.tensor_copy(rows_t, bank(6, 0, 64).rearrange("p (a b) -> p a b", a=2))
            v_.tensor_copy(g_attn, bank(6, 64, 72)).then_inc(rows_ready, 1)
            dve.wait_ge(rows_ready, 1)
            V(v_.tensor_copy(z_s.rearrange("p c (b t) -> p c b t", b=NB)[:, :, :, 0:2],
                             rows_t[:, :, 0:16].rearrange("p c (b t) -> p c b t", b=NB)))
            for c in range(KC):
                dve.wait_ge(xt_done, c + 1)
                v_.tensor_copy(u_t[:, c, :], bank(4 + c % 2, 0, NTOK)).then_inc(xt_copied, 1)
            dve.wait_ge(tabc_in, 160)
            V(v_.memset(bias_sel, 0.0))
            for kc in range(2):
                for q in range(4):
                    cols = bias_sel[32 * q:32 * q + 32, kc, 4 * kc + q:96:NS]
                    ins = v_.tensor_copy(cols, relb[32 * q:32 * q + 32, :])
            ins.then_inc(bsel_ready, 1)
            dve.wait_ge(tab_done, 1)
            v_.tensor_copy(tab_sb[0:HEADS, :], bank(6, 0, 384)[0:HEADS]).then_inc(tab_ready, 1)
            dve.wait_ge(bada_in, 64)
            dve.wait_ge(ada_used, KC)
            for m in range(3):
                ins = v_.tensor_tensor(ada_sb[:, m, :], bank(m), b_rows[:, m, :], ALU.add)
            ins.then_inc(ada_ready, 1)
            dve.wait_ge(adat_done, 1)
            src = bank(3).rearrange("p (a b) -> p a b", a=4)
            v_.tensor_copy(ada_t[:, :, 0:64], src[:, :, 0:64])
            V(v_.tensor_scalar(ada_t[:, :, 64:128], src[:, :, 64:128], 1.0, None, ALU.add))
            dve.wait_ge(xt_copied, KC)
            for c in range(KC):
                cb, j = c % 4, c // 4
                sh, sc = ada_t[:, cb, 32 * j:32 * j + 9], ada_t[:, cb, 64 + 32 * j:64 + 32 * j + 9]
                v_.tensor_scalar(u_t[:, c, 0:SEQ], u_t[:, c, 0:SEQ], sc[:, 0:1], sh[:, 0:1], ALU.mult, ALU.add)
                us = u_t[:, c, SEQ:NTOK].rearrange("p (b t) -> p b t", b=NB)
                V(v_.tensor_tensor(us, us, sc[:, 1:9].unsqueeze(2).to_broadcast([128, NB, NS]), ALU.mult))
                ins = v_.tensor_tensor(us, us, sh[:, 1:9].unsqueeze(2).to_broadcast([128, NB, NS]), ALU.add)
            ins.then_inc(u_ready, 1)
            for c in range(6):
                dve.wait_ge(pb_done, c + 1)
                v_.tensor_copy(p_bias[:, 2 * c:2 * c + 2, :], bank(6 + c % 2).rearrange("p (a b) -> p a b", a=2)
                               ).then_inc(pb_ready, 1)
            for u, (kind, c, _, eng) in enumerate(UNITS):
                if eng != "dve":
                    continue
                dve.wait_ge(proj_done, u + 1)
                src = bank(u % PB)
                if kind == "k":
                    ins = v_.tensor_copy(k_t[:, c, :], src[:, 0:NTOK])
                elif kind == "h":
                    dve.wait_ge(proj_act, copied(u - 1))
                    v_.tensor_tensor(z_p[:, c, 2:SEQ + 2], src[:, 0:SEQ], c_gate[:, c, 0:SEQ], ALU.mult)
                    ins = v_.tensor_tensor(z_s[:, c, :].rearrange("p (b t) -> p b t", b=NB)[:, :, 2:10],
                                           src[:, SEQ:NTOK].rearrange("p (b t) -> p b t", b=NB),
                                           c_gate[:, c, SEQ:NTOK].rearrange("p (b t) -> p b t", b=NB), ALU.mult)
                else:
                    n = TILES[c[0]][1]
                    ins = v_.tensor_copy(v_nat[0:n, c[0], 384:DA], src[0:n, 0:384])
                ins.then_inc(proj_dve, 1)
            for tt, (_, n) in enumerate(TILES):
                dve.wait_ge(kn_done, tt + 1)
                v_.tensor_copy(k_nat[0:n, tt, 0:512], bank(6)[0:n]).then_inc(kn_dve, 1)
            dve.wait_ge(proj_dve, copied(len(UNITS) - 1))
            zs4 = z_s.rearrange("p c (b t) -> p c b t", b=NB)
            v_.tensor_copy(z_last[:, :, 0:2], z_p[:, :, SEQ:SEQ + 2])
            v_.tensor_copy(z_last[:, :, 2:18].rearrange("p c (b t) -> p c b t", b=NB), zs4[:, :, :, 8:10]
                           ).then_inc(zl_ready, 1)
            dve.wait_ge(proj_act, copied(len(UNITS) - 2))
            for c in range(CC):
                wc = rows_t[:, c, 16:19]
                zs, cs = zs4[:, c], c_gate[:, c, SEQ:NTOK].rearrange("p (b t) -> p b t", b=NB)
                cp = c_gate[:, c, 0:SEQ]
                v_.tensor_scalar(cp, z_p[:, c, 0:SEQ], wc[:, 0:1], None, ALU.mult)
                V(v_.tensor_scalar(cs, zs[:, :, 0:8], wc[:, 0:1], None, ALU.mult))
                for w in (1, 2):
                    v_.scalar_tensor_tensor(cp, z_p[:, c, w:SEQ + w], wc[:, w:w + 1], cp, ALU.mult, ALU.add)
                    V(v_.scalar_tensor_tensor(cs, zs[:, :, w:w + 8], wc[:, w:w + 1], cs, ALU.mult, ALU.add))
                V(v_.tensor_tensor(y_c[:, c, :], y_c[:, c, :], c_gate[:, c, :], ALU.mult))
            dve.wait_ge(zn_done, 1)
            v_.tensor_copy(z_nat[0:18, :], bank(6, 0, 256)[0:18]).then_inc(zn_ready, 1)
            dve.wait_ge(sb_done, 1)
            V(v_.tensor_copy(s_bias[0:96, :], ps[0:96, 0:SB]))
            dve.sem_inc(sb_ready, 1)

            dve.wait_ge(pb_ready, 6)
            for s in range(HEADS + 1):
                if s < HEADS:
                    dve.wait_ge(ps_done, s + 1)
                    if s >= 2:
                        dve.wait_ge(pt_done, s - 1)
                    o = 4 * (s % 2)
                    v_.tensor_tensor_reduce(p_soft[:, s % 2, 0:128], bank(s % 2, 0, 128), p_bias[:, s, 128:256], 1.0,
                                            -3e38, ALU.add, ALU.max, st[:, o:o + 1])
                    V(v_.tensor_tensor_reduce(p_soft[:, s % 2, 128:384], bank(s % 2, 128, 384), p_bias[:, s, :], 1.0,
                                              -3e38, ALU.add, ALU.max, st[:, o + 1:o + 2]))
                    v_.tensor_scalar(st[:, o + 2:o + 4], st[:, o:o + 2], -1.0, None, ALU.mult).then_inc(pmax_ready, 1)
                if s >= 1:
                    h = s - 1
                    dve.wait_ge(pexp_ready, s)
                    r = 8 + 2 * (h % 2)
                    V(v_.reciprocal(st[:, r:r + 2], st[:, r:r + 2]))
                    v_.tensor_scalar(p_soft[:, h % 2, 0:128], p_soft[:, h % 2, 0:128], st[:, r:r + 1], None, ALU.mult)
                    v_.tensor_scalar(p_soft[:, h % 2, 128:384], p_soft[:, h % 2, 128:384], st[:, r + 1:r + 2], None,
                                     ALU.mult).then_inc(pnorm_ready, 1)

            dve.wait_ge(pt_done, HEADS)
            V(v_.memset(qbd, 0.0))
            dve.sem_inc(kt_dve, 1)
            dve.sem_inc(s_max, 1)
            with dve.Fori(0, NB) as b:
                V.enter(b, 3)
                dve.wait_ge(s_done, b + 1)
                for par in range(2):
                    for half in range(2):
                        lo = 16 * par + 8 * half
                        ins = v_.tensor_copy(qbd[64 * half:64 * half + 64, par:AC:2, lo:lo + 8],
                                             q_t[64 * half:64 * half + 64, par:AC:2, bass.ds(SEQ + b * NS, NS)])
                ins.then_inc(qbd_ready, 1)
                for kt in range(3):
                    for c in range(0, AC, 2):
                        n = kt * AC + c
                        w = 512 if kt < 2 else 256
                        dve.wait_ge(kt_done, b * 18 + n + 1)
                        v_.tensor_copy(kt_sb[:, c, 512 * kt:512 * kt + w], bank(3, 0, w)).then_inc(kt_dve, 1)
                dve.wait_ge(s_done, b + 2)
                v_.scalar_tensor_tensor(prob[0:96, NCACHE:NCACHE + 64], ps[0:96, NCACHE:NCACHE + 64], 1.0,
                                        s_bias[0:96, bass.ds(b * -NS + SB - 64, 64)], ALU.mult, ALU.add)
                V(v_.tensor_tensor_reduce(prob[0:96, 0:NCACHE], ps[0:96, 0:NCACHE], s_bias[0:96, 0:NCACHE], 1.0, -3e38,
                                          ALU.add, ALU.max, st[0:96, 12:13]))
                V(v_.tensor_reduce(st[0:96, 13:14], prob[0:96, NCACHE:NCACHE + 64], AX.X, ALU.max))
                v_.tensor_scalar(st[0:96, 14:15], st[0:96, 12:13], st[0:96, 13:14], -1.0, ALU.max, ALU.mult
                                 ).then_inc(s_max, 1)
                dve.wait_ge(st_done, b * 3 + 2)
                v_.tensor_copy(pt_sb[:, 5:10, :], bank(6, 0, 480).rearrange("p (a b) -> p a b", a=5)).then_inc(st_dve, 1)
                dve.wait_ge(st_done, b * 3 + 3)
                v_.tensor_copy(pt_sb[0:64, KB, :], bank(3, 0, 96)[0:64]).then_inc(st_dve, 1)
                dve.wait_ge(s_exp, b + 1)
                V(v_.reciprocal(st[0:96, 15:16], st[0:96, 15:16]))
                dve.wait_ge(sv_done, b + 1)
                v_.scalar_tensor_tensor(o_mask[0:96, :], bank(7, 0, 256)[0:96], st[0:96, 15:16], head_mask[0:96, :],
                                        ALU.mult, ALU.mult).then_inc(om_ready, 1)
                dve.wait_ge(so_done, b + 1)
                v_.tensor_copy(o_t[:, :, bass.ds(SEQ + b * NS, NS)], bank(5, 0, 48).rearrange("p (a b) -> p a b", a=AC)
                               ).then_inc(so_copied, 1)
            V.leave(NB)

            dve.wait_ge(so_copied, NB)
            dve.wait_ge(po_copied, AC)
            dve.wait_ge(out_kv, 96)
            for tt, (a, n) in enumerate(TILES):
                if tt:
                    dve.wait_ge(ss_done, tt)
                v_.tensor_tensor(sq_a[:, :, 0:n], o_t[:, :, a:a + n], o_t[:, :, a:a + n], ALU.mult)
                V(v_.tensor_tensor(sq_c[:, :, 0:n], y_c[:, :, a:a + n], y_c[:, :, a:a + n], ALU.mult))
                dve.sem_inc(sq_ready, 1)
                for c in range(AC):
                    v_.tensor_scalar(o_t[:, c, a:a + n], o_t[:, c, a:a + n], g_attn[:, c:c + 1], None, ALU.mult)
                for c in range(CC):
                    ins = v_.tensor_scalar(y_c[:, c, a:a + n], y_c[:, c, a:a + n], rows_t[:, c, 19:20], None, ALU.mult)
                ins.then_inc(og_ready, 1)
                dve.wait_ge(ss_done, tt + 1)
                v_.tensor_scalar(st[0:n, 16:17], bank(6)[0:n, 0:1], 1.0 / DA, RMS_EPS, ALU.mult, ALU.add)
                v_.tensor_scalar(st[0:n, 17:18], bank(6)[0:n, 1:2], 1.0 / DC, RMS_EPS, ALU.mult, ALU.add
                                 ).then_inc(var_ready, 1)
                dve.wait_ge(sd_ready, 2 * tt + 1)
                V(v_.reciprocal(st[0:n, 18:20], st[0:n, 18:20]))
                dve.wait_ge(wo_done, tt + 1)
                V(v_.tensor_scalar(mix[0:n], ps[0:n, 0:1024], st[0:n, 18:19], None, ALU.mult))
                V(v_.scalar_tensor_tensor(mix[0:n], ps[0:n, 1024:2048], st[0:n, 19:20], mix[0:n], ALU.mult, ALU.add))
                dve.sem_inc(mixed, 1)
                dve.wait_ge(g1_done, tt + 1)
                V(v_.scalar_tensor_tensor(mix[0:n], ps[0:n, 2048:3072], 1.0, mix[0:n], ALU.add, ALU.mult))
                dve.sem_inc(gated, 1)
                dve.wait_ge(tail_in, 64)
                x_t = x1[0:n, tt, :]
                V(v_.scalar_tensor_tensor(x_t, x_t, ALPHA, mix[0:n], ALU.mult, ALU.add))
                layer_norm(dve, V, v_, x_t, n, st, ln1, var_ready, sd_ready, 2 * tt + 2, x_t)
                dve.wait_ge(c2_done, tt + 1)
                V(v_.scalar_tensor_tensor(u2[0:n, tt, :], ps[0:n, 0:1024], 1.0, x_t, ALU.add, ALU.mult))
                V(v_.tensor_tensor(u2[0:n, tt, :], u2[0:n, tt, :], ps[0:n, 1024:2048], ALU.add))
                dve.sem_inc(u2_ready, 1)
                dve.wait_ge(lg_done, tt + 1)
                V(v_.tensor_copy(lg[0:n, :], bank(7, 0, NE)[0:n]))
                V(v_.max(lead[0:n, :], lg[0:n, :]))
                v_.tensor_scalar(st[0:n, 40:41], lead[0:n, 0:1], -1.0, None, ALU.mult).then_inc(neg_ready, 1)
                V(v_.max_index(idx_u[0:n, :], lead[0:n, :], lg[0:n, :]))
                V(v_.tensor_copy(idx_f[0:n, :], idx_u[0:n, :]))
                mk = mask_t[0:n, tt, :]
                V(v_.tensor_scalar(mk, iota[0:n, 0:NE], idx_f[0:n, 0:1], None, ALU.is_equal))
                for j in range(1, 4):
                    V(v_.scalar_tensor_tensor(mk, iota[0:n, 0:NE], idx_f[0:n, j:j + 1], mk, ALU.is_equal, ALU.add))
                dve.wait_ge(ex_ready, tt + 1)
                V(v_.tensor_tensor_reduce(ex[0:n, :], ex[0:n, :], mk, 1.0, 0.0, ALU.mult, ALU.add, st[0:n, 41:42]))
                V(v_.reciprocal(st[0:n, 41:42], st[0:n, 41:42]))
                for r in range(ROUNDS):
                    v_.tensor_scalar(gate_t[0:n, tt, NE * r:NE * r + NE], ex[0:n, :], st[0:n, 41:42], None, ALU.mult)
                V(v_.memset(gate_t[0:n, tt, ITEMS:ITEMS + 1], 0.0))
            dve.sem_inc(masks_ready, 1)
            dve.wait_ge(rank_done, 1)
            for tt, (a, n) in enumerate(TILES):
                mk, rk = mask_t[0:n, tt, :], rank_t[0:n, tt, :]
                V(v_.scalar_tensor_tensor(rk[:, 0:NE], bank(7)[0:n, NE * tt:NE * tt + NE], FAR, mk, ALU.add, ALU.mult))
                V(v_.tensor_scalar(rk[:, 0:NE], rk[:, 0:NE], -FAR, None, ALU.add))
                for r in range(1, ROUNDS):
                    v_.tensor_scalar(rk[:, NE * r:NE * r + NE], rk[:, 0:NE], -128.0 * r, None, ALU.add)
                V(v_.memset(rk[:, ITEMS:ITEMS + 1], -FAR))
            V(v_.tensor_copy(cnt[0:1, :], bank(7)[0:1, NE * 3:NE * 4]))
            V(v_.tensor_reduce(st[0:1, 44:45], cnt[0:1, :], AX.X, ALU.max))
            V(v_.memset(flag_f[0:1, :], 0.0))
            for r in range(ROUNDS):
                v_.tensor_scalar(flag_f[0:1, 1 + NE * r:1 + NE * r + NE], cnt[0:1, :], 128.0 * r + 64.5, None, ALU.is_gt)
            V(v_.tensor_scalar(st[0:1, 45:46], st[0:1, 44:45], 128.5, float(NE), ALU.is_gt, ALU.mult))
            V(v_.tensor_scalar(st[0:1, 46:47], st[0:1, 44:45], 256.5, float(NE), ALU.is_gt, ALU.mult))
            V(v_.tensor_tensor(st[0:1, 45:46], st[0:1, 45:46], st[0:1, 46:47], ALU.add))
            V(v_.tensor_scalar(flag_f[0:1, 0:1], st[0:1, 45:46], float(NE), None, ALU.add))
            V(v_.tensor_copy(flag_i[0:1, :], flag_f[0:1, :]))
            dve.sem_inc(route_ready, 1)
            dve.wait_ge(gt_done, 1)
            v_.tensor_copy(gt_sb[0:NE, :], bank(6, 0, NTOK)[0:NE]).then_inc(gt_ready, 1)
            dve.wait_ge(bd_done, 1)
            for tt, (a, n) in enumerate(TILES):
                v_.tensor_copy(acc[0:n, tt, :], ps[0:n, 1024 * tt:1024 * tt + 1024])
            v_.memset(y_sb, 0.0)
            V(v_.memset(sel_t, 0.0))
            dve.sem_inc(sc_added, 1)
            dve.sem_inc(acc_ready, 1)

            def choose(i, which):
                for tt, (_, n) in enumerate(TILES):
                    if which == "sel":
                        ins = v_.tensor_scalar(sel[0:n, tt, :], iota[0:n, :], rank_t[0:n, tt, bass.ds(i, 1)], None,
                                               ALU.is_equal)
                    else:
                        ins = v_.tensor_scalar(
                            sel_g[0:n, tt].rearrange("p (v d) s -> p v d s", v=2),
                            iota[0:n, :].rearrange("p (v s) -> p v s", v=2).unsqueeze(2).to_broadcast([n, 2, 2, 64]),
                            rank_t[0:n, tt, bass.ds(i, 1)], gate_t[0:n, tt, bass.ds(i, 1)], ALU.is_equal, ALU.mult)
                return ins

            def add_back(tt, banks):
                n = TILES[tt][1]
                for h in range(2):
                    ins = v_.tensor_tensor(acc[0:n, tt, 512 * h:512 * h + 512], acc[0:n, tt, 512 * h:512 * h + 512],
                                           bank(banks[h])[0:n], ALU.add)
                return ins

            choose(0, "sel").then_inc(sel_ready, 1)
            dve.wait_ge(ga_done, 1)
            v_.tensor_copy(xe_t[:, 4:8, :], bank(5).rearrange("p (a b) -> p a b", a=4))
            v_.tensor_copy(xe_t[:, 0:4, :], bank(4).rearrange("p (a b) -> p a b", a=4)).then_inc(xe_ready, 1)
            items = dve.value_load(flag_i[0:1, 0:1], min_val=NE, max_val=ITEMS)
            with dve.Fori(0, items) as i:
                V.enter(i, 4)
                now_b = dve.value_load(flag_i[0:1, bass.ds(i + 1, 1)], min_val=0, max_val=1)
                dve.wait_ge(ga_done, i + 1)
                choose(i + 1, "sel").then_inc(sel_ready, 1)
                dve.wait_ge(selt_done, i + 1)
                choose(i, "gated").then_inc(selg_ready, 1)

                def swiglu(v):
                    v_.tensor_scalar(act_g[:, v, :], bank(2 * v), 7.0, None, ALU.min).then_inc(g_ready[v], 1)
                    V(v_.tensor_scalar(act_l[:, v, :], bank(2 * v + 1), 7.0, -7.0, ALU.min, ALU.max))
                    V(v_.scalar_tensor_tensor(act_l[:, v, :], act_l[:, v, :], 1.0, act_g[:, v, :], ALU.add, ALU.mult))
                    dve.wait_ge(sig_ready[v], i + 1)
                    v_.tensor_tensor(act_l[:, v, :], act_l[:, v, :], act_s[:, v, :], ALU.mult).then_inc(a_ready[v], 1)

                dve.wait_ge(up_used, i * KC + KC)
                swiglu(0)
                with dve.If(now_b > 0):
                    swiglu(1)
                with dve.Else():
                    dve.sem_inc(ch_v, 2)
                    dve.sem_inc(g_ready[1], 1)
                    dve.sem_inc(a_ready[1], 1)
                dve.wait_ge(ga_done, i + 2)
                v_.tensor_copy(xe_t[:, 0:4, :], bank(4).rearrange("p (a b) -> p a b", a=4)).then_inc(xe_ready, 1)
                for tt in range(3):
                    dve.wait_ge(sc_done, i * 3 + tt + 1)
                    add_back(tt, ((6, 7), (4, 5), (6, 7))[tt]).then_inc(sc_added, 1)
            V.leave(items)
            for tt in range(3):
                dve.wait_ge(sc_done, items * 3 + tt + 1)
                add_back(tt, ((6, 7), (4, 5), (6, 7))[tt]).then_inc(sc_added, 1)
            V = Chain(dve, ch_end)
            dve.wait_ge(sc_added, items * 3 + 4)
            dve.wait_ge(ln2_in, 32)
            for tt, (a, n) in enumerate(TILES):
                dve.wait_ge(g2_done, tt + 1)
                V(v_.scalar_tensor_tensor(fin_t[0:n], ps[0:n, 1024 * tt:1024 * tt + 1024], 1.0, acc[0:n, tt, :],
                                          ALU.add, ALU.mult))
                V(v_.scalar_tensor_tensor(fin_t[0:n], x1[0:n, tt, :], ALPHA, fin_t[0:n], ALU.mult, ALU.add))
                layer_norm(dve, V, v_, fin_t[0:n], n, st, ln2, var_ready, sd_ready, 7 + tt, fin_y[0:n, tt, :])
                dve.sem_inc(y_done, 1)

        @block.tensor
        def _(pe):
            mm = nc.tensor.matmul

            def turn(o, i, n):
                return nc.tensor.transpose(o, i, ident[0:n, 0:n])

            pe.wait_ge(const_in, 16)
            pe.wait_ge(c_ready, 1)
            for k in range(KC):
                ins = turn(bank(7, 32 * k, 32 * k + 32), c_sb[0:32, 128 * k:128 * k + 128], 32)
            ins.then_inc(ct_done, 1)
            pe.wait_ge(rows_in, 64)
            for c in range(CC):
                turn(bank(6, 32 * c, 32 * c + 32), rows[0:32, 128 * c:128 * c + 128], 32)
            turn(bank(6, 64, 72), g_rows[0:8, :], 8).then_inc(rows_done, 1)
            pe.wait_ge(x_ready, 32)
            for c in range(KC):
                if c >= 2:
                    pe.wait_ge(xt_copied, c - 1)
                for tt, (a, n) in enumerate(TILES):
                    ins = turn(bank(4 + c % 2, a, a + n), x_in[0:n, tt, 128 * c:128 * c + 128], n)
                ins.then_inc(xt_done, 1)
            pe.wait_ge(tabc_in, 160)
            pe.wait_ge(zeroed, 1)
            pe.wait_ge(ct_ready, 1)
            pe.wait_ge(rows_ready, 1)
            mm(bank(6, 0, 384)[0:HEADS], relb[0:32, :], tab_hot[0:32, :], start=True, stop=False)
            mm(bank(6, 0, 384)[0:HEADS], ones[0:1, 0:HEADS], tab_log[0:1, :], start=False, stop=True).then_inc(tab_done, 1)
            for k in range(KC):
                pe.wait_ge(ada_in[k % ADA_SLOTS], 16 * (k // ADA_SLOTS) + 16)
                for m in range(3):
                    for j in range(4):
                        ins = mm(bank(m)[32 * j:32 * j + 32], c_t[:, k, :],
                                 ada_w[:, k % ADA_SLOTS, 512 * (4 * m + j):512 * (4 * m + j) + 512],
                                 start=k == 0, stop=k == KC - 1, tile_position=(0, 32 * j))
                ins.then_inc(ada_used, 1)
            pe.wait_ge(ada_ready, 1)
            for cb in range(4):
                ins = turn(bank(3, 128 * cb, 128 * cb + 128), ada_sb[:, 0, 128 * cb:128 * cb + 128], 128)
            ins.then_inc(adat_done, 1)
            pe.wait_ge(hb_in, 16)
            for c in range(6):
                pe.wait_ge(tab_ready, 1)
                if c >= 2:
                    pe.wait_ge(pb_ready, c - 1)
                mm(bank(6 + c % 2), anti, hb[:, 2 * c:2 * c + 2, :], start=True, stop=True).then_inc(pb_done, 1)
            pe.wait_ge(u_ready, 1)
            pe.wait_ge(win_in, 128)
            for u, (kind, c, col, eng) in enumerate(UNITS):
                if u >= PB:
                    pe.wait_ge(proj_act if UNITS[u - PB][3] == "act" else proj_dve, copied(u - PB))
                for k in range(KC):
                    if kind == "v":
                        a, n = TILES[c[0]]
                        ins = mm(bank(u % PB)[0:n, 0:384], u_t[:, k, a:a + n], win_w[:, k, col:col + 384],
                                 start=k == 0, stop=k == KC - 1)
                    else:
                        ins = mm(bank(u % PB)[:, 0:NTOK], win_w[:, k, col:col + 128], u_t[:, k, :],
                                 start=k == 0, stop=k == KC - 1)
                ins.then_inc(proj_done, 1)
            pe.wait_ge(proj_dve, copied(2 * AC - 1))
            pe.wait_ge(pb_ready, 6)
            for tt, (a, n) in enumerate(TILES):
                if tt:
                    pe.wait_ge(kn_dve, tt)
                    pe.wait_ge(kn_act, tt)
                for c in range(AC):
                    ins = turn(bank(6 + c // 4, 128 * (c % 4), 128 * (c % 4) + 128)[0:n], k_t[:, c, a:a + n], 128)
                ins.then_inc(kn_done, 1)
            pe.wait_ge(zl_ready, 1)
            pe.wait_ge(kn_dve, 3)
            for c in range(CC):
                ins = turn(bank(6, 128 * c, 128 * c + 128)[0:18], z_last[:, c, :], 128)
            ins.then_inc(zn_done, 1)
            pe.wait_ge(proj_act, copied(len(UNITS) - 2))
            pe.wait_ge(proj_dve, copied(len(UNITS) - 1))
            pe.wait_ge(hot_in, 64)
            pe.wait_ge(bsel_ready, 1)
            for a, z in ((0, 512), (512, 1024), (1024, SB)):
                for kc in range(2):
                    mm(ps[0:96, a:z], bias_sel[:, kc, :], hot_s[:, kc, a:z], start=kc == 0, stop=False)
                ins = mm(ps[0:96, a:z], log_sel[0:8, :], log_s[0:8, a:z], start=False, stop=True)
            ins.then_inc(sb_done, 1)
            pe.wait_ge(sb_ready, 1)
            for s in range(HEADS + 2):
                if s < HEADS:
                    c, lo = s // 2, 64 * (s % 2)
                    if s >= 2:
                        pe.wait_ge(pmax_ready, s - 1)
                    q, k = q_t[lo:lo + 64, c, :], k_t[lo:lo + 64, c, :]
                    mm(bank(s % 2, 0, 128), q[:, 0:128], k[:, 0:128], start=True, stop=True)
                    mm(bank(s % 2, 128, 384), q[:, 128:256], k[:, 0:256], start=True, stop=True).then_inc(ps_done, 1)
                if 1 <= s <= HEADS:
                    h = s - 1
                    pe.wait_ge(pnorm_ready, h + 1)
                    if h >= 2:
                        pe.wait_ge(pt_copied, h - 1)
                    for j in range(3):
                        ins = turn(bank(2 + h % 2, 128 * j, 128 * j + 128), p_soft[:, h % 2, 128 * j:128 * j + 128], 128)
                    ins.then_inc(pt_done, 1)
                if s >= 2:
                    h = s - 2
                    c, lo = h // 2, 64 * (h % 2)
                    pe.wait_ge(pt_copied, h + 1)
                    if h >= 4:
                        pe.wait_ge(po_copied, c - 1)
                    o = bank(4 + c % 2)[lo:lo + 64]
                    pt = p_turn[:, h % 2, :]
                    vv = v_nat[:, :, HD * h:HD * h + HD]
                    mm(o[:, 0:128], vv[:, 0], pt[:, 0:128], start=True, stop=True)
                    mm(o[:, 128:256], vv[:, 0], pt[:, 128:256], start=True, stop=False)
                    mm(o[:, 128:256], vv[:, 1], pt[:, 256:384], start=False, stop=True).then_inc(pv_done, 1)
            pe.wait_ge(po_copied, AC)
            for counted_from_one in (k_used, v_used, s_done):
                pe.sem_inc(counted_from_one, 1)
            with pe.Fori(0, NB) as b:
                def keys(kt):
                    nb = 4 if kt < 2 else 2
                    for c in range(AC):
                        n = kt * AC + c
                        pe.wait_ge(kt_dve if c % 2 == 0 else kt_act, b * 9 + n // 2 + 1)
                        for j in range(nb):
                            ins = turn(bank(3 + c % 2, 128 * j, 128 * j + 128),
                                       k_sb[:, 4 * kt + j, 128 * c:128 * c + 128], 128)
                        ins.then_inc(kt_done, 1)

                def scores(o, rhs):
                    for c in (0, 2, 4, 1, 3, 5):
                        j = c // 2
                        ins = mm(o[32 * j:32 * j + 32], qbd[:, c, :], rhs(c), start=c % 2 == 0, stop=c % 2 == 1,
                                 tile_position=(0, 32 * j))
                    return ins

                pe.wait_ge(k_rec_in, b * 16 + 16)
                keys(0)
                pe.wait_ge(k_old_in, b * 128 + 128)
                keys(1)
                pe.wait_ge(qbd_ready, b + 1)
                pe.wait_ge(s_max, b + 1)
                pe.wait_ge(kt_dve, b * 9 + 4)
                pe.wait_ge(kt_act, b * 9 + 4)
                scores(bank(0), lambda c: kt_sb[:, c, 0:512])
                keys(2)
                pe.wait_ge(kt_dve, b * 9 + 7)
                pe.wait_ge(kt_act, b * 9 + 7)
                scores(bank(1), lambda c: kt_sb[:, c, 512:1024]).then_inc(k_used, 1)
                pe.wait_ge(kt_dve, b * 9 + 10)
                pe.wait_ge(kt_act, b * 9 + 10)
                scores(bank(2, 0, 256), lambda c: kt_sb[:, c, 1024:NCACHE])
                scores(bank(2, 256, 320), lambda c: k_t[:, c, SEQ:NTOK]).then_inc(s_done, 1)
                pe.wait_ge(s_exp, b + 1)
                for j in range(KB + 1):
                    o = bank(5, 96 * j, 96 * j + 96) if j < 5 else (
                        bank(6, 96 * j - 480, 96 * j - 384) if j < KB else bank(3, 0, 96)[0:64])
                    ins = turn(o, prob[0:96, 128 * j:min(128 * j + 128, NCACHE + 64)], 96)
                    if j in (4, KB - 1, KB):
                        ins.then_inc(st_done, 1)
                pe.wait_ge(st_act, b + 1)
                pe.wait_ge(st_dve, b * 2 + 2)
                pe.wait_ge(v_in, b * 144 + 144)
                for j in range(KB + 1):
                    for g in range(3):
                        n = 128 if j < KB else 64
                        rhs = v_sb[:, j, 256 * g:256 * g + 256] if j < KB else v_nat[0:64, 2, 256 * g:256 * g + 256]
                        ins = mm(bank(7, 0, 256)[32 * g:32 * g + 32], pt_sb[0:n, j, 32 * g:32 * g + 32], rhs,
                                 start=j == 0, stop=j == KB, tile_position=(0, 32 * g))
                    if j == KB - 1:
                        ins.then_inc(v_used, 1)
                ins.then_inc(sv_done, 1)
                pe.wait_ge(om_ready, b + 1)
                for c in range(AC):
                    ins = mm(bank(5, 8 * c, 8 * c + 8), o_mask[0:96, 128 * (c % 2):128 * (c % 2) + 128],
                             query_sum[0:96, c // 2, :], start=True, stop=True)
                ins.then_inc(so_done, 1)

            pe.wait_ge(so_copied, NB)
            for tt, (a, n) in enumerate(TILES):
                pe.wait_ge(sq_ready, tt + 1)
                for c in range(AC):
                    mm(bank(6)[0:n, 0:1], sq_a[:, c, 0:n], ones[:, 0:1], start=c == 0, stop=c == AC - 1)
                for c in range(CC):
                    ins = mm(bank(6)[0:n, 1:2], sq_c[:, c, 0:n], ones[:, 0:1], start=c == 0, stop=c == CC - 1)
                ins.then_inc(ss_done, 1)
                pe.wait_ge(og_ready, tt + 1)
                pe.wait_ge(wo_in, 16)
                if tt:
                    pe.wait_ge(u2_ready, tt)
                for h in range(2):
                    for c in range(AC):
                        mm(bank(h)[0:n], o_t[:, c, a:a + n], wo_sb[:, c, 512 * h:512 * h + 512], start=c == 0,
                           stop=c == AC - 1)
                    for c in range(CC):
                        ins = mm(bank(2 + h)[0:n], y_c[:, c, a:a + n], wo_sb[:, AC + c, 512 * h:512 * h + 512],
                                 start=c == 0, stop=c == CC - 1)
                ins.then_inc(wo_done, 1)

                def repeat(o, m, j):
                    lhs = (rep_p if tt < 2 else rep_s)[32 * j:32 * j + 32, 0:n]
                    return mm(o, lhs, ada_sb[32 * j:32 * j + 32, m, :], start=True, stop=True)

                if tt:
                    pe.wait_ge(u2t_ready, 2 * tt)
                for h in range(2):
                    ins = repeat(bank(4 + h)[0:n], 1, h)
                ins.then_inc(g1_done, 1)
                pe.wait_ge(mixed, tt + 1)
                for h in range(2):
                    repeat(bank(h)[0:n], 2, h)
                    ins = repeat(bank(2 + h)[0:n], 1, 2 + h)
                ins.then_inc(c2_done, 1)
                pe.wait_ge(gated, tt + 1)
                pe.wait_ge(u2_ready, tt + 1)
                for h in range(2):
                    for c in range(4):
                        ins = turn(bank(4 + h, 128 * c, 128 * c + n), u2[0:n, tt, 128 * (4 * h + c):128 * (4 * h + c) + 128], n)
                    ins.then_inc(u2t_done, 1)
                pe.wait_ge(u2t_ready, 2 * tt + 2)
                if tt:
                    pe.wait_ge(neg_ready, tt)
                for k in range(KC):
                    mm(bank(7, 0, NE)[0:n], u2_t[:, k, 0:n], rw_sb[:, k, :], start=k == 0, stop=False)
                mm(bank(7, 0, NE)[0:n], ones[0:1, 0:n], rb_sb[0:1, :], start=False, stop=True).then_inc(lg_done, 1)
            pe.wait_ge(masks_ready, 1)
            for tt, (a, n) in enumerate(TILES):
                for s in range(tt + 1):
                    m = TILES[s][1]
                    mm(bank(7, NE * tt, NE * tt + NE)[0:n], tri[0:m, 0:n] if s == tt else ones[0:m, 0:n],
                       mask_t[0:m, s, :], start=s == 0, stop=s == tt)
            for s in range(3):
                m = TILES[s][1]
                ins = mm(bank(7, NE * 3, NE * 4), ones[0:m, :], mask_t[0:m, s, :], start=s == 0, stop=s == 2)
            ins.then_inc(rank_done, 1)
            for tt, (a, n) in enumerate(TILES):
                ins = turn(bank(6, a, a + n)[0:NE], gate_t[0:n, tt, 0:NE], n)
            ins.then_inc(gt_done, 1)
            pe.wait_ge(gt_ready, 1)
            pe.wait_ge(late_in, 16)
            pe.wait_ge(u2_ready, 3)
            for tt, (a, n) in enumerate(TILES):
                for h in range(2):
                    ins = mm(bank(2 * tt + h)[0:n], gt_sb[0:NE, a:a + n], bd_sb[0:NE, 512 * h:512 * h + 512],
                             start=True, stop=True)
            ins.then_inc(bd_done, 1)

            def gather():
                for c in range(KC):
                    for tt, (_, n) in enumerate(TILES):
                        ins = mm(bank(4 + c // 4, 128 * (c % 4), 128 * (c % 4) + 128),
                                 u2[0:n, tt, 128 * c:128 * c + 128], sel[0:n, tt, :], start=tt == 0, stop=tt == 2)
                ins.then_inc(ga_done, 1)

            def scatter(tt, banks, blocks):
                for v in range(blocks):
                    for h in range(2):
                        ins = mm(bank(banks[h]), sel_t[64 * h:64 * h + 64, v, 128 * tt:128 * tt + 128],
                                 y_sb[64 * h:64 * h + 64, v, :], start=v == 0, stop=v == blocks - 1)
                return ins

            pe.sem_inc(selt_done, 1)
            pe.wait_ge(acc_ready, 1)
            pe.wait_ge(sel_ready, 1)
            items = pe.value_load(flag_i[0:1, 0:1], min_val=NE, max_val=ITEMS)
            gather()
            with pe.Fori(0, items) as i:
                now_b = pe.value_load(flag_i[0:1, bass.ds(i + 1, 1)], min_val=0, max_val=1)
                last_b = pe.value_load(flag_i[0:1, bass.ds(i, 1)], min_val=0, max_val=ITEMS)
                pe.wait_ge(xe_ready, i + 1)
                pe.wait_ge(xe_act, i + 1)
                pe.wait_ge(bup_in, i * 16 + 16)

                def up_bias(v):
                    for part in range(2):
                        for h in range(2):
                            ins = mm(bank(2 * v + part)[64 * h:64 * h + 64], ones[0:1, 0:64],
                                     b_up[0:1, FF * part + 512 * h:FF * part + 512 * h + 512], start=True, stop=False)
                    return ins

                def up(blocks):
                    if blocks == 2:
                        pe.wait_ge(y_ready, i + 1)
                    for v in range(blocks):
                        ins = up_bias(v)
                    ins.then_inc(bup_used, 1)
                    for k in range(KC):
                        pe.wait_ge(up_in[k], i * 16 + 16)
                        for v in range(blocks):
                            for part in range(2):
                                for h in range(2):
                                    ins = mm(bank(2 * v + part)[64 * h:64 * h + 64], xe_t[:, k, 64 * v:64 * v + 64],
                                             up_w[:, k, FF * part + 512 * h:FF * part + 512 * h + 512],
                                             start=False, stop=k == KC - 1)
                        ins.then_inc(up_used, 1)

                with pe.If(now_b > 0):
                    up(2)
                with pe.Else():
                    up(1)
                pe.wait_ge(sel_ready, i + 2)
                pe.wait_ge(sc_added, i * 3 + 1)
                gather()

                def turn_act(v):
                    pe.wait_ge(a_ready[v], i + 1)
                    for c in range(4):
                        ins = turn(bank(2 * v, 128 * c, 128 * c + 128), act_l[:, v, 128 * c:128 * c + 128], 128)
                    ins.then_inc(at_done[v], 1)

                def add_up(tts):
                    with pe.If(last_b > 0):
                        for tt in tts:
                            scatter(tt, ((6, 7), (4, 5), (6, 7))[tt], 2).then_inc(sc_done, 1)
                    with pe.Else():
                        for tt in tts:
                            scatter(tt, ((6, 7), (4, 5), (6, 7))[tt], 1).then_inc(sc_done, 1)

                turn_act(0)
                pe.wait_ge(selt_ready, i + 1)
                with pe.If(now_b > 0):
                    turn_act(1)
                with pe.Else():
                    pe.sem_inc(at_done[1], 1)
                pe.wait_ge(y_ready, i + 1)
                pe.wait_ge(xe_ready, i + 2)
                pe.wait_ge(xe_act, i + 2)
                add_up((0, 1))

                def down(blocks, ms):
                    for m in ms:
                        pe.wait_ge(dn_in[m], i * 16 + 16)
                        for kk in (2 * m, 2 * m + 1):
                            for v in range(blocks):
                                for h in range(2):
                                    lhs = a_t[:, v, 128 * (kk % 4) + 64 * (kk // 4):128 * (kk % 4) + 64 * (kk // 4) + 64]
                                    ins = mm(bank(3 - v)[64 * h:64 * h + 64], lhs,
                                             dn_w[:, kk, 512 * h:512 * h + 512], start=kk == 0, stop=kk == KC - 1)
                        ins.then_inc(dn_used, 1)

                pe.wait_ge(at_ready[0], i + 1)
                with pe.If(now_b > 0):
                    pe.wait_ge(at_ready[1], i + 1)
                    down(2, (0,))
                with pe.Else():
                    down(1, (0,))
                pe.wait_ge(sc_added, i * 3 + 2)
                add_up((2,))
                with pe.If(now_b > 0):
                    down(2, (1, 2, 3))
                with pe.Else():
                    down(1, (1, 2, 3))
                pe.wait_ge(sc_added, i * 3 + 4)
                pe.wait_ge(selg_ready, i + 1)
                for v in range(2):
                    for tt, (a, n) in enumerate(TILES):
                        ins = turn(bank(6 + v, a, a + n), sel_g[0:n, tt, 2 * v:2 * v + 2, :], n)
                ins.then_inc(selt_done, 1)
            pe.wait_ge(selt_ready, items + 1)
            pe.wait_ge(y_ready, items + 1)
            scatter(0, (6, 7), 2).then_inc(sc_done, 1)
            scatter(1, (4, 5), 2).then_inc(sc_done, 1)
            pe.wait_ge(sc_added, items * 3 + 2)
            scatter(2, (6, 7), 2).then_inc(sc_done, 1)
            pe.wait_ge(sc_added, items * 3 + 4)
            for tt, (a, n) in enumerate(TILES):
                lhs = rep_p if tt < 2 else rep_s
                for h in range(2):
                    ins = mm(bank(2 * tt + h)[0:n], lhs[64 + 32 * h:96 + 32 * h, 0:n], ada_sb[64 + 32 * h:96 + 32 * h, 2, :],
                             start=True, stop=True)
                ins.then_inc(g2_done, 1)


def layer_norm(dve, V, v_, x, n, st, gb, var_ready, sd_ready, sd_count, y):
    for h in range(2):
        ins = v_.bn_stats(st[0:n, 20 + 6 * h:26 + 6 * h], x[:, 512 * h:512 * h + 512])
    V(ins)
    V(v_.bn_aggr(st[0:n, 32:34], st[0:n, 20:32]))
    v_.tensor_scalar(st[0:n, 35:36], st[0:n, 33:34], LN_EPS, None, ALU.add).then_inc(var_ready, 1)
    dve.wait_ge(sd_ready, sd_count)
    V(v_.reciprocal(st[0:n, 37:38], st[0:n, 36:37]))
    V(v_.tensor_scalar(x, x, st[0:n, 32:33], st[0:n, 37:38], ALU.subtract, ALU.mult))
    V(v_.tensor_tensor(x, x, gb[0:n, 0, :], ALU.mult))
    V(v_.tensor_tensor(y, x, gb[0:n, 1, :], ALU.add))


_INS = ["x_prompt", "x_sample", "cache_k", "cache_v", "state_conv", "c_prompt", "c_sample", "w_ada", "b_ada", "w_in",
        "conv_w", "norm_attn_g", "norm_conv_g", "w_o", "ln1_g", "ln1_b", "rel_bias", "router_w", "router_b", "w_up",
        "b_up", "w_down", "b_down", "ln2_g", "ln2_b"]
_OUTS = [(1, SEQ, D), (NB, NS, D), (1, 1, SEQ, HEADS, HD), (1, 1, SEQ, HEADS, HD), (1, 1, 2, DC),
         (1, NB, NS, HEADS, HD), (1, NB, NS, HEADS, HD), (1, NB, 2, DC)]
BRANCHES = ((128, 1), (512, 4), (2048, 16))


def shape_constants():
    import math
    import numpy as np

    def bucket(dist):
        df = np.maximum(dist, 16).astype(np.float32)
        large = 16 + (np.log(df / np.float32(16)) / np.float32(math.log(2048 / 16)) * np.float32(16)).astype(np.int32)
        return np.where(dist < 16, dist, np.minimum(large, 31))

    def log_count(dist):
        n = sum(((dist >= 0) & (dist <= w) & (dist % d == 0)).astype(np.int32) for w, d in BRANCHES)
        return np.where(n > 0, np.log(np.maximum(n, 1)), -1e30).astype(np.float32)

    def one_hot(dist):
        return (np.arange(32)[:, None] == bucket(np.clip(dist, 0, 2048))[None, :]).astype(np.float32)

    out = {}
    consts = np.zeros((128, NCONST), np.float32)
    p, c = np.arange(128)[:, None], np.arange(128)[None, :]
    for name, m in (("ident", p == c), ("tri", p < c), ("iota", np.broadcast_to(c, (128, 128))),
                    ("ones", np.ones((128, 128))), ("rep_p", (p % 32 == 0) & (c >= 0)),
                    ("rep_s", p % 32 == 1 + c[:, 0:64] // NS)):
        at, n = CONSTS[name]
        consts[:, at:at + n] = m
    out["consts"] = consts
    out["anti"] = (p == 127 - c).astype(np.float32)
    dist = 255 - np.arange(384)
    out["tab_hot"] = one_hot(dist)
    out["tab_log"] = log_count(dist)[None, :]
    part = np.arange(128)
    pos = [PAST - REC + 4 * part + r for r in range(4)]
    pos += [16 * (16 * r + part % 16) + part // 16 for r in range(6)]
    pos = np.concatenate(pos + [np.full(WIN, -1)])
    hot, logs = [], []
    for q in range(NS):
        dist = PAST + q - pos
        key = np.arange(WIN) - (NB * NS - NS)
        d_new = np.where((key >= 0) & (key < NS), q - key, -1)
        dist[NCACHE:] = d_new
        hot.append(one_hot(dist))
        logs.append(log_count(dist))
    out["hot_s"] = np.concatenate(hot).astype(np.float32)
    out["log_s"] = np.stack(logs)
    row = np.arange(96)[:, None]
    out["log_sel"] = (np.arange(96)[None, :] % NS == np.arange(NS)[:, None]).astype(np.float32)
    out["head_mask"] = (np.arange(256)[None, :] // HD == (row // NS) % 4).astype(np.float32)
    col = np.arange(24)[None, :]
    out["query_sum"] = ((row // 32 == col // 8) & (row % NS == col % 8)).astype(np.float32)
    return out


def kernel(**inputs):
    import numpy as _np
    import concourse.bacc as _bacc
    from concourse import mybir as _mybir
    from concourse.bass_utils import run_bass_kernel_spmd as _run

    nc = _bacc.Bacc("TRN2", target_bir_lowering=False, num_devices=1)
    arrays, t = {}, {}
    for name, a in list((n, inputs[n]) for n in _INS) + list(shape_constants().items()):
        a = _np.ascontiguousarray(a)
        arrays[f"in_{name}"] = a
        t[name] = nc.dram_tensor(f"in_{name}", a.shape, _mybir.dt.from_np(a.dtype), kind="ExternalInput").ap()
    outs = [nc.dram_tensor(f"out_{i}", shape, F32, kind="ExternalOutput").ap() for i, shape in enumerate(_OUTS)]
    scratch = nc.dram_tensor("by_distance", (HEADS, 384), F32, kind="Internal").ap()
    layer_kernel(nc, t, outs, scratch)
    r = _run(nc, [arrays], core_ids=[0])
    return tuple(r.results[0][f"out_{i}"] for i in range(len(_OUTS)))
```

```python
import concourse.bass as bass
from concourse import mybir
from contextlib import ExitStack

D = 1024
KC = D // 128
NE = 32
FF = 1024
HEADS, HD = 12, 64
DA, DC = HEADS * HD, 256
AC, CC = DA // 128, DC // 128
SEQ, NB, NS = 256, 8, 8
NTOK = SEQ + NB * NS
PAST = 2048
REC, OLD = 512, 768
KB = (REC + OLD) // 128
NCACHE = REC + OLD
WIN = 2 * NB * NS - NS
SB = NCACHE + WIN
TILES = [(0, 128), (128, 128), (256, 64)]
ALPHA = 2.0 ** 0.25
LN_EPS, RMS_EPS = 1e-5, 1e-6
ROUNDS = 3
ITEMS = ROUNDS * NE
FAR = 1000.0

F32, I32, U32 = mybir.dt.float32, mybir.dt.int32, mybir.dt.uint32
ALU = mybir.AluOpType
ACT = mybir.ActivationFunctionType
AX = mybir.AxisListType

CONSTS = {}


def lay_consts():
    at = 0
    for name, n in (("ident", 128), ("tri", 128), ("iota", 128), ("ones", 128), ("rep_p", 128), ("rep_s", 64)):
        CONSTS[name] = (at, n)
        at += n
    return at


NCONST = lay_consts()


class Chain:

    def __init__(self, eng, sem):
        self.eng, self.sem, self.n, self.before, self.off = eng, sem, 0, 0, 0

    def __call__(self, ins):
        ins.then_inc(self.sem, 1)
        self.n += 1
        self.eng.wait_ge(self.sem, self.n + self.off)

    def enter(self, i, per):
        self.start, self.per = self.n, per
        self.off = i * per + self.before

    def leave(self, turns):
        assert self.n - self.start == self.per, (self.n - self.start, self.per)
        self.n = self.start
        self.before = turns * self.per + self.before
        self.off = self.before


def layer_kernel(nc, t, out, scratch):
    ctx = ExitStack()
    with ctx:
        def sem(name):
            return ctx.enter_context(nc.semaphore(name))

        TOTAL = 53200
        arena = ctx.enter_context(nc.sbuf_tensor("arena", [128, TOTAL], F32))
        ps = ctx.enter_context(nc.psum_tensor("ps", [128, 4096], F32))

        def view(at, *dims):
            n = 1
            for d in dims:
                n *= d
            assert at + n <= TOTAL, (at, n)
            v = arena[:, at:at + n]
            if len(dims) == 2:
                v = v.rearrange("p (a b) -> p a b", a=dims[0])
            elif len(dims) == 3:
                v = v.rearrange("p (a b c) -> p a b c", a=dims[0], b=dims[1])
            return v

        def bank(b, a=0, z=512):
            return ps[:, 512 * b + a:512 * b + z]

        W = 0
        up_w = view(W, KC, 2 * FF)
        dn_w = view(W + KC * 2 * FF, KC, D)
        SLOTS, SLOT = 6, 4096
        ring_ada = [view(W + SLOT * s, 2, 2048) for s in range(SLOTS)]
        ring_in_w = [view(W + SLOT * s, KC, 512) for s in range(SLOTS)]
        KX = W
        k_sb = view(KX, KB, DA)
        VX = KX + KB * DA
        v_sb = view(VX, KB, DA)
        KTX = VX + KB * DA
        kt_sb = view(KTX, AC, NCACHE)
        hot_s = view(KTX, 2, SB)
        log_s = view(KTX + 2 * SB, SB)
        MX = KTX + AC * NCACHE
        head_mask = view(MX, 256)
        query_sum = view(MX + 256, 3, 8)
        assert MX + 280 <= 24576

        P = 24576
        consts = view(P, NCONST)
        P += NCONST
        ada_sb = view(P, 3, 512)
        P += 1536
        rows_t = view(P, 2, 32); P += 64
        g_attn = view(P, 8); P += 8
        z_last = view(P, 2, 18); P += 36
        z_nat = view(P, DC); P += 256
        rw_sb = view(P, KC, NE); P += 256
        rb_sb = view(P, NE); P += 32
        relb = view(P, 12); P += 12
        bias_sel = view(P, 2, 96); P += 192
        log_sel = view(P, 96); P += 96
        rank_t = view(P, 3, ITEMS + 1); P += 3 * (ITEMS + 1)
        gate_t = view(P, 3, ITEMS + 1); P += 3 * (ITEMS + 1)
        mask_t = view(P, 3, NE); P += 96
        lg = view(P, NE); P += NE
        ex = view(P, NE); P += NE
        flag_f = z_nat[:, 0:ITEMS + 2]
        flag_i = view(P, ITEMS + 2).bitcast(I32); P += ITEMS + 2
        cnt = view(P, NE); P += NE
        st = view(P, 96); P += 96
        idx_u = view(P, 8).bitcast(U32); P += 8
        idx_f = view(P, 8); P += 8
        lead = view(P, 8); P += 8
        R1, R2 = P, P + 3072
        R3 = R2 + 3072
        R4 = R3 + 8192
        R5 = R4 + 6144
        R6 = R5 + 1316 + 640
        assert R6 + 1920 <= TOTAL, R6 + 1920

        ident = consts[:, 0:128]
        tri = consts[:, 128:256]
        iota = consts[:, 256:384]
        ones = consts[:, 384:512]
        rep_p = consts[:, 512:640]
        rep_s = consts[:, 640:704]

        hb = view(R1, HEADS, 256)
        p_soft = view(R1, 3, 384)
        p_turn = view(R1 + 1152, 2, 384)
        s_bias = view(R1, SB)
        prob = view(R1 + SB, NCACHE + 64)
        x1 = view(R1, 3, D)
        p_bias = view(R2, HEADS, 256)
        pt_sb = view(R2, KB + 1, 96)
        qbd = view(R2 + (KB + 1) * 96, AC, 32)
        o_mask = view(R2 + (KB + 1) * 96 + AC * 32, 256)
        u2 = view(R2, 3, D)
        u_t = view(R3, KC, NTOK)
        k_nat = view(R3 + 2560, 3, DA)
        b_rows = view(R3 + 4864, 3, 512)
        c_sb = view(R3 + 6400, D)
        ada_t = view(R3 + 7424, 4, 128)
        c_t = view(R3 + 7936, KC, 32)
        wo_sb = view(R3, KC, D)
        acc = view(R3, 3, D)
        act_g = view(R3 + 3072, 2, 512)
        act_s = view(R3 + 4096, 2, 512)
        act_l = view(R3 + 5120, 2, 512)
        b_up = view(R3 + 6144, 2 * FF)
        fin_t = view(R3 + 3072, D)
        fin_y = view(R3 + 4096, 3, D)
        x_in = view(R4, 3, D)
        sig_c = view(R4 + 3 * D, D)
        rows = view(R4 + 4 * D, DC)
        g_rows = view(R4 + 4 * D + DC, 128)
        q_t = view(R4, AC, NTOK)
        k_t = view(R4 + 1920, AC, NTOK)
        v_nat = view(R4 + 3840, 3, DA)
        sq_a = view(R4, AC, NTOK)
        sq_c = view(R4 + AC * NTOK, CC, NTOK)
        norm_rep = view(R4 + (AC + CC) * NTOK, 2, NTOK)
        mix = view(R4, 2, D)
        u2_t = view(R4 + 3 * D, KC, 128)
        ln1 = view(R4 + 4 * D, 2, D)
        xe_t = view(R4, 2, 512)
        xe_nat = view(R4 + 4992, 2, 512)
        a_t = view(R4 + 1024, 2, 512)
        y_sb = view(R4 + 2048, 2, 512)
        sel = view(R4 + 3072, 3, 128)
        sel_g = view(R4 + 3456, 3, 4, 64)
        sel_t = view(R4 + 4224, 2, 384)
        z_p = view(R5, 2, SEQ + 2)
        z_s = view(R5 + 516, 2, 80)
        c_gate = view(R5 + 676, 2, NTOK)
        y_c = view(R5 + 1316, 2, NTOK)
        o_t = view(R6, AC, NTOK)
        tab_hot = view(R6, 384)
        tab_log = view(R6 + 384, 384)
        tab_sb = view(R6 + 768, 384)
        anti = view(R6 + 1152, 128)
        ln2 = view(R5, 2, D)
        bd_sb = view(R5 + 2 * D, D)
        gt_sb = view(R5 + 3 * D, NTOK)

        wada_d = t["w_ada"][0].rearrange("(k p) n -> p k n", p=128)
        win_d = t["w_in"][0].rearrange("(k p) n -> p k n", p=128)
        wo_d = t["w_o"][0].rearrange("(k p) n -> p k n", p=128)
        wup_d = t["w_up"][0].rearrange("e (k p) n -> e k p n", p=128)
        wdn_d = t["w_down"][0].rearrange("e (m k p) n -> e m p k n", p=128, k=2)
        ck = t["cache_k"][0].rearrange("b s h e -> b s (h e)")
        cv = t["cache_v"][0].rearrange("b s h e -> b s (h e)")

        ring_in = [sem(f"ring_in{s}") for s in range(SLOTS)]
        ada_used, ada_late, hot_in, k_rec_in, k_old_in, v_in, wo_in = map(
            sem, ("ada_used", "ada_late", "hot_in", "k_rec_in", "k_old_in", "v_in", "wo_in"))
        up_in = [sem(f"up_in{k}") for k in range(KC)]
        dn_in = [sem(f"dn_in{m}") for m in range(KC // 2)]
        bup_in, bup_used, up_used, dn_used = map(sem, ("bup_in", "bup_used", "up_used", "dn_used"))
        const_in, c_in, rows_in, bada_in, x_ready, tabc_in = map(
            sem, ("const_in", "c_in", "rows_in", "bada_in", "x_ready", "tabc_in"))
        zeroed, sig_done, c_ready, ct_done, ct_ready, rows_done, rows_ready = map(
            sem, ("zeroed", "sig_done", "c_ready", "ct_done", "ct_ready", "rows_done", "rows_ready"))
        xt_done, xt_copied, ada_ready, adat_done, u_ready = map(
            sem, ("xt_done", "xt_copied", "ada_ready", "adat_done", "u_ready"))
        tab_done, tab_ready, scr_out, hb_in, pb_done, pb_ready = map(
            sem, ("tab_done", "tab_ready", "scr_out", "hb_in", "pb_done", "pb_ready"))
        proj_done, proj_act, proj_dve = map(sem, ("proj_done", "proj_act", "proj_dve"))
        kn_done, kn_dve, kn_act, zl_ready, zn_done, zn_ready = map(
            sem, ("kn_done", "kn_dve", "kn_act", "zl_ready", "zn_done", "zn_ready"))
        out_kv, out_y = sem("out_kv"), sem("out_y")
        sb_done, sb_ready, bsel_ready = sem("sb_done"), sem("sb_ready"), sem("bsel_ready")
        ps_done, pmax_ready, pexp_ready, pnorm_ready, pt_done, pt_copied, pv_done, po_copied = map(
            sem, ("ps_done", "pmax_ready", "pexp_ready", "pnorm_ready", "pt_done", "pt_copied", "pv_done", "po_copied"))
        qbd_ready, kt_done, kt_dve, kt_act, s_done, s_max, s_exp, st_done, st_act, st_dve = map(
            sem, ("qbd_ready", "kt_done", "kt_dve", "kt_act", "s_done", "s_max", "s_exp", "st_done", "st_act", "st_dve"))
        v_used, sv_done, om_ready, so_done, so_copied = map(
            sem, ("v_used", "sv_done", "om_ready", "so_done", "so_copied"))
        tail_in, sq_ready, og_ready, ss_done, var_ready, sd_ready, wo_done, g1_done, c2_done = map(
            sem, ("tail_in", "sq_ready", "og_ready", "ss_done", "var_ready", "sd_ready", "wo_done", "g1_done", "c2_done"))
        mixed, gated, u2_ready, u2t_done, u2t_ready, lg_done, neg_ready, ex_ready, masks_ready = map(
            sem, ("mixed", "gated", "u2_ready", "u2t_done", "u2t_ready", "lg_done", "neg_ready", "ex_ready", "masks_ready"))
        rank_done, route_ready, gt_done, gt_ready, bd_done, acc_ready, late_in, ln2_in = map(
            sem, ("rank_done", "route_ready", "gt_done", "gt_ready", "bd_done", "acc_ready", "late_in", "ln2_in"))
        sel_ready, selg_ready, y_ready = sem("sel_ready"), sem("selg_ready"), sem("y_ready")
        g_ready, sig_ready, a_ready, at_done, at_ready = (
            [sem(f"{name}_{v}") for v in "ab"] for name in ("g_ready", "sig_ready", "a_ready", "at_done", "at_ready"))
        ga_done, xn_ready, xt2_done, xe_ready, selt_done, selt_ready, sc_done, sc_added = map(
            sem, ("ga_done", "xn_ready", "xt2_done", "xe_ready", "selt_done", "selt_ready", "sc_done", "sc_added"))
        g2_done, fin_mixed, y_done = sem("g2_done"), sem("fin_mixed"), sem("y_done")
        ch_v, ch_end = sem("vector_chain"), sem("vector_chain_at_the_end")

        UNITS = [("q", c, 128 * c, "act") for c in range(AC)]
        UNITS += [("k", c, DA + 128 * c, "dve") for c in range(AC)]
        UNITS += [("v", (tt, 0), 2 * DA, "act") for tt in range(3)]
        UNITS += [("v", (tt, 1), 2 * DA + 512, "dve") for tt in range(3)]
        UNITS += [("B", c, 3 * DA + 128 * c, "act") for c in range(CC)]
        for c in range(CC):
            UNITS += [("C", c, 3 * DA + DC + 128 * c, "act"), ("h", c, 3 * DA + 2 * DC + 128 * c, "dve")]
        VW = {0: 512, 1: 256}
        PB = 4
        ADA_BANK = (0, 4, 5)
        RING = [("ada", 0, kp) for kp in range(4)] + [("win", 0), ("win", 1), ("win", 2)]
        RING += [("ada", 1, 0), ("ada", 1, 1), ("ada", 1, 2), ("win", 3), ("ada", 1, 3), ("ada", 2, 0), ("ada", 2, 1),
                 ("win", 4), ("ada", 2, 2), ("ada", 2, 3), ("win", 5)]
        KN_AT = {12: 0, 13: 1, 14: 2}

        def copied(u):
            return sum(1 for w in UNITS[:u + 1] if w[3] == UNITS[u][3])

        def key_bank(n):
            return 3 + n % 4 if n < 12 else 3 + n % 2

        def used(n):
            if RING[n][0] == "ada":
                return ada_used, sum(1 for w in RING[:n + 1] if w[0] == "ada")
            return proj_done, sum(1 for u in UNITS if u[2] < 512 * RING[n][1] + 512)

        block = ctx.enter_context(nc.Block())

        @block.sync
        def _(sp):
            sp.dma_start(consts, t["consts"]).then_inc(const_in, 16)
            sp.wait_ge(zeroed, 1)
            sp.dma_start(c_sb[0:1, :], t["c_prompt"]).then_inc(c_in, 16)
            sp.dma_start(c_sb[1:1 + NB, :], t["c_sample"]).then_inc(c_in, 16)

            def small_inputs():
                sp.wait_ge(zeroed, 2)
                sp.dma_start(rows[0:16, :], t["state_conv"][0].rearrange("b i c -> (b i) c")).then_inc(rows_in, 16)
                sp.dma_start(rows[16:19, :], t["conv_w"][0]).then_inc(rows_in, 16)
                sp.dma_start(rows[19:20, :], t["norm_conv_g"]).then_inc(rows_in, 16)
                sp.dma_start(g_rows[0:AC, :], t["norm_attn_g"].rearrange("o (c p) -> (o c) p", p=128)).then_inc(rows_in, 16)
                sp.dma_start(x_in[:, 0:2, :], t["x_prompt"][0].rearrange("(a p) d -> p a d", p=128)).then_inc(x_ready, 16)
                sp.dma_start(x_in[0:64, 2, :], t["x_sample"].rearrange("b s d -> (b s) d")).then_inc(x_ready, 16)
                sp.dma_start(tab_hot[0:32, :], t["tab_hot"]).then_inc(tabc_in, 16)
                sp.dma_start(tab_log[0:1, :], t["tab_log"]).then_inc(tabc_in, 16)
                for q in range(4):
                    sp.dma_start(relb[32 * q:32 * q + 32, :], t["rel_bias"]).then_inc(tabc_in, 16)
                sp.dma_start(log_sel[0:8, :], t["log_sel"]).then_inc(tabc_in, 16)
                sp.dma_start(anti, t["anti"]).then_inc(tabc_in, 16)
                sp.dma_start(rw_sb, t["router_w"][0].rearrange("(k p) e -> p k e", p=128)).then_inc(tabc_in, 16)
                sp.dma_start(rb_sb[0:1, :], t["router_b"]).then_inc(tabc_in, 16)
                for j in range(4):
                    src = t["b_ada"].rearrange("o (m j c) -> j o m c", m=3, j=4)[j]
                    sp.dma_start(b_rows[32 * j:32 * j + 32], src.to_broadcast([32, 3, 512])).then_inc(bada_in, 16)

            for n, what in enumerate(RING):
                if n == 1:
                    small_inputs()
                if n >= SLOTS:
                    sp.wait_ge(*used(n - SLOTS))
                if what[0] == "ada":
                    _, m, kp = what
                    src, dst = wada_d[:, 2 * kp:2 * kp + 2, 2048 * m:2048 * m + 2048], ring_ada[n % SLOTS]
                else:
                    src, dst = win_d[:, :, 512 * what[1]:512 * what[1] + 512], ring_in_w[n % SLOTS]
                sp.dma_start(dst, src).then_inc(ring_in[n % SLOTS], 16)

            def load_rec(cache, sb, b, done):
                sp.dma_start(sb[:, 0:4, :], cache[b][:, PAST - REC:PAST, :].rearrange("o (p r) d -> (o p) r d", r=4)
                             ).then_inc(done, 16)

            def load_old(cache, sb, b, done):
                old = cache[b][:, 0:PAST - REC, :].rearrange("o (r g i) d -> i (o g) r d", r=6, g=16)
                for i in range(8):
                    sp.dma_start(sb[16 * i:16 * i + 16, 4:KB, :], old[i]).then_inc(done, 16)

            sp.wait_ge(*used(len(RING) - SLOTS + 1))
            load_rec(ck, k_sb, slice(0, 1), k_rec_in)
            load_old(ck, k_sb, slice(0, 1), k_old_in)
            sp.wait_ge(*used(len(RING) - SLOTS + 3))
            load_rec(cv, v_sb, slice(0, 1), v_in)
            load_old(cv, v_sb, slice(0, 1), v_in)
            sp.wait_ge(*used(len(RING) - 1))
            sp.dma_start(hot_s, t["hot_s"].rearrange("(a p) n -> p a n", p=128)).then_inc(hot_in, 16)
            sp.dma_start(log_s[0:8, :], t["log_s"]).then_inc(hot_in, 16)
            sp.dma_start(head_mask[0:96, :], t["head_mask"]).then_inc(hot_in, 16)
            sp.dma_start(query_sum[0:96], t["query_sum"].rearrange("p (a b) -> p a b", a=3)).then_inc(hot_in, 16)

            def load_keys(cache, b, before):
                sp.wait_ge(kt_done, before * 18 + AC)
                load_rec(cache, k_sb, b, k_rec_in)
                sp.wait_ge(kt_done, before * 18 + 3 * AC)
                load_old(cache, k_sb, b, k_old_in)

            def load_values(b, used):
                sp.wait_ge(v_used, used)
                load_rec(cv, v_sb, b, v_in)
                load_old(cv, v_sb, b, v_in)

            sp.wait_ge(out_kv, 96)
            sp.wait_ge(ada_late, 1)
            sp.dma_start(wo_sb, wo_d).then_inc(wo_in, 16)
            load_keys(ck, slice(1, 2), 0)
            with sp.Fori(1, NB - 1) as b:
                load_keys(ck[1:NB], bass.ds(b, 1), b)
                load_values(bass.ds(b, 1), b)
            load_values(slice(NB - 1, NB), NB - 1)
            def load_expert(e, slot_free):
                if slot_free is not None:
                    sp.wait_ge(bup_used, slot_free)
                sp.dma_start(b_up[0:1, :], t["b_up"][0, bass.ds(e, 1), :]).then_inc(bup_in, 16)

            sp.wait_ge(v_used, NB)
            sp.wait_ge(so_copied, NB)
            for k in range(KC):
                sp.dma_start(up_w[:, k, :], wup_d[0, k]).then_inc(up_in[k], 16)
            for m in range(KC // 2):
                sp.dma_start(dn_w[:, 2 * m:2 * m + 2, :], wdn_d[0, m]).then_inc(dn_in[m], 16)
            sp.wait_ge(route_ready, 1)
            load_expert(0, None)
            items = sp.value_load(flag_i[0:1, 0:1], min_val=NE, max_val=ITEMS)
            with sp.Fori(1, items) as i:
                e = i % NE
                load_expert(e, i)
                for k in range(KC):
                    sp.wait_ge(up_used, (i - 1) * KC + k + 1)
                    sp.dma_start(up_w[:, k, :], wup_d[bass.ds(e, 1), k].rearrange("o p n -> (o p) n")
                                 ).then_inc(up_in[k], 16)
                for m in range(KC // 2):
                    sp.wait_ge(dn_used, (i - 1) * (KC // 2) + m + 1)
                    sp.dma_start(dn_w[:, 2 * m:2 * m + 2, :], wdn_d[bass.ds(e, 1), m].rearrange(
                        "o p k n -> (o p) k n")).then_inc(dn_in[m], 16)
            sp.wait_ge(y_done, 2)
            sp.dma_start(out[0][0].rearrange("(a p) d -> p a d", p=128), fin_y[:, 0:2, :]).then_inc(out_y, 16)
            sp.wait_ge(y_done, 3)
            sp.dma_start(out[1].rearrange("b s d -> (b s) d"), fin_y[0:64, 2, :]).then_inc(out_y, 16)
            sp.wait_ge(out_y, 32)

        @block.gpsimd
        def _(pool):
            pool.wait_ge(tab_ready, 1)
            pool.dma_start(scratch, tab_sb[0:HEADS, :]).then_inc(scr_out, 16)
            pool.wait_ge(scr_out, 16)
            pool.dma_start(hb, bass.AP(scratch.tensor, 0, [[1, 128], [384, HEADS], [1, 256]])).then_inc(hb_in, 16)
            pool.wait_ge(kn_dve, 3)
            pool.wait_ge(kn_act, 3)
            pool.dma_start(out[2][0, 0].rearrange("(a p) h e -> p a (h e)", p=128), k_nat[:, 0:2, :]).then_inc(out_kv, 16)
            pool.dma_start(out[5][0].rearrange("b s h e -> (b s) (h e)"), k_nat[0:64, 2, :]).then_inc(out_kv, 16)
            pool.wait_ge(proj_act, len([w for w in UNITS if w[3] == "act"]))
            pool.wait_ge(proj_dve, len([w for w in UNITS if w[3] == "dve"]))
            pool.dma_start(out[3][0, 0].rearrange("(a p) h e -> p a (h e)", p=128), v_nat[:, 0:2, :]).then_inc(out_kv, 16)
            pool.dma_start(out[6][0].rearrange("b s h e -> (b s) (h e)"), v_nat[0:64, 2, :]).then_inc(out_kv, 16)
            pool.wait_ge(zn_ready, 1)
            pool.dma_start(out[4][0, 0], z_nat[0:2, :]).then_inc(out_kv, 16)
            pool.dma_start(out[7][0].rearrange("b s c -> (b s) c"), z_nat[2:18, :]).then_inc(out_kv, 16)
            pool.wait_ge(out_kv, 96)
            pool.wait_ge(so_copied, NB)
            pool.dma_start(x1[:, 0:2, :], t["x_prompt"][0].rearrange("(a p) d -> p a d", p=128)).then_inc(tail_in, 16)
            pool.dma_start(x1[0:64, 2, :], t["x_sample"].rearrange("b s d -> (b s) d")).then_inc(tail_in, 16)
            for a, name in enumerate(("ln1_g", "ln1_b")):
                pool.dma_start(ln1[:, a, :], t[name][0:1, :].to_broadcast([128, D])).then_inc(tail_in, 16)
            pool.wait_ge(wo_done, 3)
            pool.wait_ge(mixed, 3)
            pool.dma_start(bd_sb[0:NE, :], t["b_down"][0]).then_inc(late_in, 16)
            for a, name in enumerate(("ln2_g", "ln2_b")):
                pool.dma_start(ln2[:, a, :], t[name][0:1, :].to_broadcast([128, D])).then_inc(ln2_in, 16)

        @block.scalar
        def _(act):
            act.wait_ge(c_in, 32)
            nc.scalar.activation(sig_c[0:32, :], c_sb[0:32, :], ACT.Sigmoid).then_inc(sig_done, 1)

            def act_keys(tt):
                n = TILES[tt][1]
                act.wait_ge(kn_done, tt + 1)
                nc.scalar.copy(k_nat[0:n, tt, 512:DA], bank(7)[0:n, 0:256]).then_inc(kn_act, 1)

            for u, (kind, c, _, eng) in enumerate(UNITS):
                if u - 1 in KN_AT:
                    act_keys(KN_AT[u - 1])
                if eng != "act":
                    continue
                act.wait_ge(proj_done, u + 1)
                src = bank(u % PB)
                if kind == "q":
                    ins = nc.scalar.mul(q_t[:, c, :], src[:, 0:NTOK], HD ** -0.5)
                elif kind == "C":
                    ins = nc.scalar.copy(c_gate[:, c, :], src[:, 0:NTOK])
                elif kind == "B":
                    ins = nc.scalar.copy(y_c[:, c, :], src[:, 0:NTOK])
                else:
                    n = TILES[c[0]][1]
                    ins = nc.scalar.copy(v_nat[0:n, c[0], 0:512], src[0:n, 0:512])
                ins.then_inc(proj_act, 1)

            for s in range(HEADS + 3):
                if s < HEADS:
                    act.wait_ge(pmax_ready, s + 1)
                    for q, (a, z) in enumerate(((0, 128), (128, 384))):
                        ins = nc.scalar.activation(p_soft[:, s % 3, a:z], p_soft[:, s % 3, a:z], ACT.Exp,
                                                   bias=st[:, 4 * (s % 2) + 2 + q:4 * (s % 2) + 3 + q],
                                                   accum_out=st[:, 8 + 2 * (s % 2) + q:9 + 2 * (s % 2) + q])
                    ins.then_inc(pexp_ready, 1)
                if 2 <= s <= HEADS + 1:
                    h = s - 2
                    act.wait_ge(pt_done, h + 1)
                    if h >= 2:
                        act.wait_ge(pv_done, h - 1)
                    nc.scalar.copy(p_turn[:, h % 2, :], bank(2 + h % 2, 0, 384)).then_inc(pt_copied, 1)
                if s >= 4 and s % 2 == 0:
                    c = (s - 4) // 2
                    act.wait_ge(pv_done, s - 2)
                    nc.scalar.copy(o_t[:, c, 0:SEQ], bank(4 + c % 2, 0, SEQ)).then_inc(po_copied, 1)

            act.sem_inc(kt_act, 1)

            def act_turned(kt, b, chunks=(1, 3, 5)):
                for c in chunks:
                    w = 512 if kt < 2 else 256
                    act.wait_ge(kt_done, b * 18 + kt * AC + c + 1)
                    nc.scalar.copy(kt_sb[:, c, 512 * kt:512 * kt + w], bank(key_bank(kt * AC + c), 0, w)).then_inc(kt_act, 1)

            def act_batch(b, more):
                if more:
                    act_turned(0, b + 1, (1,))
                act.wait_ge(s_max, b + 2)
                nc.scalar.activation(prob[0:96, :], prob[0:96, :], ACT.Exp, bias=st[0:96, 14:15],
                                     accum_out=st[0:96, 15:16]).then_inc(s_exp, 1)
                if more:
                    act_turned(0, b + 1, (3, 5))
                    act_turned(1, b + 1)
                act.wait_ge(st_done, b * 3 + 1)
                nc.scalar.copy(pt_sb[:, 0:5, :], bank(5, 0, 480).rearrange("p (a b) -> p a b", a=5)).then_inc(st_act, 1)
                if more:
                    act_turned(2, b + 1)

            for kt in range(3):
                act_turned(kt, 0)
            with act.Fori(0, NB - 1) as b:
                act_batch(b, True)
            act_batch(NB - 1, False)

            act.wait_ge(so_copied, NB)
            act.wait_ge(var_ready, 1)
            nc.scalar.activation(norm_rep, norm_rep, ACT.Sqrt).then_inc(sd_ready, 1)

            def act_mix(tt):
                n = TILES[tt][1]
                act.wait_ge(wo_done, tt + 1)
                nc.scalar.copy(mix[0:n, tt % 2, :], ps[0:n, 1024 * (tt % 2):1024 * (tt % 2) + 1024]).then_inc(mixed, 1)

            def act_root(tt):
                n = TILES[tt][1]
                act.wait_ge(var_ready, tt + 2)
                nc.scalar.activation(st[0:n, 36:37], st[0:n, 35:36], ACT.Sqrt).then_inc(sd_ready, 1)

            def act_turn(tt):
                n = TILES[tt][1]
                for h in range(2):
                    act.wait_ge(u2t_done, 2 * tt + h + 1)
                    nc.scalar.copy(u2_t[:, 4 * h:4 * h + 4, 0:n],
                                   bank(6 + h).rearrange("p (a b) -> p a b", a=4)[:, :, 0:n]).then_inc(u2t_ready, 1)

            def act_exp(tt):
                n = TILES[tt][1]
                act.wait_ge(neg_ready, tt + 1)
                nc.scalar.activation(ex[0:n, :], lg[0:n, :], ACT.Exp, bias=st[0:n, 40:41]).then_inc(ex_ready, 1)

            for step, tt in ((act_mix, 0), (act_root, 0), (act_mix, 1), (act_turn, 0), (act_root, 1), (act_exp, 0),
                             (act_mix, 2), (act_turn, 1), (act_root, 2), (act_exp, 1), (act_turn, 2), (act_exp, 2)):
                step(tt)
            act.wait_ge(gt_done, 1)
            nc.scalar.copy(gt_sb[0:NE, :], bank(6, 0, NTOK)[0:NE]).then_inc(gt_ready, 1)
            act.wait_ge(bd_done, 1)
            for tt, (a, n) in enumerate(TILES):
                ins = nc.scalar.copy(acc[0:n, tt, :], ps[0:n, 1024 * tt:1024 * tt + 1024])
            ins.then_inc(acc_ready, 1)

            act.wait_ge(route_ready, 1)
            for counted_from_one in (y_ready, selt_ready):
                act.sem_inc(counted_from_one, 1)
            items = act.value_load(flag_i[0:1, 0:1], min_val=NE, max_val=ITEMS)

            def gathered(blocks, turn_no):
                act.wait_ge(ga_done, turn_no)
                for v in reversed(range(blocks)):
                    ins = nc.scalar.copy(xe_nat[:, v, :], bank(4 + v))
                ins.then_inc(xn_ready, 1)

            gathered(2, 1)
            with act.Fori(0, items) as i:
                now_b = act.value_load(flag_i[0:1, bass.ds(i + 1, 1)], min_val=0, max_val=1)
                next_b = act.value_load(flag_i[0:1, bass.ds(i + 2, 1)], min_val=0, max_val=1)

                def sigmoid(v):
                    act.wait_ge(g_ready[v], i + 1)
                    nc.scalar.activation(act_s[:, v, :], act_g[:, v, :], ACT.Sigmoid, scale=1.702
                                         ).then_inc(sig_ready[v], 1)

                def turned(v):
                    act.wait_ge(at_done[v], i + 1)
                    nc.scalar.copy(a_t[:, v, :], bank(2 * v)).then_inc(at_ready[v], 1)

                sigmoid(0)
                with act.If(now_b > 0):
                    sigmoid(1)
                with act.Else():
                    act.sem_inc(sig_ready[1], 1)
                with act.If(next_b > 0):
                    gathered(2, i + 2)
                with act.Else():
                    gathered(1, i + 2)
                turned(0)
                with act.If(now_b > 0):
                    turned(1)
                with act.Else():
                    act.sem_inc(at_ready[1], 1)
                with act.If(now_b > 0):
                    act.wait_ge(dn_used, i * (KC // 2) + KC // 2)
                    nc.scalar.copy(y_sb[:, 1, :], bank(2))
                    nc.scalar.copy(y_sb[:, 0, :], bank(3)).then_inc(y_ready, 1)
                with act.Else():
                    act.wait_ge(dn_used, i * (KC // 2) + KC // 2)
                    nc.scalar.copy(y_sb[:, 0, :], bank(3)).then_inc(y_ready, 1)
                act.wait_ge(selt_done, i + 2)
                for v in range(2):
                    ins = nc.scalar.copy(sel_t[:, v, 0:320], bank(6 + v, 0, 320))
                ins.then_inc(selt_ready, 1)
            for tt, (a, n) in enumerate(TILES):
                act.wait_ge(var_ready, 5 + tt)
                nc.scalar.activation(st[0:n, 36:37], st[0:n, 35:36], ACT.Sqrt).then_inc(sd_ready, 1)

        @block.vector
        def _(dve):
            V = Chain(dve, ch_v)
            v_ = nc.vector
            v_.memset(c_sb[0:32, :], 0.0).then_inc(zeroed, 1)
            v_.memset(rows[0:32, :], 0.0)
            v_.memset(z_p[:, :, 0:2], 0.0)
            v_.memset(g_rows[0:8, :], 0.0).then_inc(zeroed, 1)
            dve.wait_ge(sig_done, 1)
            v_.tensor_tensor(c_sb[0:32, :], c_sb[0:32, :], sig_c[0:32, :], ALU.mult).then_inc(c_ready, 1)
            dve.wait_ge(ct_done, 1)
            v_.tensor_copy(c_t, bank(7, 0, 256).rearrange("p (a b) -> p a b", a=KC)).then_inc(ct_ready, 1)
            dve.wait_ge(rows_done, 1)
            v_.tensor_copy(rows_t, bank(6, 0, 64).rearrange("p (a b) -> p a b", a=2))
            v_.tensor_copy(g_attn, bank(6, 64, 72)).then_inc(rows_ready, 1)
            dve.wait_ge(rows_ready, 1)
            V(v_.tensor_copy(z_s.rearrange("p c (b t) -> p c b t", b=NB)[:, :, :, 0:2],
                             rows_t[:, :, 0:16].rearrange("p c (b t) -> p c b t", b=NB)))
            for c in range(KC):
                dve.wait_ge(xt_done, c + 1)
                v_.tensor_copy(u_t[:, c, :], bank(4 + c % 2, 0, NTOK)).then_inc(xt_copied, 1)
            dve.wait_ge(tabc_in, 160)
            V(v_.memset(bias_sel, 0.0))
            for kc in range(2):
                for q in range(4):
                    cols = bias_sel[32 * q:32 * q + 32, kc, 4 * kc + q:96:NS]
                    ins = v_.tensor_copy(cols, relb[32 * q:32 * q + 32, :])
            ins.then_inc(bsel_ready, 1)
            dve.wait_ge(tab_done, 1)
            v_.tensor_copy(tab_sb[0:HEADS, :], bank(6, 0, 384)[0:HEADS]).then_inc(tab_ready, 1)
            dve.wait_ge(bada_in, 64)
            dve.wait_ge(ada_used, 4)
            v_.tensor_tensor(ada_sb[:, 0, :], bank(ADA_BANK[0]), b_rows[:, 0, :], ALU.add).then_inc(ada_ready, 1)
            dve.wait_ge(adat_done, 1)
            src = bank(3).rearrange("p (a b) -> p a b", a=4)
            v_.tensor_copy(ada_t[:, :, 0:64], src[:, :, 0:64])
            V(v_.tensor_scalar(ada_t[:, :, 64:128], src[:, :, 64:128], 1.0, None, ALU.add))
            dve.wait_ge(xt_copied, KC)
            for c in range(KC):
                cb, j = c % 4, c // 4
                sh, sc = ada_t[:, cb, 32 * j:32 * j + 9], ada_t[:, cb, 64 + 32 * j:64 + 32 * j + 9]
                v_.tensor_scalar(u_t[:, c, 0:SEQ], u_t[:, c, 0:SEQ], sc[:, 0:1], sh[:, 0:1], ALU.mult, ALU.add)
                us = u_t[:, c, SEQ:NTOK].rearrange("p (b t) -> p b t", b=NB)
                V(v_.tensor_tensor(us, us, sc[:, 1:9].unsqueeze(2).to_broadcast([128, NB, NS]), ALU.mult))
                ins = v_.tensor_tensor(us, us, sh[:, 1:9].unsqueeze(2).to_broadcast([128, NB, NS]), ALU.add)
            ins.then_inc(u_ready, 1)
            def dve_keys(tt):
                n = TILES[tt][1]
                dve.wait_ge(kn_done, tt + 1)
                v_.tensor_copy(k_nat[0:n, tt, 0:512], bank(6)[0:n]).then_inc(kn_dve, 1)

            for u, (kind, c, _, eng) in enumerate(UNITS):
                if u - 1 in KN_AT:
                    dve_keys(KN_AT[u - 1])
                if eng != "dve":
                    continue
                dve.wait_ge(proj_done, u + 1)
                src = bank(u % PB)
                if kind == "k":
                    v_.tensor_copy(k_t[:, c, :], src[:, 0:NTOK]).then_inc(proj_dve, 1)
                    dve.wait_ge(pb_done, c + 1)
                    v_.tensor_copy(p_bias[:, 2 * c:2 * c + 2, :], bank(6 + c % 2).rearrange("p (a b) -> p a b", a=2)
                                   ).then_inc(pb_ready, 1)
                    continue
                elif kind == "h":
                    dve.wait_ge(proj_act, copied(u - 1))
                    v_.tensor_tensor(z_p[:, c, 2:SEQ + 2], src[:, 0:SEQ], c_gate[:, c, 0:SEQ], ALU.mult)
                    ins = v_.tensor_tensor(z_s[:, c, :].rearrange("p (b t) -> p b t", b=NB)[:, :, 2:10],
                                           src[:, SEQ:NTOK].rearrange("p (b t) -> p b t", b=NB),
                                           c_gate[:, c, SEQ:NTOK].rearrange("p (b t) -> p b t", b=NB), ALU.mult)
                else:
                    n = TILES[c[0]][1]
                    ins = v_.tensor_copy(v_nat[0:n, c[0], 512:DA], src[0:n, 0:256])
                ins.then_inc(proj_dve, 1)
            dve.wait_ge(ada_used, 12)
            for m in (1, 2):
                ins = v_.tensor_tensor(ada_sb[:, m, :], bank(ADA_BANK[m]), b_rows[:, m, :], ALU.add)
            ins.then_inc(ada_late, 1)
            dve.wait_ge(proj_dve, len([w for w in UNITS if w[3] == "dve"]))
            zs4 = z_s.rearrange("p c (b t) -> p c b t", b=NB)
            v_.tensor_copy(z_last[:, :, 0:2], z_p[:, :, SEQ:SEQ + 2])
            v_.tensor_copy(z_last[:, :, 2:18].rearrange("p c (b t) -> p c b t", b=NB), zs4[:, :, :, 8:10]
                           ).then_inc(zl_ready, 1)
            dve.wait_ge(proj_act, len([w for w in UNITS if w[3] == "act"]))
            for c in range(CC):
                wc = rows_t[:, c, 16:19]
                zs, cs = zs4[:, c], c_gate[:, c, SEQ:NTOK].rearrange("p (b t) -> p b t", b=NB)
                cp = c_gate[:, c, 0:SEQ]
                v_.tensor_scalar(cp, z_p[:, c, 0:SEQ], wc[:, 0:1], None, ALU.mult)
                V(v_.tensor_scalar(cs, zs[:, :, 0:8], wc[:, 0:1], None, ALU.mult))
                for w in (1, 2):
                    v_.scalar_tensor_tensor(cp, z_p[:, c, w:SEQ + w], wc[:, w:w + 1], cp, ALU.mult, ALU.add)
                    V(v_.scalar_tensor_tensor(cs, zs[:, :, w:w + 8], wc[:, w:w + 1], cs, ALU.mult, ALU.add))
                V(v_.tensor_tensor(y_c[:, c, :], y_c[:, c, :], c_gate[:, c, :], ALU.mult))
            dve.wait_ge(zn_done, 1)
            v_.tensor_copy(z_nat[0:18, :], bank(6, 0, 256)[0:18]).then_inc(zn_ready, 1)

            dve.wait_ge(pb_ready, 6)
            for s in range(HEADS + 1):
                if s < HEADS:
                    dve.wait_ge(ps_done, s + 1)
                    if s >= 3:
                        dve.wait_ge(pt_done, s - 2)
                    o = 4 * (s % 2)
                    v_.tensor_tensor_reduce(p_soft[:, s % 3, 0:128], bank(s % 2, 0, 128), p_bias[:, s, 128:256], 1.0,
                                            -3e38, ALU.add, ALU.max, st[:, o:o + 1])
                    V(v_.tensor_tensor_reduce(p_soft[:, s % 3, 128:384], bank(s % 2, 128, 384), p_bias[:, s, :], 1.0,
                                              -3e38, ALU.add, ALU.max, st[:, o + 1:o + 2]))
                    v_.tensor_scalar(st[:, o + 2:o + 4], st[:, o:o + 2], -1.0, None, ALU.mult).then_inc(pmax_ready, 1)
                if s >= 1:
                    h = s - 1
                    dve.wait_ge(pexp_ready, s)
                    r = 8 + 2 * (h % 2)
                    V(v_.reciprocal(st[:, r:r + 2], st[:, r:r + 2]))
                    v_.tensor_scalar(p_soft[:, h % 3, 0:128], p_soft[:, h % 3, 0:128], st[:, r:r + 1], None, ALU.mult)
                    v_.tensor_scalar(p_soft[:, h % 3, 128:384], p_soft[:, h % 3, 128:384], st[:, r + 1:r + 2], None,
                                     ALU.mult).then_inc(pnorm_ready, 1)
            dve.wait_ge(sb_done, 1)
            V(v_.tensor_copy(s_bias[0:96, :], ps[0:96, 0:SB]))
            dve.sem_inc(sb_ready, 1)

            dve.wait_ge(pt_done, HEADS)
            V(v_.memset(qbd, 0.0))
            dve.sem_inc(kt_dve, 1)
            dve.sem_inc(s_max, 1)

            def dve_turned(kt, b):
                for c in range(0, AC, 2):
                    w = 512 if kt < 2 else 256
                    dve.wait_ge(kt_done, b * 18 + kt * AC + c + 1)
                    v_.tensor_copy(kt_sb[:, c, 512 * kt:512 * kt + w], bank(key_bank(kt * AC + c), 0, w)).then_inc(kt_dve, 1)

            def queries(cols):
                for par in range(2):
                    for half in range(2):
                        lo = 16 * par + 8 * half
                        ins = v_.tensor_copy(qbd[64 * half:64 * half + 64, par:AC:2, lo:lo + 8],
                                             q_t[64 * half:64 * half + 64, par:AC:2, cols])
                ins.then_inc(qbd_ready, 1)

            def dve_batch(b, more):
                dve.wait_ge(s_done, b + 1)
                at = b * -NS + SB - 64
                v_.scalar_tensor_tensor(prob[0:96, NCACHE:NCACHE + 64], ps[0:96, NCACHE:NCACHE + 64], 1.0,
                                        s_bias[0:96, bass.ds(at, 64)], ALU.mult, ALU.add)
                V(v_.tensor_tensor_reduce(prob[0:96, 0:NCACHE], ps[0:96, 0:NCACHE], s_bias[0:96, 0:NCACHE], 1.0, -3e38,
                                          ALU.add, ALU.max, st[0:96, 12:13]))
                V(v_.tensor_reduce(st[0:96, 13:14], prob[0:96, NCACHE:NCACHE + 64], AX.X, ALU.max))
                v_.tensor_scalar(st[0:96, 14:15], st[0:96, 12:13], st[0:96, 13:14], -1.0, ALU.max, ALU.mult
                                 ).then_inc(s_max, 1)
                if more:
                    queries(bass.ds(b * NS + SEQ + NS, NS))
                    dve_turned(0, b + 1)
                    dve_turned(1, b + 1)
                dve.wait_ge(st_done, b * 3 + 2)
                v_.tensor_copy(pt_sb[:, 5:10, :], bank(6, 0, 480).rearrange("p (a b) -> p a b", a=5)).then_inc(st_dve, 1)
                dve.wait_ge(st_done, b * 3 + 3)
                v_.tensor_copy(pt_sb[0:64, KB, :], bank(7, 256, 352)[0:64]).then_inc(st_dve, 1)
                if more:
                    dve_turned(2, b + 1)
                dve.wait_ge(s_exp, b + 1)
                V(v_.reciprocal(st[0:96, 15:16], st[0:96, 15:16]))
                dve.wait_ge(sv_done, b + 1)
                v_.scalar_tensor_tensor(o_mask[0:96, :], bank(7, 0, 256)[0:96], st[0:96, 15:16], head_mask[0:96, :],
                                        ALU.mult, ALU.mult).then_inc(om_ready, 1)
                dve.wait_ge(so_done, b + 1)
                v_.tensor_copy(o_t[:, :, bass.ds(b * NS + SEQ, NS)], bank(7, 352, 400).rearrange("p (a b) -> p a b", a=AC)
                               ).then_inc(so_copied, 1)

            queries(slice(SEQ, SEQ + NS))
            for kt in range(3):
                dve_turned(kt, 0)
            with dve.Fori(0, NB - 1) as b:
                V.enter(b, 3)
                dve_batch(b, True)
            V.leave(NB - 1)
            dve_batch(NB - 1, False)

            dve.wait_ge(so_copied, NB)
            dve.wait_ge(po_copied, AC)
            dve.wait_ge(out_kv, 96)
            v_.tensor_tensor(sq_a, o_t, o_t, ALU.mult)
            v_.tensor_tensor(sq_c, y_c, y_c, ALU.mult).then_inc(sq_ready, 1)
            dve.wait_ge(ss_done, 1)
            v_.tensor_scalar(norm_rep[:, 0, :], bank(6, 0, NTOK), 1.0 / DA, RMS_EPS, ALU.mult, ALU.add)
            v_.tensor_scalar(norm_rep[:, 1, :], bank(7, 0, NTOK), 1.0 / DC, RMS_EPS, ALU.mult, ALU.add
                             ).then_inc(var_ready, 1)
            dve.wait_ge(sd_ready, 1)
            V(v_.reciprocal(norm_rep, norm_rep))
            for c in range(AC):
                v_.scalar_tensor_tensor(o_t[:, c, :], o_t[:, c, :], g_attn[:, c:c + 1], norm_rep[:, 0, :], ALU.mult,
                                        ALU.mult)
            for c in range(CC):
                ins = v_.scalar_tensor_tensor(y_c[:, c, :], y_c[:, c, :], rows_t[:, c, 19:20], norm_rep[:, 1, :],
                                              ALU.mult, ALU.mult)
            ins.then_inc(og_ready, 1)

            def residual(tt):
                n = TILES[tt][1]
                m = mix[0:n, tt % 2, :]
                dve.wait_ge(mixed, tt + 1)
                dve.wait_ge(g1_done, tt + 1)
                V(v_.scalar_tensor_tensor(m, ps[0:n, 2048:3072], 1.0, m, ALU.add, ALU.mult))
                dve.sem_inc(gated, 1)
                dve.wait_ge(tail_in, 64)
                x_t = x1[0:n, tt, :]
                V(v_.scalar_tensor_tensor(x_t, x_t, ALPHA, m, ALU.mult, ALU.add))
                layer_norm(dve, V, v_, x_t, n, st, ln1, var_ready, sd_ready, tt + 2, x_t)
                dve.wait_ge(c2_done, tt + 1)
                V(v_.scalar_tensor_tensor(u2[0:n, tt, :], ps[0:n, 1024 * (tt % 2):1024 * (tt % 2) + 1024], 1.0, x_t,
                                          ALU.add, ALU.mult))
                V(v_.tensor_tensor(u2[0:n, tt, :], u2[0:n, tt, :], ps[0:n, 2048:3072], ALU.add))
                dve.sem_inc(u2_ready, 1)

            def route(tt):
                n = TILES[tt][1]
                dve.wait_ge(lg_done, tt + 1)
                V(v_.tensor_copy(lg[0:n, :], bank(6, 0, NE)[0:n]))
                V(v_.max(lead[0:n, :], lg[0:n, :]))
                v_.tensor_scalar(st[0:n, 40:41], lead[0:n, 0:1], -1.0, None, ALU.mult).then_inc(neg_ready, 1)
                V(v_.max_index(idx_u[0:n, :], lead[0:n, :], lg[0:n, :]))
                V(v_.tensor_copy(idx_f[0:n, :], idx_u[0:n, :]))
                mk = mask_t[0:n, tt, :]
                V(v_.tensor_scalar(mk, iota[0:n, 0:NE], idx_f[0:n, 0:1], None, ALU.is_equal))
                for j in range(1, 4):
                    V(v_.scalar_tensor_tensor(mk, iota[0:n, 0:NE], idx_f[0:n, j:j + 1], mk, ALU.is_equal, ALU.add))
                dve.wait_ge(ex_ready, tt + 1)
                V(v_.tensor_tensor_reduce(ex[0:n, :], ex[0:n, :], mk, 1.0, 0.0, ALU.mult, ALU.add, st[0:n, 41:42]))
                V(v_.reciprocal(st[0:n, 41:42], st[0:n, 41:42]))
                for r in range(ROUNDS):
                    v_.tensor_scalar(gate_t[0:n, tt, NE * r:NE * r + NE], ex[0:n, :], st[0:n, 41:42], None, ALU.mult)
                V(v_.memset(gate_t[0:n, tt, ITEMS:ITEMS + 1], 0.0))

            for step, tt in ((residual, 0), (residual, 1), (route, 0), (residual, 2), (route, 1), (route, 2)):
                step(tt)
            dve.sem_inc(masks_ready, 1)
            v_.memset(y_sb, 0.0)
            V(v_.memset(sel_t, 0.0))
            dve.wait_ge(rank_done, 1)
            for tt, (a, n) in enumerate(TILES):
                mk, rk = mask_t[0:n, tt, :], rank_t[0:n, tt, :]
                V(v_.scalar_tensor_tensor(rk[:, 0:NE], bank(7)[0:n, NE * tt:NE * tt + NE], FAR, mk, ALU.add, ALU.mult))
                V(v_.tensor_scalar(rk[:, 0:NE], rk[:, 0:NE], -FAR, None, ALU.add))
                for r in range(1, ROUNDS):
                    v_.tensor_scalar(rk[:, NE * r:NE * r + NE], rk[:, 0:NE], -128.0 * r, None, ALU.add)
                V(v_.memset(rk[:, ITEMS:ITEMS + 1], -FAR))

            def choose(i, which):
                for tt, (_, n) in enumerate(TILES):
                    if which == "sel":
                        ins = v_.tensor_scalar(sel[0:n, tt, :], iota[0:n, :], rank_t[0:n, tt, bass.ds(i, 1)], None,
                                               ALU.is_equal)
                    else:
                        ins = v_.tensor_scalar(
                            sel_g[0:n, tt].rearrange("p (v d) s -> p v d s", v=2),
                            iota[0:n, :].rearrange("p (v s) -> p v s", v=2).unsqueeze(2).to_broadcast([n, 2, 2, 64]),
                            rank_t[0:n, tt, bass.ds(i, 1)], gate_t[0:n, tt, bass.ds(i, 1)], ALU.is_equal, ALU.mult)
                return ins

            def add_back(tt, banks):
                n = TILES[tt][1]
                for h in range(2):
                    ins = v_.tensor_tensor(acc[0:n, tt, 512 * h:512 * h + 512], acc[0:n, tt, 512 * h:512 * h + 512],
                                           bank(banks[h])[0:n], ALU.add)
                return ins

            choose(0, "sel").then_inc(sel_ready, 1)
            V(v_.tensor_copy(cnt[0:1, :], bank(7)[0:1, NE * 3:NE * 4]))
            V(v_.tensor_reduce(st[0:1, 44:45], cnt[0:1, :], AX.X, ALU.max))
            V(v_.memset(flag_f[0:1, :], 0.0))
            for r in range(ROUNDS):
                v_.tensor_scalar(flag_f[0:1, 1 + NE * r:1 + NE * r + NE], cnt[0:1, :], 128.0 * r + 64.5, None, ALU.is_gt)
            V(v_.tensor_scalar(st[0:1, 45:46], st[0:1, 44:45], 128.5, float(NE), ALU.is_gt, ALU.mult))
            V(v_.tensor_scalar(st[0:1, 46:47], st[0:1, 44:45], 256.5, float(NE), ALU.is_gt, ALU.mult))
            V(v_.tensor_tensor(st[0:1, 45:46], st[0:1, 45:46], st[0:1, 46:47], ALU.add))
            V(v_.tensor_scalar(flag_f[0:1, 0:1], st[0:1, 45:46], float(NE), None, ALU.add))
            V(v_.tensor_copy(flag_i[0:1, :], flag_f[0:1, :]))
            dve.sem_inc(sc_added, 1)
            dve.sem_inc(route_ready, 1)

            def gathered_turned(blocks, turn_no):
                dve.wait_ge(xt2_done, turn_no)
                for v in range(blocks):
                    ins = v_.tensor_copy(xe_t[:, v, :], bank(1 + 2 * v))
                ins.then_inc(xe_ready, 1)

            gathered_turned(2, 1)
            items = dve.value_load(flag_i[0:1, 0:1], min_val=NE, max_val=ITEMS)
            with dve.Fori(0, items) as i:
                V.enter(i, 4)
                now_b = dve.value_load(flag_i[0:1, bass.ds(i + 1, 1)], min_val=0, max_val=1)
                next_b = dve.value_load(flag_i[0:1, bass.ds(i + 2, 1)], min_val=0, max_val=1)
                dve.wait_ge(ga_done, i + 1)
                choose(i + 1, "sel").then_inc(sel_ready, 1)
                dve.wait_ge(selt_done, i + 1)
                choose(i, "gated").then_inc(selg_ready, 1)

                def swiglu(v):
                    v_.tensor_scalar(act_g[:, v, :], bank(2 * v), 7.0, None, ALU.min).then_inc(g_ready[v], 1)
                    V(v_.tensor_scalar(act_l[:, v, :], bank(2 * v + 1), 7.0, -7.0, ALU.min, ALU.max))
                    V(v_.scalar_tensor_tensor(act_l[:, v, :], act_l[:, v, :], 1.0, act_g[:, v, :], ALU.add, ALU.mult))
                    dve.wait_ge(sig_ready[v], i + 1)
                    v_.tensor_tensor(act_l[:, v, :], act_l[:, v, :], act_s[:, v, :], ALU.mult).then_inc(a_ready[v], 1)

                dve.wait_ge(up_used, i * KC + KC)
                swiglu(0)
                with dve.If(now_b > 0):
                    swiglu(1)
                with dve.Else():
                    dve.sem_inc(ch_v, 2)
                    dve.sem_inc(g_ready[1], 1)
                    dve.sem_inc(a_ready[1], 1)
                with dve.If(next_b > 0):
                    gathered_turned(2, i + 2)
                with dve.Else():
                    gathered_turned(1, i + 2)
                for tt in range(3):
                    dve.wait_ge(sc_done, i * 3 + tt + 1)
                    add_back(tt, ((6, 7), (4, 5), (6, 7))[tt]).then_inc(sc_added, 1)
            V.leave(items)
            for tt in range(3):
                dve.wait_ge(sc_done, items * 3 + tt + 1)
                add_back(tt, ((6, 7), (4, 5), (6, 7))[tt]).then_inc(sc_added, 1)
            V = Chain(dve, ch_end)
            dve.wait_ge(sc_added, items * 3 + 4)
            dve.wait_ge(ln2_in, 32)
            for tt, (a, n) in enumerate(TILES):
                dve.wait_ge(g2_done, tt + 1)
                V(v_.scalar_tensor_tensor(fin_t[0:n], ps[0:n, 1024 * tt:1024 * tt + 1024], 1.0, acc[0:n, tt, :],
                                          ALU.add, ALU.mult))
                V(v_.scalar_tensor_tensor(fin_t[0:n], x1[0:n, tt, :], ALPHA, fin_t[0:n], ALU.mult, ALU.add))
                layer_norm(dve, V, v_, fin_t[0:n], n, st, ln2, var_ready, sd_ready, 5 + tt, fin_y[0:n, tt, :])
                dve.sem_inc(y_done, 1)

        @block.tensor
        def _(pe):
            mm = nc.tensor.matmul

            def turn(o, i, n):
                return nc.tensor.transpose(o, i, ident[0:n, 0:n])

            pe.wait_ge(const_in, 16)
            pe.wait_ge(c_ready, 1)
            for k in range(KC):
                ins = turn(bank(7, 32 * k, 32 * k + 32), c_sb[0:32, 128 * k:128 * k + 128], 32)
            ins.then_inc(ct_done, 1)
            pe.wait_ge(rows_in, 64)
            for c in range(CC):
                turn(bank(6, 32 * c, 32 * c + 32), rows[0:32, 128 * c:128 * c + 128], 32)
            turn(bank(6, 64, 72), g_rows[0:8, :], 8).then_inc(rows_done, 1)
            pe.wait_ge(x_ready, 32)
            for c in range(KC):
                if c >= 2:
                    pe.wait_ge(xt_copied, c - 1)
                for tt, (a, n) in enumerate(TILES):
                    ins = turn(bank(4 + c % 2, a, a + n), x_in[0:n, tt, 128 * c:128 * c + 128], n)
                ins.then_inc(xt_done, 1)
            pe.wait_ge(tabc_in, 160)
            pe.wait_ge(ct_ready, 1)
            pe.wait_ge(rows_ready, 1)
            mm(bank(6, 0, 384)[0:HEADS], relb[0:32, :], tab_hot[0:32, :], start=True, stop=False)
            mm(bank(6, 0, 384)[0:HEADS], ones[0:1, 0:HEADS], tab_log[0:1, :], start=False, stop=True).then_inc(tab_done, 1)
            def ada(n):
                _, m, kp = RING[n]
                pe.wait_ge(ring_in[n % SLOTS], 16 * (n // SLOTS) + 16)
                for kk in range(2):
                    k = 2 * kp + kk
                    for j in range(4):
                        ins = mm(bank(ADA_BANK[m])[32 * j:32 * j + 32], c_t[:, k, :],
                                 ring_ada[n % SLOTS][:, kk, 512 * j:512 * j + 512],
                                 start=k == 0, stop=k == KC - 1, tile_position=(0, 32 * j))
                ins.then_inc(ada_used, 1)

            for n in range(4):
                ada(n)
            pe.wait_ge(ada_ready, 1)
            for cb in range(4):
                ins = turn(bank(3, 128 * cb, 128 * cb + 128), ada_sb[:, 0, 128 * cb:128 * cb + 128], 128)
            ins.then_inc(adat_done, 1)
            pe.wait_ge(u_ready, 1)
            pe.wait_ge(tab_ready, 1)
            for n in range(4, len(RING)):
                if RING[n][0] == "ada":
                    ada(n)
                    continue
                block_lo, w = 512 * RING[n][1], ring_in_w[n % SLOTS]
                here = [u for u, unit in enumerate(UNITS) if block_lo <= unit[2] < block_lo + 512]
                pe.wait_ge(ring_in[n % SLOTS], 16 * (n // SLOTS) + 16)
                for u in here:
                    kind, c, col, eng = UNITS[u]
                    col -= block_lo
                    if u >= PB:
                        pe.wait_ge(proj_act if UNITS[u - PB][3] == "act" else proj_dve, copied(u - PB))
                    for k in range(KC):
                        if kind == "v":
                            (a, m), cols = TILES[c[0]], VW[c[1]]
                            ins = mm(bank(u % PB)[0:m, 0:cols], u_t[:, k, a:a + m], w[:, k, col:col + cols],
                                     start=k == 0, stop=k == KC - 1)
                        else:
                            ins = mm(bank(u % PB)[:, 0:NTOK], w[:, k, col:col + 128], u_t[:, k, :],
                                     start=k == 0, stop=k == KC - 1)
                    ins.then_inc(proj_done, 1)
                    if kind == "k":
                        if c == 0:
                            pe.wait_ge(hb_in, 16)
                        if c >= 2:
                            pe.wait_ge(pb_ready, c - 1)
                        mm(bank(6 + c % 2), anti, hb[:, 2 * c:2 * c + 2, :], start=True, stop=True).then_inc(pb_done, 1)
                    if u in KN_AT:
                        tt = KN_AT[u]
                        a, m = TILES[tt]
                        if tt:
                            pe.wait_ge(kn_dve, tt)
                            pe.wait_ge(kn_act, tt)
                        else:
                            pe.wait_ge(proj_dve, copied(2 * AC - 1))
                            pe.wait_ge(pb_ready, 6)
                        for c in range(AC):
                            ins = turn(bank(6 + c // 4, 128 * (c % 4), 128 * (c % 4) + 128)[0:m], k_t[:, c, a:a + m], 128)
                        ins.then_inc(kn_done, 1)
            pe.wait_ge(zl_ready, 1)
            pe.wait_ge(kn_dve, 3)
            for c in range(CC):
                ins = turn(bank(6, 128 * c, 128 * c + 128)[0:18], z_last[:, c, :], 128)
            ins.then_inc(zn_done, 1)
            pe.wait_ge(proj_act, len([w for w in UNITS if w[3] == "act"]))
            pe.wait_ge(proj_dve, len([w for w in UNITS if w[3] == "dve"]))
            pe.wait_ge(ada_late, 1)
            for s in range(HEADS + 3):
                if s < HEADS:
                    c, lo = s // 2, 64 * (s % 2)
                    if s >= 2:
                        pe.wait_ge(pmax_ready, s - 1)
                    q, k = q_t[lo:lo + 64, c, :], k_t[lo:lo + 64, c, :]
                    mm(bank(s % 2, 0, 128), q[:, 0:128], k[:, 0:128], start=True, stop=True)
                    mm(bank(s % 2, 128, 384), q[:, 128:256], k[:, 0:256], start=True, stop=True).then_inc(ps_done, 1)
                if s >= 3:
                    h = s - 3
                    c, lo = h // 2, 64 * (h % 2)
                    pe.wait_ge(pt_copied, h + 1)
                    if h >= 4:
                        pe.wait_ge(po_copied, c - 1)
                    o = bank(4 + c % 2)[lo:lo + 64]
                    pt = p_turn[:, h % 2, :]
                    vv = v_nat[:, :, HD * h:HD * h + HD]
                    mm(o[:, 0:128], vv[:, 0], pt[:, 0:128], start=True, stop=True)
                    mm(o[:, 128:256], vv[:, 0], pt[:, 128:256], start=True, stop=False)
                    mm(o[:, 128:256], vv[:, 1], pt[:, 256:384], start=False, stop=True).then_inc(pv_done, 1)
                if 2 <= s <= HEADS + 1:
                    h = s - 2
                    pe.wait_ge(pnorm_ready, h + 1)
                    if h >= 2:
                        pe.wait_ge(pt_copied, h - 1)
                    for j in range(3):
                        ins = turn(bank(2 + h % 2, 128 * j, 128 * j + 128), p_soft[:, h % 3, 128 * j:128 * j + 128], 128)
                    ins.then_inc(pt_done, 1)
            pe.wait_ge(hot_in, 64)
            pe.wait_ge(bsel_ready, 1)
            for a, z in ((0, 512), (512, 1024), (1024, SB)):
                for kc in range(2):
                    mm(ps[0:96, a:z], bias_sel[:, kc, :], hot_s[:, kc, a:z], start=kc == 0, stop=False)
                ins = mm(ps[0:96, a:z], log_sel[0:8, :], log_s[0:8, a:z], start=False, stop=True)
            ins.then_inc(sb_done, 1)
            pe.wait_ge(sb_ready, 1)
            pe.wait_ge(po_copied, AC)
            pe.wait_ge(pt_copied, HEADS)

            def keys(kt, b):
                if kt == 0:
                    pe.wait_ge(k_rec_in, b * 16 + 16)
                if kt == 1:
                    pe.wait_ge(k_old_in, b * 128 + 128)
                nb = 4 if kt < 2 else 2
                for c in range(AC):
                    n = kt * AC + c
                    if n < 2 or n >= 4:
                        before = n if n < 2 else n - 2 if n < 14 else n
                        pe.wait_ge(kt_dve if c % 2 == 0 else kt_act, b * 9 + before // 2 + 1)
                    for j in range(nb):
                        ins = turn(bank(key_bank(n), 128 * j, 128 * j + 128),
                                   k_sb[:, 4 * kt + j, 128 * c:128 * c + 128], 128)
                    ins.then_inc(kt_done, 1)

            def scores(o, rhs):
                for c in (0, 2, 4, 1, 3, 5):
                    j = c // 2
                    ins = mm(o[32 * j:32 * j + 32], qbd[:, c, :], rhs(c), start=c % 2 == 0, stop=c % 2 == 1,
                             tile_position=(0, 32 * j))
                return ins

            def pe_batch(b, more):
                pe.wait_ge(qbd_ready, b + 1)
                pe.wait_ge(s_max, b + 1)
                pe.wait_ge(kt_dve, b * 9 + 10)
                pe.wait_ge(kt_act, b * 9 + 10)
                scores(bank(0), lambda c: kt_sb[:, c, 0:512])
                scores(bank(1), lambda c: kt_sb[:, c, 512:1024])
                scores(bank(2, 0, 256), lambda c: kt_sb[:, c, 1024:NCACHE])
                scores(bank(2, 256, 320), lambda c: k_t[:, c, SEQ:NTOK]).then_inc(s_done, 1)
                if more:
                    keys(0, b + 1)
                    keys(1, b + 1)
                pe.wait_ge(s_exp, b + 1)
                if more:
                    pe.wait_ge(kt_dve, b * 9 + 9 + 6 + 1)
                    pe.wait_ge(kt_act, b * 9 + 9 + 6 + 1)
                for j in range(KB + 1):
                    o = bank(5, 96 * j, 96 * j + 96) if j < 5 else (
                        bank(6, 96 * j - 480, 96 * j - 384) if j < KB else bank(7, 256, 352)[0:64])
                    ins = turn(o, prob[0:96, 128 * j:min(128 * j + 128, NCACHE + 64)], 96)
                    if j in (4, KB - 1, KB):
                        ins.then_inc(st_done, 1)
                if more:
                    keys(2, b + 1)
                pe.wait_ge(st_act, b + 1)
                pe.wait_ge(st_dve, b * 2 + 2)
                pe.wait_ge(v_in, b * 144 + 144)
                for j in range(KB + 1):
                    for g in range(3):
                        n = 128 if j < KB else 64
                        rhs = v_sb[:, j, 256 * g:256 * g + 256] if j < KB else v_nat[0:64, 2, 256 * g:256 * g + 256]
                        ins = mm(bank(7, 0, 256)[32 * g:32 * g + 32], pt_sb[0:n, j, 32 * g:32 * g + 32], rhs,
                                 start=j == 0, stop=j == KB, tile_position=(0, 32 * g))
                    if j == KB - 1:
                        ins.then_inc(v_used, 1)
                ins.then_inc(sv_done, 1)
                pe.wait_ge(om_ready, b + 1)
                for c in range(AC):
                    ins = mm(bank(7, 352 + 8 * c, 360 + 8 * c), o_mask[0:96, 128 * (c % 2):128 * (c % 2) + 128],
                             query_sum[0:96, c // 2, :], start=True, stop=True)
                ins.then_inc(so_done, 1)

            for kt in range(3):
                keys(kt, 0)
            with pe.Fori(0, NB - 1) as b:
                pe_batch(b, True)
            pe_batch(NB - 1, False)

            pe.wait_ge(so_copied, NB)
            pe.wait_ge(sq_ready, 1)
            for c in range(AC):
                mm(bank(6, 0, NTOK), ones, sq_a[:, c, :], start=c == 0, stop=c == AC - 1)
            for c in range(CC):
                ins = mm(bank(7, 0, NTOK), ones, sq_c[:, c, :], start=c == 0, stop=c == CC - 1)
            ins.then_inc(ss_done, 1)

            def output(tt):
                a, n = TILES[tt]
                if tt >= 2:
                    pe.wait_ge(u2_ready, tt - 1)
                for h in range(2):
                    for c in range(KC):
                        lhs = o_t[:, c, a:a + n] if c < AC else y_c[:, c - AC, a:a + n]
                        ins = mm(bank(2 * (tt % 2) + h)[0:n], lhs, wo_sb[:, c, 512 * h:512 * h + 512],
                                 start=c == 0, stop=c == KC - 1)
                ins.then_inc(wo_done, 1)

            def repeat(tt, o, m, j):
                n = TILES[tt][1]
                lhs = (rep_p if tt < 2 else rep_s)[32 * j:32 * j + 32, 0:n]
                return mm(bank(o)[0:n], lhs, ada_sb[32 * j:32 * j + 32, m, :], start=True, stop=True)

            def gate1(tt):
                if tt:
                    pe.wait_ge(u2_ready, tt)
                for h in range(2):
                    ins = repeat(tt, 4 + h, 1, h)
                ins.then_inc(g1_done, 1)

            def scale2_shift2(tt):
                pe.wait_ge(mixed, tt + 1)
                for h in range(2):
                    repeat(tt, 2 * (tt % 2) + h, 2, h)
                pe.wait_ge(gated, tt + 1)
                for h in range(2):
                    ins = repeat(tt, 4 + h, 1, 2 + h)
                ins.then_inc(c2_done, 1)

            def router(tt):
                n = TILES[tt][1]
                pe.wait_ge(u2_ready, tt + 1)
                if tt:
                    pe.wait_ge(neg_ready, tt)
                for h in range(2):
                    for c in range(4):
                        ins = turn(bank(6 + h, 128 * c, 128 * c + n),
                                   u2[0:n, tt, 128 * (4 * h + c):128 * (4 * h + c) + 128], n)
                    ins.then_inc(u2t_done, 1)
                pe.wait_ge(u2t_ready, 2 * tt + 2)
                for k in range(KC):
                    mm(bank(6, 0, NE)[0:n], u2_t[:, k, 0:n], rw_sb[:, k, :], start=k == 0, stop=False)
                mm(bank(6, 0, NE)[0:n], ones[0:1, 0:n], rb_sb[0:1, :], start=False, stop=True).then_inc(lg_done, 1)

            pe.wait_ge(og_ready, 1)
            pe.wait_ge(wo_in, 16)
            for step, tt in ((output, 0), (gate1, 0), (scale2_shift2, 0), (output, 1), (gate1, 1), (router, 0),
                             (scale2_shift2, 1), (output, 2), (gate1, 2), (router, 1), (scale2_shift2, 2),
                             (router, 2)):
                step(tt)
            pe.wait_ge(masks_ready, 1)
            for tt, (a, n) in enumerate(TILES):
                for s in range(tt + 1):
                    m = TILES[s][1]
                    mm(bank(7, NE * tt, NE * tt + NE)[0:n], tri[0:m, 0:n] if s == tt else ones[0:m, 0:n],
                       mask_t[0:m, s, :], start=s == 0, stop=s == tt)
            for s in range(3):
                m = TILES[s][1]
                ins = mm(bank(7, NE * 3, NE * 4), ones[0:m, :], mask_t[0:m, s, :], start=s == 0, stop=s == 2)
            ins.then_inc(rank_done, 1)
            for tt, (a, n) in enumerate(TILES):
                ins = turn(bank(6, a, a + n)[0:NE], gate_t[0:n, tt, 0:NE], n)
            ins.then_inc(gt_done, 1)
            pe.wait_ge(gt_ready, 1)
            pe.wait_ge(late_in, 16)
            pe.wait_ge(u2_ready, 3)
            for tt, (a, n) in enumerate(TILES):
                for h in range(2):
                    ins = mm(bank(2 * tt + h)[0:n], gt_sb[0:NE, a:a + n], bd_sb[0:NE, 512 * h:512 * h + 512],
                             start=True, stop=True)
            ins.then_inc(bd_done, 1)

            def gather(blocks):
                for v in range(blocks):
                    for tt, (_, n) in enumerate(TILES):
                        for h in range(2):
                            ins = mm(bank(4 + v)[64 * h:64 * h + 64], sel[0:n, tt, 64 * v:64 * v + 64],
                                     u2[0:n, tt, 512 * h:512 * h + 512], start=tt == 0, stop=tt == 2)
                ins.then_inc(ga_done, 1)

            def turn_gathered(blocks, turn_no):
                pe.wait_ge(xn_ready, turn_no)
                for v in range(blocks):
                    for c in range(4):
                        ins = turn(bank(1 + 2 * v, 128 * c, 128 * c + 128), xe_nat[:, v, 128 * c:128 * c + 128], 128)
                ins.then_inc(xt2_done, 1)

            def scatter(tt, banks, blocks):
                for v in range(blocks):
                    for h in range(2):
                        ins = mm(bank(banks[h]), sel_t[64 * h:64 * h + 64, v, 128 * tt:128 * tt + 128],
                                 y_sb[64 * h:64 * h + 64, v, :], start=v == 0, stop=v == blocks - 1)
                return ins

            pe.sem_inc(selt_done, 1)
            pe.wait_ge(acc_ready, 1)
            pe.wait_ge(sel_ready, 1)
            gather(2)
            turn_gathered(2, 1)
            pe.wait_ge(route_ready, 1)
            items = pe.value_load(flag_i[0:1, 0:1], min_val=NE, max_val=ITEMS)
            with pe.Fori(0, items) as i:
                now_b = pe.value_load(flag_i[0:1, bass.ds(i + 1, 1)], min_val=0, max_val=1)
                last_b = pe.value_load(flag_i[0:1, bass.ds(i, 1)], min_val=0, max_val=ITEMS)
                next_b = pe.value_load(flag_i[0:1, bass.ds(i + 2, 1)], min_val=0, max_val=1)
                pe.wait_ge(xe_ready, i + 1)
                pe.wait_ge(bup_in, i * 16 + 16)

                def up_bias(v):
                    for part in range(2):
                        for h in range(2):
                            ins = mm(bank(2 * v + part)[64 * h:64 * h + 64], ones[0:1, 0:64],
                                     b_up[0:1, FF * part + 512 * h:FF * part + 512 * h + 512], start=True, stop=False)
                    return ins

                def up(blocks):
                    if blocks == 2:
                        pe.wait_ge(y_ready, i + 1)
                    for v in range(blocks):
                        ins = up_bias(v)
                    ins.then_inc(bup_used, 1)
                    for k in range(KC):
                        pe.wait_ge(up_in[k], i * 16 + 16)
                        for v in range(blocks):
                            for part in range(2):
                                for h in range(2):
                                    at = 128 * (k % 4) + 64 * (k // 4)
                                    ins = mm(bank(2 * v + part)[64 * h:64 * h + 64], xe_t[:, v, at:at + 64],
                                             up_w[:, k, FF * part + 512 * h:FF * part + 512 * h + 512],
                                             start=False, stop=k == KC - 1)
                        ins.then_inc(up_used, 1)

                with pe.If(now_b > 0):
                    up(2)
                with pe.Else():
                    up(1)
                pe.wait_ge(sel_ready, i + 2)
                pe.wait_ge(sc_added, i * 3 + 1)
                with pe.If(next_b > 0):
                    gather(2)
                with pe.Else():
                    gather(1)

                def turn_act(v):
                    pe.wait_ge(a_ready[v], i + 1)
                    for c in range(4):
                        ins = turn(bank(2 * v, 128 * c, 128 * c + 128), act_l[:, v, 128 * c:128 * c + 128], 128)
                    ins.then_inc(at_done[v], 1)

                def add_up(tts):
                    with pe.If(last_b > 0):
                        for tt in tts:
                            scatter(tt, ((6, 7), (4, 5), (6, 7))[tt], 2).then_inc(sc_done, 1)
                    with pe.Else():
                        for tt in tts:
                            scatter(tt, ((6, 7), (4, 5), (6, 7))[tt], 1).then_inc(sc_done, 1)

                pe.wait_ge(selt_ready, i + 1)
                pe.wait_ge(y_ready, i + 1)
                add_up((0,))
                turn_act(0)
                with pe.If(now_b > 0):
                    turn_act(1)
                with pe.Else():
                    pe.sem_inc(at_done[1], 1)
                with pe.If(next_b > 0):
                    turn_gathered(2, i + 2)
                with pe.Else():
                    turn_gathered(1, i + 2)
                add_up((1,))

                def down(blocks, ms):
                    for m in ms:
                        pe.wait_ge(dn_in[m], i * 16 + 16)
                        for kk in (2 * m, 2 * m + 1):
                            for v in range(blocks):
                                for h in range(2):
                                    lhs = a_t[:, v, 128 * (kk % 4) + 64 * (kk // 4):128 * (kk % 4) + 64 * (kk // 4) + 64]
                                    ins = mm(bank(3 - v)[64 * h:64 * h + 64], lhs,
                                             dn_w[:, kk, 512 * h:512 * h + 512], start=kk == 0, stop=kk == KC - 1)
                        ins.then_inc(dn_used, 1)

                pe.wait_ge(at_ready[0], i + 1)
                pe.wait_ge(xe_ready, i + 2)
                with pe.If(now_b > 0):
                    pe.wait_ge(at_ready[1], i + 1)
                    down(2, (0,))
                with pe.Else():
                    down(1, (0,))
                pe.wait_ge(sc_added, i * 3 + 2)
                add_up((2,))
                with pe.If(now_b > 0):
                    down(2, (1, 2, 3))
                with pe.Else():
                    down(1, (1, 2, 3))
                pe.wait_ge(sc_added, i * 3 + 4)
                pe.wait_ge(selg_ready, i + 1)
                for v in range(2):
                    for tt, (a, n) in enumerate(TILES):
                        ins = turn(bank(6 + v, a, a + n), sel_g[0:n, tt, 2 * v:2 * v + 2, :], n)
                ins.then_inc(selt_done, 1)
            pe.wait_ge(selt_ready, items + 1)
            pe.wait_ge(y_ready, items + 1)
            scatter(0, (6, 7), 2).then_inc(sc_done, 1)
            scatter(1, (4, 5), 2).then_inc(sc_done, 1)
            pe.wait_ge(sc_added, items * 3 + 2)
            scatter(2, (6, 7), 2).then_inc(sc_done, 1)
            pe.wait_ge(sc_added, items * 3 + 4)
            for tt, (a, n) in enumerate(TILES):
                lhs = rep_p if tt < 2 else rep_s
                for h in range(2):
                    ins = mm(bank(2 * tt + h)[0:n], lhs[64 + 32 * h:96 + 32 * h, 0:n], ada_sb[64 + 32 * h:96 + 32 * h, 2, :],
                             start=True, stop=True)
                ins.then_inc(g2_done, 1)


def layer_norm(dve, V, v_, x, n, st, gb, var_ready, sd_ready, sd_count, y):
    for h in range(2):
        ins = v_.bn_stats(st[0:n, 20 + 6 * h:26 + 6 * h], x[:, 512 * h:512 * h + 512])
    V(ins)
    V(v_.bn_aggr(st[0:n, 32:34], st[0:n, 20:32]))
    v_.tensor_scalar(st[0:n, 35:36], st[0:n, 33:34], LN_EPS, None, ALU.add).then_inc(var_ready, 1)
    dve.wait_ge(sd_ready, sd_count)
    V(v_.reciprocal(st[0:n, 37:38], st[0:n, 36:37]))
    V(v_.tensor_scalar(x, x, st[0:n, 32:33], st[0:n, 37:38], ALU.subtract, ALU.mult))
    V(v_.tensor_tensor(x, x, gb[0:n, 0, :], ALU.mult))
    V(v_.tensor_tensor(y, x, gb[0:n, 1, :], ALU.add))


_INS = ["x_prompt", "x_sample", "cache_k", "cache_v", "state_conv", "c_prompt", "c_sample", "w_ada", "b_ada", "w_in",
        "conv_w", "norm_attn_g", "norm_conv_g", "w_o", "ln1_g", "ln1_b", "rel_bias", "router_w", "router_b", "w_up",
        "b_up", "w_down", "b_down", "ln2_g", "ln2_b"]
_OUTS = [(1, SEQ, D), (NB, NS, D), (1, 1, SEQ, HEADS, HD), (1, 1, SEQ, HEADS, HD), (1, 1, 2, DC),
         (1, NB, NS, HEADS, HD), (1, NB, NS, HEADS, HD), (1, NB, 2, DC)]
BRANCHES = ((128, 1), (512, 4), (2048, 16))


def shape_constants():
    import math
    import numpy as np

    def bucket(dist):
        df = np.maximum(dist, 16).astype(np.float32)
        large = 16 + (np.log(df / np.float32(16)) / np.float32(math.log(2048 / 16)) * np.float32(16)).astype(np.int32)
        return np.where(dist < 16, dist, np.minimum(large, 31))

    def log_count(dist):
        n = sum(((dist >= 0) & (dist <= w) & (dist % d == 0)).astype(np.int32) for w, d in BRANCHES)
        return np.where(n > 0, np.log(np.maximum(n, 1)), -1e30).astype(np.float32)

    def one_hot(dist):
        return (np.arange(32)[:, None] == bucket(np.clip(dist, 0, 2048))[None, :]).astype(np.float32)

    out = {}
    consts = np.zeros((128, NCONST), np.float32)
    p, c = np.arange(128)[:, None], np.arange(128)[None, :]
    for name, m in (("ident", p == c), ("tri", p < c), ("iota", np.broadcast_to(c, (128, 128))),
                    ("ones", np.ones((128, 128))), ("rep_p", (p % 32 == 0) & (c >= 0)),
                    ("rep_s", p % 32 == 1 + c[:, 0:64] // NS)):
        at, n = CONSTS[name]
        consts[:, at:at + n] = m
    out["consts"] = consts
    out["anti"] = (p == 127 - c).astype(np.float32)
    dist = 255 - np.arange(384)
    out["tab_hot"] = one_hot(dist)
    out["tab_log"] = log_count(dist)[None, :]
    part = np.arange(128)
    pos = [PAST - REC + 4 * part + r for r in range(4)]
    pos += [16 * (16 * r + part % 16) + part // 16 for r in range(6)]
    pos = np.concatenate(pos + [np.full(WIN, -1)])
    hot, logs = [], []
    for q in range(NS):
        dist = PAST + q - pos
        key = np.arange(WIN) - (NB * NS - NS)
        d_new = np.where((key >= 0) & (key < NS), q - key, -1)
        dist[NCACHE:] = d_new
        hot.append(one_hot(dist))
        logs.append(log_count(dist))
    out["hot_s"] = np.concatenate(hot).astype(np.float32)
    out["log_s"] = np.stack(logs)
    row = np.arange(96)[:, None]
    out["log_sel"] = (np.arange(96)[None, :] % NS == np.arange(NS)[:, None]).astype(np.float32)
    out["head_mask"] = (np.arange(256)[None, :] // HD == (row // NS) % 4).astype(np.float32)
    col = np.arange(24)[None, :]
    out["query_sum"] = ((row // 32 == col // 8) & (row % NS == col % 8)).astype(np.float32)
    return out


def kernel(**inputs):
    import numpy as _np
    import concourse.bacc as _bacc
    from concourse import mybir as _mybir
    from concourse.bass_utils import run_bass_kernel_spmd as _run

    nc = _bacc.Bacc("TRN2", target_bir_lowering=False, num_devices=1)
    arrays, t = {}, {}
    for name, a in list((n, inputs[n]) for n in _INS) + list(shape_constants().items()):
        a = _np.ascontiguousarray(a)
        arrays[f"in_{name}"] = a
        t[name] = nc.dram_tensor(f"in_{name}", a.shape, _mybir.dt.from_np(a.dtype), kind="ExternalInput").ap()
    outs = [nc.dram_tensor(f"out_{i}", shape, F32, kind="ExternalOutput").ap() for i, shape in enumerate(_OUTS)]
    scratch = nc.dram_tensor("by_distance", (HEADS, 384), F32, kind="Internal").ap()
    layer_kernel(nc, t, outs, scratch)
    r = _run(nc, [arrays], core_ids=[0])
    return tuple(r.results[0][f"out_{i}"] for i in range(len(_OUTS)))
```

```python
import concourse.bass as bass
from concourse import mybir
from contextlib import ExitStack

D = 1024
KC = D // 128
NE = 32
FF = 1024
HEADS, HD = 12, 64
DA, DC = HEADS * HD, 256
AC, CC = DA // 128, DC // 128
SEQ, NB, NS = 256, 8, 8
NTOK = SEQ + NB * NS
PAST = 2048
REC, OLD = 512, 768
KB = (REC + OLD) // 128
NCACHE = REC + OLD
WIN = 2 * NB * NS - NS
SB = NCACHE + WIN
TILES = [(0, 128), (128, 128), (256, 64)]
ALPHA = 2.0 ** 0.25
LN_EPS, RMS_EPS = 1e-5, 1e-6
ROUNDS = 3
ITEMS = ROUNDS * NE
FAR = 1000.0

F32, I32, U32 = mybir.dt.float32, mybir.dt.int32, mybir.dt.uint32
ALU = mybir.AluOpType
ACT = mybir.ActivationFunctionType
AX = mybir.AxisListType

CONSTS = {}


def lay_consts():
    at = 0
    for name, n in (("ident", 128), ("tri", 128), ("iota", 128), ("ones", 128), ("rep_p", 128), ("rep_s", 64)):
        CONSTS[name] = (at, n)
        at += n
    return at


NCONST = lay_consts()


class Chain:

    def __init__(self, eng, sem):
        self.eng, self.sem, self.n, self.before, self.off = eng, sem, 0, 0, 0

    def __call__(self, ins):
        ins.then_inc(self.sem, 1)
        self.n += 1
        self.eng.wait_ge(self.sem, self.n + self.off)

    def enter(self, i, per):
        self.start, self.per = self.n, per
        self.off = i * per + self.before

    def leave(self, turns):
        assert self.n - self.start == self.per, (self.n - self.start, self.per)
        self.n = self.start
        self.before = turns * self.per + self.before
        self.off = self.before


def layer_kernel(nc, t, out, scratch, vectors):
    ctx = ExitStack()
    with ctx:
        def sem(name):
            return ctx.enter_context(nc.semaphore(name))

        TOTAL = 53200
        arena = ctx.enter_context(nc.sbuf_tensor("arena", [128, TOTAL], F32))
        ps = ctx.enter_context(nc.psum_tensor("ps", [128, 4096], F32))

        def view(at, *dims):
            n = 1
            for d in dims:
                n *= d
            assert at + n <= TOTAL, (at, n)
            v = arena[:, at:at + n]
            if len(dims) == 2:
                v = v.rearrange("p (a b) -> p a b", a=dims[0])
            elif len(dims) == 3:
                v = v.rearrange("p (a b c) -> p a b c", a=dims[0], b=dims[1])
            return v

        def bank(b, a=0, z=512):
            return ps[:, 512 * b + a:512 * b + z]

        W = 0
        up_w = view(W, KC, 2 * FF)
        dn_w = view(W + KC * 2 * FF, KC, D)
        SLOTS, SLOT = 6, 4096
        ring_ada = [view(W + SLOT * s, 2, 2048) for s in range(SLOTS)]
        ring_in_w = [view(W + SLOT * s, KC, 512) for s in range(SLOTS)]
        k_sb = view(W, KB, DA)
        VX = W + KB * DA
        v_sb = view(VX, KB, DA)
        KTX = VX + KB * DA
        kt_sb = view(KTX, AC, NCACHE)
        MX = KTX + AC * NCACHE
        head_mask = view(MX, 256)
        query_sum = view(MX + 256, 3, 8)
        assert MX + 280 <= 24576

        P = 24576
        consts = view(P, NCONST)
        P += NCONST
        ada_sb = view(P, 3, 512)
        P += 1536
        rows_t = view(P, 2, 32); P += 64
        g_attn = view(P, 8); P += 8
        z_last = view(P, 2, 18); P += 36
        z_nat = view(P, DC); P += 256
        rw_sb = view(P, KC, NE); P += 256
        rb_sb = view(P, NE); P += 32
        relb = view(P, 12); P += 12
        bias_sel = view(P, 2, 96); P += 192
        log_sel = view(P, 96); P += 96
        rank_t = view(P, 3, ITEMS + 1); P += 3 * (ITEMS + 1)
        gate_t = view(P, 3, ITEMS + 1); P += 3 * (ITEMS + 1)
        mask_t = view(P, 3, NE); P += 96
        lg = view(P, NE); P += NE
        ex = view(P, NE); P += NE
        flag_f = z_nat[:, 0:ITEMS + 2]
        flag_i = view(P, ITEMS + 2).bitcast(I32); P += ITEMS + 2
        cnt = view(P, NE); P += NE
        st = view(P, 96); P += 96
        idx_u = view(P, 8).bitcast(U32); P += 8
        idx_f = view(P, 8); P += 8
        lead = view(P, 8); P += 8
        R1, R2 = P, P + 3072
        R3 = R2 + 3072
        R4 = R3 + 8192
        R5 = R4 + 6144
        R6 = R5 + 1316 + 640
        assert R6 + 1920 <= TOTAL, R6 + 1920

        ident = consts[:, 0:128]
        tri = consts[:, 128:256]
        iota = consts[:, 256:384]
        ones = consts[:, 384:512]
        rep_p = consts[:, 512:640]
        rep_s = consts[:, 640:704]

        hb = view(R1, HEADS, 256)
        p_soft = view(R1, 3, 384)
        p_turn = view(R1 + 1152, 2, 384)
        s_bias = view(R1, SB)
        prob = view(R1 + SB, NCACHE + 64)
        x1 = view(R1, 3, D)
        mod_p = view(W + 18 * D, 3, D)
        mod_s = view(W + 21 * D, 3, D)
        p_bias = view(R2, HEADS, 256)
        pt_sb = view(R2, KB + 1, 96)
        qbd = view(R2 + (KB + 1) * 96, AC, 32)
        o_mask = view(R2 + (KB + 1) * 96 + AC * 32, 256)
        u2 = view(R2, 3, D)
        u_t = view(R3, KC, NTOK)
        k_nat = view(R3 + 2560, 3, DA)
        b_rows = view(R3 + 4864, 3, 512)
        c_sb = view(R3 + 6400, D)
        ada_t = view(R3 + 7424, 4, 128)
        c_t = view(R3 + 7936, KC, 32)
        hot_s = view(R3 + 4864, 2, SB)
        log_s = view(R3, SB)
        wo_sb = view(R3, KC, D)
        acc = view(R3, 3, D)
        act_g = view(R3 + 3072, 2, 512)
        act_s = view(R3 + 4096, 2, 512)
        act_l = view(R3 + 5120, 2, 512)
        b_up = view(R3 + 6144, 2 * FF)
        fin_t = view(R3 + 3072, D)
        fin_y = view(R3 + 4096, 3, D)
        x_in = view(R4, 3, D)
        sig_c = view(R4 + 3 * D, D)
        rows = view(R4 + 4 * D, DC)
        g_rows = view(R4 + 4 * D + DC, 128)
        q_t = view(R4, AC, NTOK)
        k_t = view(R4 + 1920, AC, NTOK)
        v_nat = view(R4 + 3840, 3, DA)
        sq_a = [view(R2 + 1504, AC, SEQ), view(R4 + 2 * D, AC, 64)]
        sq_c = [view(R5, CC, SEQ), view(R4 + 2 * D + 384, CC, 64)]
        norm_rep = [view(R5 + CC * SEQ, 2, SEQ), view(R4 + 2 * D + 512, 2, 64)]
        mix = view(R4, 2, D)
        u2_t = view(R4 + 3 * D, KC, 128)
        ln1 = view(R4 + 4 * D, 2, D)
        xe_t = view(R4, 2, 512)
        xe_nat = view(R4 + 4992, 2, 512)
        a_t = view(R4 + 1024, 2, 512)
        y_sb = view(R4 + 2048, 2, 512)
        sel = view(R4 + 3072, 3, 128)
        sel_g = view(R4 + 3456, 3, 4, 64)
        sel_t = view(R4 + 4224, 2, 384)
        z_p = view(R5, 2, SEQ + 2)
        z_s = view(R5 + 516, 2, 80)
        c_gate = view(R5 + 676, 2, NTOK)
        y_c = view(R5 + 1316, 2, NTOK)
        o_t = view(R6, AC, NTOK)
        tab_hot = view(R6, 384)
        tab_log = view(R6 + 384, 384)
        tab_sb = view(R6 + 768, 384)
        anti = view(R6 + 1152, 128)
        ln2 = view(R5, 2, D)
        bd_sb = view(R5 + 2 * D, D)
        gt_sb = view(R5 + 3 * D, NTOK)

        wada_d = t["w_ada"][0].rearrange("(k p) n -> p k n", p=128)
        win_d = t["w_in"][0].rearrange("(k p) n -> p k n", p=128)
        wo_d = t["w_o"][0].rearrange("(k p) n -> p k n", p=128)
        wup_d = t["w_up"][0].rearrange("e (k p) n -> e k p n", p=128)
        wdn_d = t["w_down"][0].rearrange("e (m k p) n -> e m p k n", p=128, k=2)
        ck = t["cache_k"][0].rearrange("b s h e -> b s (h e)")
        cv = t["cache_v"][0].rearrange("b s h e -> b s (h e)")

        vec_out, mod_in = sem("vec_out"), sem("mod_in")
        ring_in = [sem(f"ring_in{s}") for s in range(SLOTS)]
        ada_used, ada_late, hot_in, k_rec_in, k_old_in, v_in, wo_in = map(
            sem, ("ada_used", "ada_late", "hot_in", "k_rec_in", "k_old_in", "v_in", "wo_in"))
        up_in = [sem(f"up_in{k}") for k in range(KC)]
        dn_in = [sem(f"dn_in{m}") for m in range(KC // 2)]
        bup_in, bup_used, up_used, dn_used = map(sem, ("bup_in", "bup_used", "up_used", "dn_used"))
        const_in, c_in, rows_in, bada_in, x_ready, tabc_in = map(
            sem, ("const_in", "c_in", "rows_in", "bada_in", "x_ready", "tabc_in"))
        zeroed, sig_done, c_ready, ct_done, ct_ready, rows_done, rows_ready = map(
            sem, ("zeroed", "sig_done", "c_ready", "ct_done", "ct_ready", "rows_done", "rows_ready"))
        xt_done, xt_copied, ada_ready, adat_done, u_ready = map(
            sem, ("xt_done", "xt_copied", "ada_ready", "adat_done", "u_ready"))
        tab_done, tab_ready, scr_out, hb_in, pb_done, pb_ready = map(
            sem, ("tab_done", "tab_ready", "scr_out", "hb_in", "pb_done", "pb_ready"))
        proj_done, proj_act, proj_dve = map(sem, ("proj_done", "proj_act", "proj_dve"))
        kn_done, kn_dve, kn_act, zl_ready, zn_done, zn_ready = map(
            sem, ("kn_done", "kn_dve", "kn_act", "zl_ready", "zn_done", "zn_ready"))
        out_kv, out_y = sem("out_kv"), sem("out_y")
        sb_done, sb_ready, bsel_ready = sem("sb_done"), sem("sb_ready"), sem("bsel_ready")
        ps_done, pmax_ready, pexp_ready, pnorm_ready, pt_done, pt_copied, pv_done, po_copied = map(
            sem, ("ps_done", "pmax_ready", "pexp_ready", "pnorm_ready", "pt_done", "pt_copied", "pv_done", "po_copied"))
        qbd_ready, kt_done, kt_dve, kt_act, s_done, s_max, s_exp, st_done, st_act, st_dve = map(
            sem, ("qbd_ready", "kt_done", "kt_dve", "kt_act", "s_done", "s_max", "s_exp", "st_done", "st_act", "st_dve"))
        v_used, sv_done, om_ready, so_done, so_copied = map(
            sem, ("v_used", "sv_done", "om_ready", "so_done", "so_copied"))
        tail_in, sq_ready, og_ready, ss_done, var_ready, sd_ready, wo_done = map(
            sem, ("tail_in", "sq_ready", "og_ready", "ss_done", "var_ready", "sd_ready", "wo_done"))
        u2_ready, u2t_done, u2t_ready, lg_done, neg_ready, ex_ready, masks_ready = map(
            sem, ("u2_ready", "u2t_done", "u2t_ready", "lg_done", "neg_ready", "ex_ready", "masks_ready"))
        rank_done, route_ready, gt_done, gt_ready, acc_ready, late_in, ln2_in = map(
            sem, ("rank_done", "route_ready", "gt_done", "gt_ready", "acc_ready", "late_in", "ln2_in"))
        sel_ready, selg_ready, y_ready = sem("sel_ready"), sem("selg_ready"), sem("y_ready")
        g_ready, sig_ready, a_ready, at_done, at_ready = (
            [sem(f"{name}_{v}") for v in "ab"] for name in ("g_ready", "sig_ready", "a_ready", "at_done", "at_ready"))
        ga_done, xn_ready, gathered_turned_done, xe_ready, selt_done, selt_ready, sc_done, sc_added = map(
            sem, ("ga_done", "xn_ready", "gathered_turned_done", "xe_ready", "selt_done", "selt_ready", "sc_done",
                  "sc_added"))
        g2_done, y_done = sem("g2_done"), sem("y_done")
        ch_v, ch_end = sem("vector_chain"), sem("vector_chain_at_the_end")

        UNITS = [("q", c, 128 * c, "act") for c in range(AC)]
        UNITS += [("k", c, DA + 128 * c, "dve") for c in range(AC)]
        UNITS += [("v", (tt, 0), 2 * DA, "act") for tt in range(3)]
        UNITS += [("v", (tt, 1), 2 * DA + 512, "dve") for tt in range(3)]
        UNITS += [("B", c, 3 * DA + 128 * c, "act") for c in range(CC)]
        for c in range(CC):
            UNITS += [("C", c, 3 * DA + DC + 128 * c, "act"), ("h", c, 3 * DA + 2 * DC + 128 * c, "dve")]
        VW = {0: 512, 1: 256}
        PB = 4
        ADA_BANK = (0, 4, 5)
        RING = [("ada", 0, kp) for kp in range(4)] + [("win", 0), ("win", 1), ("win", 2)]
        RING += [("ada", 1, 0), ("ada", 1, 1), ("ada", 1, 2), ("win", 3), ("ada", 1, 3), ("ada", 2, 0), ("ada", 2, 1),
                 ("win", 4), ("ada", 2, 2), ("ada", 2, 3), ("win", 5)]
        LAG = 4
        KN_AT = {12: 0, 13: 1, 14: 2}

        def copied(u):
            return sum(1 for w in UNITS[:u + 1] if w[3] == UNITS[u][3])

        def key_bank(n):
            return 3 + n % 4 if n < 12 else 3 + n % 2

        def used(n):
            if RING[n][0] == "ada":
                return ada_used, sum(1 for w in RING[:n + 1] if w[0] == "ada")
            return proj_done, sum(1 for u in UNITS if u[2] < 512 * RING[n][1] + 512)

        block = ctx.enter_context(nc.Block())

        @block.sync
        def _(sp):
            sp.dma_start(consts, t["consts"]).then_inc(const_in, 16)
            sp.wait_ge(zeroed, 1)
            sp.dma_start(c_sb[0:1, :], t["c_prompt"]).then_inc(c_in, 16)
            sp.dma_start(c_sb[1:1 + NB, :], t["c_sample"]).then_inc(c_in, 16)

            def small_inputs():
                sp.wait_ge(zeroed, 2)
                sp.dma_start(rows[0:16, :], t["state_conv"][0].rearrange("b i c -> (b i) c")).then_inc(rows_in, 16)
                sp.dma_start(rows[16:19, :], t["conv_w"][0]).then_inc(rows_in, 16)
                sp.dma_start(rows[19:20, :], t["norm_conv_g"]).then_inc(rows_in, 16)
                sp.dma_start(g_rows[0:AC, :], t["norm_attn_g"].rearrange("o (c p) -> (o c) p", p=128)).then_inc(rows_in, 16)
                sp.dma_start(x_in[:, 0:2, :], t["x_prompt"][0].rearrange("(a p) d -> p a d", p=128)).then_inc(x_ready, 16)
                sp.dma_start(x_in[0:64, 2, :], t["x_sample"].rearrange("b s d -> (b s) d")).then_inc(x_ready, 16)
                sp.dma_start(tab_hot[0:32, :], t["tab_hot"]).then_inc(tabc_in, 16)
                sp.dma_start(tab_log[0:1, :], t["tab_log"]).then_inc(tabc_in, 16)
                for q in range(4):
                    sp.dma_start(relb[32 * q:32 * q + 32, :], t["rel_bias"]).then_inc(tabc_in, 16)
                sp.dma_start(log_sel[0:8, :], t["log_sel"]).then_inc(tabc_in, 16)
                sp.dma_start(anti, t["anti"]).then_inc(tabc_in, 16)
                sp.dma_start(rw_sb, t["router_w"][0].rearrange("(k p) e -> p k e", p=128)).then_inc(tabc_in, 16)
                sp.dma_start(rb_sb[0:1, :], t["router_b"]).then_inc(tabc_in, 16)
                for j in range(4):
                    src = t["b_ada"].rearrange("o (m j c) -> j o m c", m=3, j=4)[j]
                    sp.dma_start(b_rows[32 * j:32 * j + 32], src.to_broadcast([32, 3, 512])).then_inc(bada_in, 16)

            for n, what in enumerate(RING):
                if n == 1:
                    small_inputs()
                if n >= SLOTS:
                    sp.wait_ge(*used(n - SLOTS))
                if what[0] == "ada":
                    _, m, kp = what
                    src, dst = wada_d[:, 2 * kp:2 * kp + 2, 2048 * m:2048 * m + 2048], ring_ada[n % SLOTS]
                else:
                    src, dst = win_d[:, :, 512 * what[1]:512 * what[1] + 512], ring_in_w[n % SLOTS]
                sp.dma_start(dst, src).then_inc(ring_in[n % SLOTS], 16)

            def load_rec(cache, sb, b, done):
                sp.dma_start(sb[:, 0:4, :], cache[b][:, PAST - REC:PAST, :].rearrange("o (p r) d -> (o p) r d", r=4)
                             ).then_inc(done, 16)

            def load_old(cache, sb, b, done):
                old = cache[b][:, 0:PAST - REC, :].rearrange("o (r g i) d -> i (o g) r d", r=6, g=16)
                for i in range(8):
                    sp.dma_start(sb[16 * i:16 * i + 16, 4:KB, :], old[i]).then_inc(done, 16)

            sp.wait_ge(*used(len(RING) - SLOTS + 1))
            load_rec(ck, k_sb, slice(0, 1), k_rec_in)
            load_old(ck, k_sb, slice(0, 1), k_old_in)
            sp.wait_ge(*used(len(RING) - SLOTS + 3))
            load_rec(cv, v_sb, slice(0, 1), v_in)
            load_old(cv, v_sb, slice(0, 1), v_in)
            sp.wait_ge(*used(len(RING) - 1))
            sp.wait_ge(ada_late, 1)
            sp.dma_start(hot_s, t["hot_s"].rearrange("(a p) n -> p a n", p=128)).then_inc(hot_in, 16)
            sp.dma_start(log_s[0:8, :], t["log_s"]).then_inc(hot_in, 16)
            sp.dma_start(head_mask[0:96, :], t["head_mask"]).then_inc(hot_in, 16)
            sp.dma_start(query_sum[0:96], t["query_sum"].rearrange("p (a b) -> p a b", a=3)).then_inc(hot_in, 16)

            def load_keys(cache, b, before):
                sp.wait_ge(kt_done, before * 18 + AC)
                load_rec(cache, k_sb, b, k_rec_in)
                sp.wait_ge(kt_done, before * 18 + 3 * AC)
                load_old(cache, k_sb, b, k_old_in)

            def load_values(b, used):
                sp.wait_ge(v_used, used)
                load_rec(cv, v_sb, b, v_in)
                load_old(cv, v_sb, b, v_in)

            load_keys(ck, slice(1, 2), 0)
            sp.wait_ge(out_kv, 96)
            sp.wait_ge(sb_done, 1)
            sp.dma_start(wo_sb, wo_d).then_inc(wo_in, 16)
            with sp.Fori(1, NB - 1) as b:
                load_keys(ck[1:NB], bass.ds(b, 1), b)
                load_values(bass.ds(b, 1), b)
            load_values(slice(NB - 1, NB), NB - 1)
            def load_expert(e, slot_free):
                if slot_free is not None:
                    sp.wait_ge(bup_used, slot_free)
                sp.dma_start(b_up[0:1, :], t["b_up"][0, bass.ds(e, 1), :]).then_inc(bup_in, 16)

            sp.wait_ge(v_used, NB)
            sp.wait_ge(so_copied, NB)
            sp.wait_ge(vec_out, 64)
            sp.dma_start(mod_p, vectors[0:1, 0:3 * D].to_broadcast([128, 3 * D]).rearrange("p (a b) -> p a b", a=3)
                         ).then_inc(mod_in, 16)
            for b in range(NB):
                src = vectors[1 + b:2 + b, 0:3 * D].to_broadcast([NS, 3 * D]).rearrange("p (a b) -> p a b", a=3)
                sp.dma_start(mod_s[NS * b:NS * b + NS], src).then_inc(mod_in, 16)
            for k in range(KC):
                sp.dma_start(up_w[:, k, :], wup_d[0, k]).then_inc(up_in[k], 16)
            for m in range(KC // 2):
                if m == 1:
                    sp.wait_ge(u2_ready, 3)
                sp.dma_start(dn_w[:, 2 * m:2 * m + 2, :], wdn_d[0, m]).then_inc(dn_in[m], 16)
            sp.wait_ge(route_ready, 1)
            load_expert(0, None)
            items = sp.value_load(flag_i[0:1, 0:1], min_val=NE, max_val=ITEMS)
            with sp.Fori(1, items) as i:
                e = i % NE
                load_expert(e, i)
                for k in range(KC):
                    sp.wait_ge(up_used, (i - 1) * KC + k + 1)
                    sp.dma_start(up_w[:, k, :], wup_d[bass.ds(e, 1), k].rearrange("o p n -> (o p) n")
                                 ).then_inc(up_in[k], 16)
                for m in range(KC // 2):
                    sp.wait_ge(dn_used, (i - 1) * (KC // 2) + m + 1)
                    sp.dma_start(dn_w[:, 2 * m:2 * m + 2, :], wdn_d[bass.ds(e, 1), m].rearrange(
                        "o p k n -> (o p) k n")).then_inc(dn_in[m], 16)
            sp.wait_ge(y_done, 2)
            sp.dma_start(out[0][0].rearrange("(a p) d -> p a d", p=128), fin_y[:, 0:2, :]).then_inc(out_y, 16)
            sp.wait_ge(y_done, 3)
            sp.dma_start(out[1].rearrange("b s d -> (b s) d"), fin_y[0:64, 2, :]).then_inc(out_y, 16)
            sp.wait_ge(out_y, 32)

        @block.gpsimd
        def _(pool):
            pool.wait_ge(tab_ready, 1)
            pool.dma_start(scratch, tab_sb[0:HEADS, :]).then_inc(scr_out, 16)
            pool.wait_ge(scr_out, 16)
            pool.dma_start(hb, bass.AP(scratch.tensor, 0, [[1, 128], [384, HEADS], [1, 256]])).then_inc(hb_in, 16)
            pool.wait_ge(kn_dve, 3)
            pool.wait_ge(kn_act, 3)
            pool.dma_start(out[2][0, 0].rearrange("(a p) h e -> p a (h e)", p=128), k_nat[:, 0:2, :]).then_inc(out_kv, 16)
            pool.dma_start(out[5][0].rearrange("b s h e -> (b s) (h e)"), k_nat[0:64, 2, :]).then_inc(out_kv, 16)
            pool.wait_ge(proj_act, len([w for w in UNITS if w[3] == "act"]))
            pool.wait_ge(proj_dve, len([w for w in UNITS if w[3] == "dve"]))
            pool.dma_start(out[3][0, 0].rearrange("(a p) h e -> p a (h e)", p=128), v_nat[:, 0:2, :]).then_inc(out_kv, 16)
            pool.dma_start(out[6][0].rearrange("b s h e -> (b s) (h e)"), v_nat[0:64, 2, :]).then_inc(out_kv, 16)
            pool.wait_ge(zn_ready, 1)
            pool.dma_start(out[4][0, 0], z_nat[0:2, :]).then_inc(out_kv, 16)
            pool.dma_start(out[7][0].rearrange("b s c -> (b s) c"), z_nat[2:18, :]).then_inc(out_kv, 16)
            pool.wait_ge(ada_late, 1)
            for j in range(4):
                pool.dma_start(vectors.rearrange("r (m j c) -> j r m c", m=2, j=4)[j],
                               ada_sb[32 * j:32 * j + 1 + NB, 1:3, :]).then_inc(vec_out, 16)
            pool.wait_ge(out_kv, 96)
            pool.wait_ge(so_copied, NB)
            pool.dma_start(x1[:, 0:2, :], t["x_prompt"][0].rearrange("(a p) d -> p a d", p=128)).then_inc(tail_in, 16)
            pool.dma_start(x1[0:64, 2, :], t["x_sample"].rearrange("b s d -> (b s) d")).then_inc(tail_in, 16)
            for a, name in enumerate(("ln1_g", "ln1_b")):
                pool.dma_start(ln1[:, a, :], t[name][0:1, :].to_broadcast([128, D])).then_inc(tail_in, 16)
            pool.wait_ge(wo_done, 3)
            nc.gpsimd.memset(acc, 0.0).then_inc(acc_ready, 1)
            pool.dma_start(bd_sb[0:NE, :], t["b_down"][0]).then_inc(late_in, 16)
            for a, name in enumerate(("ln2_g", "ln2_b")):
                pool.dma_start(ln2[:, a, :], t[name][0:1, :].to_broadcast([128, D])).then_inc(ln2_in, 16)

        @block.scalar
        def _(act):
            act.wait_ge(c_in, 32)
            nc.scalar.activation(sig_c[0:32, :], c_sb[0:32, :], ACT.Sigmoid).then_inc(sig_done, 1)

            def act_keys(tt):
                n = TILES[tt][1]
                act.wait_ge(kn_done, tt + 1)
                nc.scalar.copy(k_nat[0:n, tt, 512:DA], bank(7)[0:n, 0:256]).then_inc(kn_act, 1)

            for u, (kind, c, _, eng) in enumerate(UNITS):
                if u - 1 in KN_AT:
                    act_keys(KN_AT[u - 1])
                if eng != "act":
                    continue
                act.wait_ge(proj_done, u + 1)
                src = bank(u % PB)
                if kind == "q":
                    ins = nc.scalar.mul(q_t[:, c, :], src[:, 0:NTOK], HD ** -0.5)
                elif kind == "C":
                    ins = nc.scalar.copy(c_gate[:, c, :], src[:, 0:NTOK])
                elif kind == "B":
                    ins = nc.scalar.copy(y_c[:, c, :], src[:, 0:NTOK])
                else:
                    n = TILES[c[0]][1]
                    ins = nc.scalar.copy(v_nat[0:n, c[0], 0:512], src[0:n, 0:512])
                ins.then_inc(proj_act, 1)

            act.sem_inc(kt_act, 1)

            def act_turned(kt, b, chunks=(1, 3, 5)):
                for c in chunks:
                    w = 512 if kt < 2 else 256
                    act.wait_ge(kt_done, b * 18 + kt * AC + c + 1)
                    nc.scalar.copy(kt_sb[:, c, 512 * kt:512 * kt + w], bank(key_bank(kt * AC + c), 0, w)).then_inc(kt_act, 1)

            for kt in range(3):
                act_turned(kt, 0)

            for s in range(HEADS + LAG):
                if s < HEADS:
                    act.wait_ge(pmax_ready, s + 1)
                    for q, (a, z) in enumerate(((0, 128), (128, 384))):
                        ins = nc.scalar.activation(p_soft[:, s % 3, a:z], p_soft[:, s % 3, a:z], ACT.Exp,
                                                   bias=st[:, 4 * (s % 2) + 2 + q:4 * (s % 2) + 3 + q],
                                                   accum_out=st[:, 8 + 2 * (s % 2) + q:9 + 2 * (s % 2) + q])
                    ins.then_inc(pexp_ready, 1)
                if 2 <= s <= HEADS + 1:
                    h = s - 2
                    act.wait_ge(pt_done, h + 1)
                    if h >= 2:
                        act.wait_ge(pv_done, h - 1)
                    nc.scalar.copy(p_turn[:, h % 2, :], bank(2 + h % 2, 0, 384)).then_inc(pt_copied, 1)
                if s > LAG and (s - LAG) % 2 == 1:
                    c = (s - LAG) // 2
                    act.wait_ge(pv_done, s - LAG + 1)
                    nc.scalar.copy(o_t[:, c, 0:SEQ], bank(4 + c % 2, 0, SEQ)).then_inc(po_copied, 1)

            def act_norm(g):
                act.wait_ge(var_ready, g + 1)
                nc.scalar.activation(norm_rep[g], norm_rep[g], ACT.Sqrt).then_inc(sd_ready, 1)

            def act_batch(b, more):
                if more:
                    act_turned(0, b + 1, (1,))
                act.wait_ge(s_max, b + 2)
                nc.scalar.activation(prob[0:96, :], prob[0:96, :], ACT.Exp, bias=st[0:96, 14:15],
                                     accum_out=st[0:96, 15:16]).then_inc(s_exp, 1)
                if more:
                    act_turned(0, b + 1, (3, 5))
                    act_turned(1, b + 1)
                act.wait_ge(st_done, b * 3 + 1)
                nc.scalar.copy(pt_sb[:, 0:5, :], bank(5, 0, 480).rearrange("p (a b) -> p a b", a=5)).then_inc(st_act, 1)
                if more:
                    act_turned(2, b + 1)

            act_norm(0)
            with act.Fori(0, NB - 1) as b:
                act_batch(b, True)
            act_batch(NB - 1, False)

            act.wait_ge(so_copied, NB)
            act_norm(1)

            def act_root(tt):
                n = TILES[tt][1]
                act.wait_ge(var_ready, tt + 3)
                nc.scalar.activation(st[0:n, 36:37], st[0:n, 35:36], ACT.Sqrt).then_inc(sd_ready, 1)

            def act_turn(tt):
                n = TILES[tt][1]
                for h in range(2):
                    act.wait_ge(u2t_done, 2 * tt + h + 1)
                    nc.scalar.copy(u2_t[:, 4 * h:4 * h + 4, 0:n],
                                   bank(6 + h).rearrange("p (a b) -> p a b", a=4)[:, :, 0:n]).then_inc(u2t_ready, 1)

            def act_exp(tt):
                n = TILES[tt][1]
                act.wait_ge(neg_ready, tt + 1)
                nc.scalar.activation(ex[0:n, :], lg[0:n, :], ACT.Exp, bias=st[0:n, 40:41]).then_inc(ex_ready, 1)

            for step, tt in ((act_root, 0), (act_turn, 0), (act_root, 1), (act_exp, 0), (act_turn, 1), (act_root, 2),
                             (act_exp, 1), (act_turn, 2), (act_exp, 2)):
                step(tt)
            act.wait_ge(gt_done, 1)
            nc.scalar.copy(gt_sb[0:NE, :], bank(6, 0, NTOK)[0:NE]).then_inc(gt_ready, 1)

            act.wait_ge(route_ready, 1)
            for counted_from_one in (y_ready, selt_ready):
                act.sem_inc(counted_from_one, 1)
            items = act.value_load(flag_i[0:1, 0:1], min_val=NE, max_val=ITEMS)

            def gathered(blocks, turn_no):
                act.wait_ge(ga_done, turn_no)
                for v in reversed(range(blocks)):
                    ins = nc.scalar.copy(xe_nat[:, v, :], bank(4 + v))
                ins.then_inc(xn_ready, 1)

            gathered(2, 1)
            with act.Fori(0, items) as i:
                now_b = act.value_load(flag_i[0:1, bass.ds(i + 1, 1)], min_val=0, max_val=1)
                next_b = act.value_load(flag_i[0:1, bass.ds(i + 2, 1)], min_val=0, max_val=1)

                def sigmoid(v):
                    act.wait_ge(g_ready[v], i + 1)
                    nc.scalar.activation(act_s[:, v, :], act_g[:, v, :], ACT.Sigmoid, scale=1.702
                                         ).then_inc(sig_ready[v], 1)

                def turned(v):
                    act.wait_ge(at_done[v], i + 1)
                    nc.scalar.copy(a_t[:, v, :], bank(2 * v)).then_inc(at_ready[v], 1)

                sigmoid(0)
                with act.If(now_b > 0):
                    sigmoid(1)
                with act.Else():
                    act.sem_inc(sig_ready[1], 1)
                with act.If(next_b > 0):
                    gathered(2, i + 2)
                with act.Else():
                    gathered(1, i + 2)
                turned(0)
                with act.If(now_b > 0):
                    turned(1)
                with act.Else():
                    act.sem_inc(at_ready[1], 1)
                with act.If(now_b > 0):
                    act.wait_ge(dn_used, i * (KC // 2) + KC // 2)
                    nc.scalar.copy(y_sb[:, 1, :], bank(2))
                    nc.scalar.copy(y_sb[:, 0, :], bank(3)).then_inc(y_ready, 1)
                with act.Else():
                    act.wait_ge(dn_used, i * (KC // 2) + KC // 2)
                    nc.scalar.copy(y_sb[:, 0, :], bank(3)).then_inc(y_ready, 1)
                act.wait_ge(selt_done, i + 2)
                for v in range(2):
                    ins = nc.scalar.copy(sel_t[:, v, 0:320], bank(6 + v, 0, 320))
                ins.then_inc(selt_ready, 1)
            for tt, (a, n) in enumerate(TILES):
                act.wait_ge(var_ready, 6 + tt)
                nc.scalar.activation(st[0:n, 36:37], st[0:n, 35:36], ACT.Sqrt).then_inc(sd_ready, 1)

        @block.vector
        def _(dve):
            V = Chain(dve, ch_v)
            v_ = nc.vector
            v_.memset(c_sb[0:32, :], 0.0).then_inc(zeroed, 1)
            v_.memset(rows[0:32, :], 0.0)
            v_.memset(z_p[:, :, 0:2], 0.0)
            v_.memset(g_rows[0:8, :], 0.0).then_inc(zeroed, 1)
            dve.wait_ge(sig_done, 1)
            v_.tensor_tensor(c_sb[0:32, :], c_sb[0:32, :], sig_c[0:32, :], ALU.mult).then_inc(c_ready, 1)
            dve.wait_ge(ct_done, 1)
            v_.tensor_copy(c_t, bank(7, 0, 256).rearrange("p (a b) -> p a b", a=KC)).then_inc(ct_ready, 1)
            dve.wait_ge(rows_done, 1)
            v_.tensor_copy(rows_t, bank(6, 0, 64).rearrange("p (a b) -> p a b", a=2))
            v_.tensor_copy(g_attn, bank(6, 64, 72)).then_inc(rows_ready, 1)
            dve.wait_ge(rows_ready, 1)
            V(v_.tensor_copy(z_s.rearrange("p c (b t) -> p c b t", b=NB)[:, :, :, 0:2],
                             rows_t[:, :, 0:16].rearrange("p c (b t) -> p c b t", b=NB)))
            for c in range(KC):
                dve.wait_ge(xt_done, c + 1)
                v_.tensor_copy(u_t[:, c, :], bank(4 + c % 2, 0, NTOK)).then_inc(xt_copied, 1)
            dve.wait_ge(tabc_in, 160)
            V(v_.memset(bias_sel, 0.0))
            for kc in range(2):
                for q in range(4):
                    cols = bias_sel[32 * q:32 * q + 32, kc, 4 * kc + q:96:NS]
                    ins = v_.tensor_copy(cols, relb[32 * q:32 * q + 32, :])
            ins.then_inc(bsel_ready, 1)
            dve.wait_ge(tab_done, 1)
            v_.tensor_copy(tab_sb[0:HEADS, :], bank(6, 0, 384)[0:HEADS]).then_inc(tab_ready, 1)
            dve.wait_ge(bada_in, 64)
            dve.wait_ge(ada_used, 4)
            v_.tensor_tensor(ada_sb[:, 0, :], bank(ADA_BANK[0]), b_rows[:, 0, :], ALU.add).then_inc(ada_ready, 1)
            dve.wait_ge(adat_done, 1)
            src = bank(3).rearrange("p (a b) -> p a b", a=4)
            v_.tensor_copy(ada_t[:, :, 0:64], src[:, :, 0:64])
            V(v_.tensor_scalar(ada_t[:, :, 64:128], src[:, :, 64:128], 1.0, None, ALU.add))
            dve.wait_ge(xt_copied, KC)
            for c in range(KC):
                cb, j = c % 4, c // 4
                sh, sc = ada_t[:, cb, 32 * j:32 * j + 9], ada_t[:, cb, 64 + 32 * j:64 + 32 * j + 9]
                v_.tensor_scalar(u_t[:, c, 0:SEQ], u_t[:, c, 0:SEQ], sc[:, 0:1], sh[:, 0:1], ALU.mult, ALU.add)
                us = u_t[:, c, SEQ:NTOK].rearrange("p (b t) -> p b t", b=NB)
                V(v_.tensor_tensor(us, us, sc[:, 1:9].unsqueeze(2).to_broadcast([128, NB, NS]), ALU.mult))
                v_.tensor_tensor(us, us, sh[:, 1:9].unsqueeze(2).to_broadcast([128, NB, NS]), ALU.add
                                 ).then_inc(u_ready, 1)
            def dve_keys(tt):
                n = TILES[tt][1]
                dve.wait_ge(kn_done, tt + 1)
                v_.tensor_copy(k_nat[0:n, tt, 0:512], bank(6)[0:n]).then_inc(kn_dve, 1)

            for u, (kind, c, _, eng) in enumerate(UNITS):
                if u - 1 in KN_AT:
                    dve_keys(KN_AT[u - 1])
                if eng != "dve":
                    continue
                dve.wait_ge(proj_done, u + 1)
                src = bank(u % PB)
                if kind == "k":
                    v_.tensor_copy(k_t[:, c, :], src[:, 0:NTOK]).then_inc(proj_dve, 1)
                    dve.wait_ge(pb_done, c + 1)
                    v_.tensor_copy(p_bias[:, 2 * c:2 * c + 2, :], bank(6 + c % 2).rearrange("p (a b) -> p a b", a=2)
                                   ).then_inc(pb_ready, 1)
                    continue
                elif kind == "h":
                    dve.wait_ge(proj_act, copied(u - 1))
                    v_.tensor_tensor(z_p[:, c, 2:SEQ + 2], src[:, 0:SEQ], c_gate[:, c, 0:SEQ], ALU.mult)
                    ins = v_.tensor_tensor(z_s[:, c, :].rearrange("p (b t) -> p b t", b=NB)[:, :, 2:10],
                                           src[:, SEQ:NTOK].rearrange("p (b t) -> p b t", b=NB),
                                           c_gate[:, c, SEQ:NTOK].rearrange("p (b t) -> p b t", b=NB), ALU.mult)
                else:
                    n = TILES[c[0]][1]
                    ins = v_.tensor_copy(v_nat[0:n, c[0], 512:DA], src[0:n, 0:256])
                ins.then_inc(proj_dve, 1)
            dve.wait_ge(ada_used, 12)
            for m in (1, 2):
                ins = v_.tensor_tensor(ada_sb[:, m, :], bank(ADA_BANK[m]), b_rows[:, m, :], ALU.add)
            ins.then_inc(ada_late, 1)
            dve.wait_ge(proj_dve, len([w for w in UNITS if w[3] == "dve"]))
            zs4 = z_s.rearrange("p c (b t) -> p c b t", b=NB)
            v_.tensor_copy(z_last[:, :, 0:2], z_p[:, :, SEQ:SEQ + 2])
            v_.tensor_copy(z_last[:, :, 2:18].rearrange("p c (b t) -> p c b t", b=NB), zs4[:, :, :, 8:10]
                           ).then_inc(zl_ready, 1)
            dve.wait_ge(zn_done, 1)
            v_.tensor_copy(z_nat[0:18, :], bank(6, 0, 256)[0:18]).then_inc(zn_ready, 1)

            dve.sem_inc(kt_dve, 1)

            def dve_turned(kt, b):
                for c in range(0, AC, 2):
                    w = 512 if kt < 2 else 256
                    dve.wait_ge(kt_done, b * 18 + kt * AC + c + 1)
                    v_.tensor_copy(kt_sb[:, c, 512 * kt:512 * kt + w], bank(key_bank(kt * AC + c), 0, w)).then_inc(kt_dve, 1)

            for kt in range(3):
                dve_turned(kt, 0)

            dve.wait_ge(pb_ready, 6)
            for s in range(HEADS + 1):
                if s < HEADS:
                    dve.wait_ge(ps_done, s + 1)
                    if s >= 3:
                        dve.wait_ge(pt_done, s - 2)
                    o = 4 * (s % 2)
                    v_.tensor_tensor_reduce(p_soft[:, s % 3, 0:128], bank(s % 2, 0, 128), p_bias[:, s, 128:256], 1.0,
                                            -3e38, ALU.add, ALU.max, st[:, o:o + 1])
                    V(v_.tensor_tensor_reduce(p_soft[:, s % 3, 128:384], bank(s % 2, 128, 384), p_bias[:, s, :], 1.0,
                                              -3e38, ALU.add, ALU.max, st[:, o + 1:o + 2]))
                    v_.tensor_scalar(st[:, o + 2:o + 4], st[:, o:o + 2], -1.0, None, ALU.mult).then_inc(pmax_ready, 1)
                if s >= 1:
                    h = s - 1
                    dve.wait_ge(pexp_ready, s)
                    r = 8 + 2 * (h % 2)
                    V(v_.reciprocal(st[:, r:r + 2], st[:, r:r + 2]))
                    v_.tensor_scalar(p_soft[:, h % 3, 0:128], p_soft[:, h % 3, 0:128], st[:, r:r + 1], None, ALU.mult)
                    v_.tensor_scalar(p_soft[:, h % 3, 128:384], p_soft[:, h % 3, 128:384], st[:, r + 1:r + 2], None,
                                     ALU.mult).then_inc(pnorm_ready, 1)
            def squares(g):
                a, z = ((0, SEQ), (SEQ, NTOK))[g]
                v_.tensor_tensor(sq_a[g], o_t[:, :, a:z], o_t[:, :, a:z], ALU.mult)
                v_.tensor_tensor(sq_c[g], y_c[:, :, a:z], y_c[:, :, a:z], ALU.mult).then_inc(sq_ready, 1)

            def mean_squares(g):
                a, z = ((0, SEQ), (SEQ, NTOK))[g]
                dve.wait_ge(ss_done, g + 1)
                v_.tensor_scalar(norm_rep[g][:, 0, :], bank(7, 0, z - a), 1.0 / DA, RMS_EPS, ALU.mult, ALU.add)
                v_.tensor_scalar(norm_rep[g][:, 1, :], bank(7, 256, 256 + z - a), 1.0 / DC, RMS_EPS, ALU.mult, ALU.add
                                 ).then_inc(var_ready, 1)

            def inverse_roots(g):
                dve.wait_ge(sd_ready, g + 1)
                V(v_.reciprocal(norm_rep[g], norm_rep[g]))

            def scale(g):
                a, z = ((0, SEQ), (SEQ, NTOK))[g]
                for c in range(AC):
                    v_.scalar_tensor_tensor(o_t[:, c, a:z], o_t[:, c, a:z], g_attn[:, c:c + 1], norm_rep[g][:, 0, :],
                                            ALU.mult, ALU.mult)
                for c in range(CC):
                    ins = v_.scalar_tensor_tensor(y_c[:, c, a:z], y_c[:, c, a:z], rows_t[:, c, 19:20],
                                                  norm_rep[g][:, 1, :], ALU.mult, ALU.mult)
                ins.then_inc(og_ready, 1)

            dve.wait_ge(proj_act, len([w for w in UNITS if w[3] == "act"]))
            for c in range(CC):
                wc = rows_t[:, c, 16:19]
                zs, cs = zs4[:, c], c_gate[:, c, SEQ:NTOK].rearrange("p (b t) -> p b t", b=NB)
                cp = c_gate[:, c, 0:SEQ]
                v_.tensor_scalar(cp, z_p[:, c, 0:SEQ], wc[:, 0:1], None, ALU.mult)
                V(v_.tensor_scalar(cs, zs[:, :, 0:8], wc[:, 0:1], None, ALU.mult))
                for w in (1, 2):
                    v_.scalar_tensor_tensor(cp, z_p[:, c, w:SEQ + w], wc[:, w:w + 1], cp, ALU.mult, ALU.add)
                    V(v_.scalar_tensor_tensor(cs, zs[:, :, w:w + 8], wc[:, w:w + 1], cs, ALU.mult, ALU.add))
                V(v_.tensor_tensor(y_c[:, c, :], y_c[:, c, :], c_gate[:, c, :], ALU.mult))
            dve.wait_ge(po_copied, AC)
            squares(0)
            dve.wait_ge(sb_done, 1)
            V(v_.tensor_copy(s_bias[0:96, :], ps[0:96, 0:SB]))
            dve.sem_inc(sb_ready, 1)
            mean_squares(0)

            dve.wait_ge(pt_done, HEADS)
            V(v_.memset(qbd, 0.0))
            dve.sem_inc(s_max, 1)

            def queries(cols):
                for par in range(2):
                    for half in range(2):
                        lo = 16 * par + 8 * half
                        ins = v_.tensor_copy(qbd[64 * half:64 * half + 64, par:AC:2, lo:lo + 8],
                                             q_t[64 * half:64 * half + 64, par:AC:2, cols])
                ins.then_inc(qbd_ready, 1)

            def keep_output(b):
                dve.wait_ge(so_done, b + 1)
                v_.tensor_copy(o_t[:, :, bass.ds(b * NS + SEQ, NS)], bank(7, 352, 400).rearrange("p (a b) -> p a b", a=AC)
                               ).then_inc(so_copied, 1)

            def dve_batch(b, first, more):
                dve.wait_ge(s_done, b + 1)
                at = b * -NS + SB - 64
                v_.scalar_tensor_tensor(prob[0:96, NCACHE:NCACHE + 64], ps[0:96, NCACHE:NCACHE + 64], 1.0,
                                        s_bias[0:96, bass.ds(at, 64)], ALU.mult, ALU.add)
                V(v_.tensor_tensor_reduce(prob[0:96, 0:NCACHE], ps[0:96, 0:NCACHE], s_bias[0:96, 0:NCACHE], 1.0, -3e38,
                                          ALU.add, ALU.max, st[0:96, 12:13]))
                V(v_.tensor_reduce(st[0:96, 13:14], prob[0:96, NCACHE:NCACHE + 64], AX.X, ALU.max))
                v_.tensor_scalar(st[0:96, 14:15], st[0:96, 12:13], st[0:96, 13:14], -1.0, ALU.max, ALU.mult
                                 ).then_inc(s_max, 1)
                if not first:
                    keep_output(b - 1)
                if more:
                    queries(bass.ds(b * NS + SEQ + NS, NS))
                    dve_turned(0, b + 1)
                    dve_turned(1, b + 1)
                dve.wait_ge(st_done, b * 3 + 2)
                v_.tensor_copy(pt_sb[:, 5:10, :], bank(6, 0, 480).rearrange("p (a b) -> p a b", a=5)).then_inc(st_dve, 1)
                dve.wait_ge(st_done, b * 3 + 3)
                v_.tensor_copy(pt_sb[0:64, KB, :], bank(7, 256, 352)[0:64]).then_inc(st_dve, 1)
                if more:
                    dve_turned(2, b + 1)
                dve.wait_ge(s_exp, b + 1)
                V(v_.reciprocal(st[0:96, 15:16], st[0:96, 15:16]))
                if not more:
                    scale(0)
                dve.wait_ge(sv_done, b + 1)
                v_.scalar_tensor_tensor(o_mask[0:96, :], bank(7, 0, 256)[0:96], st[0:96, 15:16], head_mask[0:96, :],
                                        ALU.mult, ALU.mult).then_inc(om_ready, 1)

            queries(slice(SEQ, SEQ + NS))
            dve_batch(0, True, True)
            with dve.Fori(1, NB - 1) as b:
                V.enter(b - 1, 3)
                dve_batch(b, False, True)
            V.leave(NB - 2)
            inverse_roots(0)
            dve_batch(NB - 1, False, False)
            keep_output(NB - 1)

            dve.wait_ge(so_copied, NB)
            dve.wait_ge(po_copied, AC)
            dve.wait_ge(out_kv, 96)
            squares(1)
            mean_squares(1)
            inverse_roots(1)
            scale(1)

            def residual(tt):
                n = TILES[tt][1]
                m, mod = mix[0:n, tt % 2, :], mod_p if tt < 2 else mod_s
                dve.wait_ge(mod_in, 144)
                dve.wait_ge(wo_done, tt + 1)
                V(v_.scalar_tensor_tensor(m, mod[0:n, 0, :], 1.0, ps[0:n, 1024 * tt:1024 * tt + 1024], ALU.add, ALU.mult))
                dve.wait_ge(tail_in, 64)
                x_t = x1[0:n, tt, :]
                V(v_.scalar_tensor_tensor(x_t, x_t, ALPHA, m, ALU.mult, ALU.add))
                layer_norm(dve, V, v_, x_t, n, st, ln1, var_ready, sd_ready, tt + 3, x_t)
                V(v_.scalar_tensor_tensor(u2[0:n, tt, :], mod[0:n, 2, :], 1.0, x_t, ALU.add, ALU.mult))
                V(v_.tensor_tensor(u2[0:n, tt, :], u2[0:n, tt, :], mod[0:n, 1, :], ALU.add))
                dve.sem_inc(u2_ready, 1)

            def route(tt):
                n = TILES[tt][1]
                dve.wait_ge(lg_done, tt + 1)
                V(v_.tensor_copy(lg[0:n, :], bank(6, 0, NE)[0:n]))
                V(v_.max(lead[0:n, :], lg[0:n, :]))
                v_.tensor_scalar(st[0:n, 40:41], lead[0:n, 0:1], -1.0, None, ALU.mult).then_inc(neg_ready, 1)
                V(v_.max_index(idx_u[0:n, :], lead[0:n, :], lg[0:n, :]))
                V(v_.tensor_copy(idx_f[0:n, :], idx_u[0:n, :]))
                mk = mask_t[0:n, tt, :]
                V(v_.tensor_scalar(mk, iota[0:n, 0:NE], idx_f[0:n, 0:1], None, ALU.is_equal))
                for j in range(1, 4):
                    V(v_.scalar_tensor_tensor(mk, iota[0:n, 0:NE], idx_f[0:n, j:j + 1], mk, ALU.is_equal, ALU.add))
                dve.wait_ge(ex_ready, tt + 1)
                V(v_.tensor_tensor_reduce(ex[0:n, :], ex[0:n, :], mk, 1.0, 0.0, ALU.mult, ALU.add, st[0:n, 41:42]))
                V(v_.reciprocal(st[0:n, 41:42], st[0:n, 41:42]))
                for r in range(ROUNDS):
                    v_.tensor_scalar(gate_t[0:n, tt, NE * r:NE * r + NE], ex[0:n, :], st[0:n, 41:42], None, ALU.mult)
                V(v_.memset(gate_t[0:n, tt, ITEMS:ITEMS + 1], 0.0))

            for step, tt in ((residual, 0), (residual, 1), (route, 0), (residual, 2), (route, 1), (route, 2)):
                step(tt)
            dve.sem_inc(masks_ready, 1)
            v_.memset(y_sb, 0.0)
            V(v_.memset(sel_t, 0.0))
            dve.wait_ge(rank_done, 1)
            for tt, (a, n) in enumerate(TILES):
                mk, rk = mask_t[0:n, tt, :], rank_t[0:n, tt, :]
                V(v_.scalar_tensor_tensor(rk[:, 0:NE], bank(7)[0:n, NE * tt:NE * tt + NE], FAR, mk, ALU.add, ALU.mult))
                V(v_.tensor_scalar(rk[:, 0:NE], rk[:, 0:NE], -FAR, None, ALU.add))
                for r in range(1, ROUNDS):
                    v_.tensor_scalar(rk[:, NE * r:NE * r + NE], rk[:, 0:NE], -128.0 * r, None, ALU.add)
                V(v_.memset(rk[:, ITEMS:ITEMS + 1], -FAR))

            def choose(i, which):
                for tt, (_, n) in enumerate(TILES):
                    if which == "sel":
                        ins = v_.tensor_scalar(sel[0:n, tt, :], iota[0:n, :], rank_t[0:n, tt, bass.ds(i, 1)], None,
                                               ALU.is_equal)
                    else:
                        ins = v_.tensor_scalar(
                            sel_g[0:n, tt].rearrange("p (v d) s -> p v d s", v=2),
                            iota[0:n, :].rearrange("p (v s) -> p v s", v=2).unsqueeze(2).to_broadcast([n, 2, 2, 64]),
                            rank_t[0:n, tt, bass.ds(i, 1)], gate_t[0:n, tt, bass.ds(i, 1)], ALU.is_equal, ALU.mult)
                return ins

            def add_back(tt, banks):
                n = TILES[tt][1]
                for h in range(2):
                    ins = v_.tensor_tensor(acc[0:n, tt, 512 * h:512 * h + 512], acc[0:n, tt, 512 * h:512 * h + 512],
                                           bank(banks[h])[0:n], ALU.add)
                return ins

            choose(0, "sel").then_inc(sel_ready, 1)
            V(v_.tensor_copy(cnt[0:1, :], bank(7)[0:1, NE * 3:NE * 4]))
            V(v_.tensor_reduce(st[0:1, 44:45], cnt[0:1, :], AX.X, ALU.max))
            V(v_.memset(flag_f[0:1, :], 0.0))
            for r in range(ROUNDS):
                v_.tensor_scalar(flag_f[0:1, 1 + NE * r:1 + NE * r + NE], cnt[0:1, :], 128.0 * r + 64.5, None, ALU.is_gt)
            V(v_.tensor_scalar(st[0:1, 45:46], st[0:1, 44:45], 128.5, float(NE), ALU.is_gt, ALU.mult))
            V(v_.tensor_scalar(st[0:1, 46:47], st[0:1, 44:45], 256.5, float(NE), ALU.is_gt, ALU.mult))
            V(v_.tensor_tensor(st[0:1, 45:46], st[0:1, 45:46], st[0:1, 46:47], ALU.add))
            V(v_.tensor_scalar(flag_f[0:1, 0:1], st[0:1, 45:46], float(NE), None, ALU.add))
            V(v_.tensor_copy(flag_i[0:1, :], flag_f[0:1, :]))
            dve.sem_inc(sc_added, 1)
            dve.sem_inc(route_ready, 1)

            def gathered_turned(blocks, turn_no):
                dve.wait_ge(gathered_turned_done, turn_no)
                for v in range(blocks):
                    ins = v_.tensor_copy(xe_t[:, v, :], bank(1 + 2 * v))
                ins.then_inc(xe_ready, 1)

            gathered_turned(2, 1)
            dve.wait_ge(acc_ready, 1)
            items = dve.value_load(flag_i[0:1, 0:1], min_val=NE, max_val=ITEMS)
            with dve.Fori(0, items) as i:
                V.enter(i, 4)
                now_b = dve.value_load(flag_i[0:1, bass.ds(i + 1, 1)], min_val=0, max_val=1)
                next_b = dve.value_load(flag_i[0:1, bass.ds(i + 2, 1)], min_val=0, max_val=1)
                dve.wait_ge(ga_done, i + 1)
                choose(i + 1, "sel").then_inc(sel_ready, 1)
                dve.wait_ge(selt_done, i + 1)
                choose(i, "gated").then_inc(selg_ready, 1)

                def swiglu(v):
                    v_.tensor_scalar(act_g[:, v, :], bank(2 * v), 7.0, None, ALU.min).then_inc(g_ready[v], 1)
                    V(v_.tensor_scalar(act_l[:, v, :], bank(2 * v + 1), 7.0, -7.0, ALU.min, ALU.max))
                    V(v_.scalar_tensor_tensor(act_l[:, v, :], act_l[:, v, :], 1.0, act_g[:, v, :], ALU.add, ALU.mult))
                    dve.wait_ge(sig_ready[v], i + 1)
                    v_.tensor_tensor(act_l[:, v, :], act_l[:, v, :], act_s[:, v, :], ALU.mult).then_inc(a_ready[v], 1)

                dve.wait_ge(up_used, i * KC + KC)
                swiglu(0)
                with dve.If(now_b > 0):
                    swiglu(1)
                with dve.Else():
                    dve.sem_inc(ch_v, 2)
                    dve.sem_inc(g_ready[1], 1)
                    dve.sem_inc(a_ready[1], 1)
                with dve.If(next_b > 0):
                    gathered_turned(2, i + 2)
                with dve.Else():
                    gathered_turned(1, i + 2)
                for tt in range(3):
                    dve.wait_ge(sc_done, i * 3 + tt + 1)
                    add_back(tt, ((6, 7), (4, 5), (6, 7))[tt]).then_inc(sc_added, 1)
            V.leave(items)
            V = Chain(dve, ch_end)

            def last_rows(tt):
                dve.wait_ge(sc_done, items * 3 + tt + 1)
                add_back(tt, ((6, 7), (4, 5), (2, 3))[tt]).then_inc(sc_added, 1)

            def finish(tt):
                n = TILES[tt][1]
                dve.wait_ge(sc_added, items * 3 + 2 + tt)
                dve.wait_ge(g2_done, tt + 1)
                at = 512 * (0, 6, 4)[tt]
                V(v_.scalar_tensor_tensor(fin_t[0:n], ps[0:n, at:at + 1024], 1.0, acc[0:n, tt, :], ALU.add, ALU.mult))
                V(v_.scalar_tensor_tensor(fin_t[0:n], x1[0:n, tt, :], ALPHA, fin_t[0:n], ALU.mult, ALU.add))
                layer_norm(dve, V, v_, fin_t[0:n], n, st, ln2, var_ready, sd_ready, 6 + tt, fin_y[0:n, tt, :])
                dve.sem_inc(y_done, 1)

            last_rows(0)
            last_rows(1)
            dve.wait_ge(ln2_in, 32)
            finish(0)
            last_rows(2)
            finish(1)
            finish(2)

        @block.tensor
        def _(pe):
            mm = nc.tensor.matmul

            def turn(o, i, n):
                return nc.tensor.transpose(o, i, ident[0:n, 0:n])

            pe.wait_ge(const_in, 16)
            pe.wait_ge(c_ready, 1)
            for k in range(KC):
                ins = turn(bank(7, 32 * k, 32 * k + 32), c_sb[0:32, 128 * k:128 * k + 128], 32)
            ins.then_inc(ct_done, 1)
            pe.wait_ge(rows_in, 64)
            for c in range(CC):
                turn(bank(6, 32 * c, 32 * c + 32), rows[0:32, 128 * c:128 * c + 128], 32)
            turn(bank(6, 64, 72), g_rows[0:8, :], 8).then_inc(rows_done, 1)
            pe.wait_ge(x_ready, 32)
            for c in range(KC):
                if c >= 2:
                    pe.wait_ge(xt_copied, c - 1)
                for tt, (a, n) in enumerate(TILES):
                    ins = turn(bank(4 + c % 2, a, a + n), x_in[0:n, tt, 128 * c:128 * c + 128], n)
                ins.then_inc(xt_done, 1)
            pe.wait_ge(tabc_in, 160)
            pe.wait_ge(ct_ready, 1)
            pe.wait_ge(rows_ready, 1)
            mm(bank(6, 0, 384)[0:HEADS], relb[0:32, :], tab_hot[0:32, :], start=True, stop=False)
            mm(bank(6, 0, 384)[0:HEADS], ones[0:1, 0:HEADS], tab_log[0:1, :], start=False, stop=True).then_inc(tab_done, 1)
            def ada(n):
                _, m, kp = RING[n]
                pe.wait_ge(ring_in[n % SLOTS], 16 * (n // SLOTS) + 16)
                for kk in range(2):
                    k = 2 * kp + kk
                    for j in range(4):
                        ins = mm(bank(ADA_BANK[m])[32 * j:32 * j + 32], c_t[:, k, :],
                                 ring_ada[n % SLOTS][:, kk, 512 * j:512 * j + 512],
                                 start=k == 0, stop=k == KC - 1, tile_position=(0, 32 * j))
                ins.then_inc(ada_used, 1)

            for n in range(4):
                ada(n)
            pe.wait_ge(ada_ready, 1)
            for cb in range(4):
                ins = turn(bank(3, 128 * cb, 128 * cb + 128), ada_sb[:, 0, 128 * cb:128 * cb + 128], 128)
            ins.then_inc(adat_done, 1)
            pe.wait_ge(tab_ready, 1)
            for n in range(4, len(RING)):
                if RING[n][0] == "ada":
                    ada(n)
                    continue
                block_lo, w = 512 * RING[n][1], ring_in_w[n % SLOTS]
                here = [u for u, unit in enumerate(UNITS) if block_lo <= unit[2] < block_lo + 512]
                pe.wait_ge(ring_in[n % SLOTS], 16 * (n // SLOTS) + 16)
                for u in here:
                    kind, c, col, eng = UNITS[u]
                    col -= block_lo
                    if u >= PB:
                        pe.wait_ge(proj_act if UNITS[u - PB][3] == "act" else proj_dve, copied(u - PB))
                    for k in range(KC):
                        if u == 0:
                            pe.wait_ge(u_ready, k + 1)
                        if kind == "v":
                            (a, m), cols = TILES[c[0]], VW[c[1]]
                            ins = mm(bank(u % PB)[0:m, 0:cols], u_t[:, k, a:a + m], w[:, k, col:col + cols],
                                     start=k == 0, stop=k == KC - 1)
                        else:
                            ins = mm(bank(u % PB)[:, 0:NTOK], w[:, k, col:col + 128], u_t[:, k, :],
                                     start=k == 0, stop=k == KC - 1)
                    ins.then_inc(proj_done, 1)
                    if kind == "k":
                        if c == 0:
                            pe.wait_ge(hb_in, 16)
                        if c >= 2:
                            pe.wait_ge(pb_ready, c - 1)
                        mm(bank(6 + c % 2), anti, hb[:, 2 * c:2 * c + 2, :], start=True, stop=True).then_inc(pb_done, 1)
                    if u in KN_AT:
                        tt = KN_AT[u]
                        a, m = TILES[tt]
                        if tt:
                            pe.wait_ge(kn_dve, tt)
                            pe.wait_ge(kn_act, tt)
                        else:
                            pe.wait_ge(proj_dve, copied(2 * AC - 1))
                            pe.wait_ge(pb_ready, 6)
                        for c in range(AC):
                            ins = turn(bank(6 + c // 4, 128 * (c % 4), 128 * (c % 4) + 128)[0:m], k_t[:, c, a:a + m], 128)
                        ins.then_inc(kn_done, 1)
            pe.wait_ge(zl_ready, 1)
            pe.wait_ge(kn_dve, 3)
            for c in range(CC):
                ins = turn(bank(6, 128 * c, 128 * c + 128)[0:18], z_last[:, c, :], 128)
            ins.then_inc(zn_done, 1)
            pe.wait_ge(zn_ready, 1)
            pe.wait_ge(proj_act, len([w for w in UNITS if w[3] == "act"]))
            pe.wait_ge(proj_dve, len([w for w in UNITS if w[3] == "dve"]))
            pe.wait_ge(ada_late, 1)

            def keys(kt, b):
                if kt == 0:
                    pe.wait_ge(k_rec_in, b * 16 + 16)
                if kt == 1:
                    pe.wait_ge(k_old_in, b * 128 + 128)
                nb = 4 if kt < 2 else 2
                for c in range(AC):
                    n = kt * AC + c
                    if n < 2 or n >= 4:
                        before = n if n < 2 else n - 2 if n < 14 else n
                        pe.wait_ge(kt_dve if c % 2 == 0 else kt_act, b * 9 + before // 2 + 1)
                    for j in range(nb):
                        ins = turn(bank(key_bank(n), 128 * j, 128 * j + 128),
                                   k_sb[:, 4 * kt + j, 128 * c:128 * c + 128], 128)
                    ins.then_inc(kt_done, 1)

            for kt in range(3):
                keys(kt, 0)
            pe.wait_ge(kt_dve, 10)
            pe.wait_ge(kt_act, 10)
            for s in range(HEADS + LAG):
                if s < HEADS:
                    c, lo = s // 2, 64 * (s % 2)
                    if s >= 2:
                        pe.wait_ge(pmax_ready, s - 1)
                    q, k = q_t[lo:lo + 64, c, :], k_t[lo:lo + 64, c, :]
                    mm(bank(s % 2, 0, 128), q[:, 0:128], k[:, 0:128], start=True, stop=True)
                    mm(bank(s % 2, 128, 384), q[:, 128:256], k[:, 0:256], start=True, stop=True).then_inc(ps_done, 1)
                if s >= LAG:
                    h = s - LAG
                    c, lo = h // 2, 64 * (h % 2)
                    pe.wait_ge(pt_copied, h + 1)
                    if h >= 4:
                        pe.wait_ge(po_copied, c - 1)
                    o = bank(4 + c % 2)[lo:lo + 64]
                    pt = p_turn[:, h % 2, :]
                    vv = v_nat[:, :, HD * h:HD * h + HD]
                    mm(o[:, 0:128], vv[:, 0], pt[:, 0:128], start=True, stop=True)
                    mm(o[:, 128:256], vv[:, 0], pt[:, 128:256], start=True, stop=False)
                    mm(o[:, 128:256], vv[:, 1], pt[:, 256:384], start=False, stop=True).then_inc(pv_done, 1)
                if 2 <= s <= HEADS + 1:
                    h = s - 2
                    pe.wait_ge(pnorm_ready, h + 1)
                    if h >= 2:
                        pe.wait_ge(pt_copied, h - 1)
                    for j in range(3):
                        ins = turn(bank(2 + h % 2, 128 * j, 128 * j + 128), p_soft[:, h % 3, 128 * j:128 * j + 128], 128)
                    ins.then_inc(pt_done, 1)
            def sums_of_squares(g):
                pe.wait_ge(sq_ready, g + 1)
                n = (SEQ, NTOK - SEQ)[g]
                for c in range(AC):
                    mm(bank(7, 0, n), ones, sq_a[g][:, c, :], start=c == 0, stop=c == AC - 1)
                for c in range(CC):
                    ins = mm(bank(7, 256, 256 + n), ones, sq_c[g][:, c, :], start=c == 0, stop=c == CC - 1)
                ins.then_inc(ss_done, 1)

            pe.wait_ge(hot_in, 64)
            pe.wait_ge(bsel_ready, 1)
            for a, z in ((0, 512), (512, 1024), (1024, SB)):
                for kc in range(2):
                    mm(ps[0:96, a:z], bias_sel[:, kc, :], hot_s[:, kc, a:z], start=kc == 0, stop=False)
                ins = mm(ps[0:96, a:z], log_sel[0:8, :], log_s[0:8, a:z], start=False, stop=True)
            ins.then_inc(sb_done, 1)
            sums_of_squares(0)
            pe.wait_ge(sb_ready, 1)
            pe.wait_ge(po_copied, AC)
            pe.wait_ge(pt_copied, HEADS)

            def scores(o, rhs):
                for c in (0, 2, 4, 1, 3, 5):
                    j = c // 2
                    ins = mm(o[32 * j:32 * j + 32], qbd[:, c, :], rhs(c), start=c % 2 == 0, stop=c % 2 == 1,
                             tile_position=(0, 32 * j))
                return ins

            def heads_apart(b):
                pe.wait_ge(om_ready, b + 1)
                for c in range(AC):
                    ins = mm(bank(7, 352 + 8 * c, 360 + 8 * c), o_mask[0:96, 128 * (c % 2):128 * (c % 2) + 128],
                             query_sum[0:96, c // 2, :], start=True, stop=True)
                ins.then_inc(so_done, 1)

            def pe_batch(b, first, more):
                pe.wait_ge(qbd_ready, b + 1)
                pe.wait_ge(s_max, b + 1)
                pe.wait_ge(kt_dve, b * 9 + 10)
                pe.wait_ge(kt_act, b * 9 + 10)
                scores(bank(0), lambda c: kt_sb[:, c, 0:512])
                scores(bank(1), lambda c: kt_sb[:, c, 512:1024])
                scores(bank(2, 0, 256), lambda c: kt_sb[:, c, 1024:NCACHE])
                scores(bank(2, 256, 320), lambda c: k_t[:, c, SEQ:NTOK]).then_inc(s_done, 1)
                if not first:
                    heads_apart(b - 1)
                if more:
                    keys(0, b + 1)
                    keys(1, b + 1)
                if not first:
                    pe.wait_ge(so_copied, b)
                pe.wait_ge(s_exp, b + 1)
                if more:
                    pe.wait_ge(kt_dve, b * 9 + 9 + 6 + 1)
                    pe.wait_ge(kt_act, b * 9 + 9 + 6 + 1)
                for j in range(KB + 1):
                    o = bank(5, 96 * j, 96 * j + 96) if j < 5 else (
                        bank(6, 96 * j - 480, 96 * j - 384) if j < KB else bank(7, 256, 352)[0:64])
                    ins = turn(o, prob[0:96, 128 * j:min(128 * j + 128, NCACHE + 64)], 96)
                    if j in (4, KB - 1, KB):
                        ins.then_inc(st_done, 1)
                if more:
                    keys(2, b + 1)
                pe.wait_ge(st_act, b + 1)
                pe.wait_ge(st_dve, b * 2 + 2)
                pe.wait_ge(v_in, b * 144 + 144)
                for j in range(KB + 1):
                    for g in range(3):
                        n = 128 if j < KB else 64
                        rhs = v_sb[:, j, 256 * g:256 * g + 256] if j < KB else v_nat[0:64, 2, 256 * g:256 * g + 256]
                        ins = mm(bank(7, 0, 256)[32 * g:32 * g + 32], pt_sb[0:n, j, 32 * g:32 * g + 32], rhs,
                                 start=j == 0, stop=j == KB, tile_position=(0, 32 * g))
                    if j == KB - 1:
                        ins.then_inc(v_used, 1)
                ins.then_inc(sv_done, 1)

            pe_batch(0, True, True)
            with pe.Fori(1, NB - 1) as b:
                pe_batch(b, False, True)
            pe_batch(NB - 1, False, False)
            heads_apart(NB - 1)

            pe.wait_ge(so_copied, NB)
            def output(tt):
                a, n = TILES[tt]
                for h in range(2):
                    for c in range(KC):
                        lhs = o_t[:, c, a:a + n] if c < AC else y_c[:, c - AC, a:a + n]
                        ins = mm(bank(2 * tt + h)[0:n], lhs, wo_sb[:, c, 512 * h:512 * h + 512],
                                 start=c == 0, stop=c == KC - 1)
                ins.then_inc(wo_done, 1)

            def router(tt):
                n = TILES[tt][1]
                pe.wait_ge(u2_ready, tt + 1)
                if tt:
                    pe.wait_ge(neg_ready, tt)
                for h in range(2):
                    for c in range(4):
                        ins = turn(bank(6 + h, 128 * c, 128 * c + n),
                                   u2[0:n, tt, 128 * (4 * h + c):128 * (4 * h + c) + 128], n)
                    ins.then_inc(u2t_done, 1)
                pe.wait_ge(u2t_ready, 2 * tt + 2)
                for k in range(KC):
                    mm(bank(6, 0, NE)[0:n], u2_t[:, k, 0:n], rw_sb[:, k, :], start=k == 0, stop=False)
                mm(bank(6, 0, NE)[0:n], ones[0:1, 0:n], rb_sb[0:1, :], start=False, stop=True).then_inc(lg_done, 1)

            pe.wait_ge(og_ready, 1)
            pe.wait_ge(wo_in, 16)
            output(0)
            sums_of_squares(1)
            output(1)
            router(0)
            pe.wait_ge(og_ready, 2)
            output(2)
            router(1)
            router(2)
            pe.wait_ge(masks_ready, 1)
            for tt, (a, n) in enumerate(TILES):
                for s in range(tt + 1):
                    m = TILES[s][1]
                    mm(bank(7, NE * tt, NE * tt + NE)[0:n], tri[0:m, 0:n] if s == tt else ones[0:m, 0:n],
                       mask_t[0:m, s, :], start=s == 0, stop=s == tt)
            for s in range(3):
                m = TILES[s][1]
                ins = mm(bank(7, NE * 3, NE * 4), ones[0:m, :], mask_t[0:m, s, :], start=s == 0, stop=s == 2)
            ins.then_inc(rank_done, 1)
            for tt, (a, n) in enumerate(TILES):
                ins = turn(bank(6, a, a + n)[0:NE], gate_t[0:n, tt, 0:NE], n)
            ins.then_inc(gt_done, 1)

            def gather(blocks):
                for v in range(blocks):
                    for tt, (_, n) in enumerate(TILES):
                        for h in range(2):
                            ins = mm(bank(4 + v)[64 * h:64 * h + 64], sel[0:n, tt, 64 * v:64 * v + 64],
                                     u2[0:n, tt, 512 * h:512 * h + 512], start=tt == 0, stop=tt == 2)
                ins.then_inc(ga_done, 1)

            def turn_gathered(blocks, turn_no):
                pe.wait_ge(xn_ready, turn_no)
                for v in range(blocks):
                    for c in range(4):
                        ins = turn(bank(1 + 2 * v, 128 * c, 128 * c + 128), xe_nat[:, v, 128 * c:128 * c + 128], 128)
                ins.then_inc(gathered_turned_done, 1)

            def scatter(tt, banks, blocks, more=False):
                for v in range(blocks):
                    for h in range(2):
                        ins = mm(bank(banks[h]), sel_t[64 * h:64 * h + 64, v, 128 * tt:128 * tt + 128],
                                 y_sb[64 * h:64 * h + 64, v, :], start=v == 0, stop=v == blocks - 1 and not more)
                return ins

            def last_scatter(blocks):
                for tt, banks in enumerate(((6, 7), (4, 5), (2, 3))):
                    a, n = TILES[tt]
                    scatter(tt, banks, blocks, more=True)
                    for h in range(2):
                        ins = mm(bank(banks[h])[0:n], gt_sb[0:NE, a:a + n], bd_sb[0:NE, 512 * h:512 * h + 512],
                                 start=False, stop=True)
                    ins.then_inc(sc_done, 1)

            def gate2(tt, b):
                n, lhs = TILES[tt][1], rep_p if tt < 2 else rep_s
                for h in range(2):
                    ins = mm(bank(b + h)[0:n], lhs[64 + 32 * h:96 + 32 * h, 0:n],
                             ada_sb[64 + 32 * h:96 + 32 * h, 2, :], start=True, stop=True)
                ins.then_inc(g2_done, 1)

            pe.sem_inc(selt_done, 1)
            pe.wait_ge(gt_ready, 1)
            pe.wait_ge(u2_ready, 3)
            pe.wait_ge(sel_ready, 1)
            gather(2)
            turn_gathered(2, 1)
            pe.wait_ge(route_ready, 1)
            items = pe.value_load(flag_i[0:1, 0:1], min_val=NE, max_val=ITEMS)
            with pe.Fori(0, items) as i:
                now_b = pe.value_load(flag_i[0:1, bass.ds(i + 1, 1)], min_val=0, max_val=1)
                last_b = pe.value_load(flag_i[0:1, bass.ds(i, 1)], min_val=0, max_val=ITEMS)
                next_b = pe.value_load(flag_i[0:1, bass.ds(i + 2, 1)], min_val=0, max_val=1)
                pe.wait_ge(xe_ready, i + 1)
                pe.wait_ge(bup_in, i * 16 + 16)

                def up_bias(v):
                    for part in range(2):
                        for h in range(2):
                            ins = mm(bank(2 * v + part)[64 * h:64 * h + 64], ones[0:1, 0:64],
                                     b_up[0:1, FF * part + 512 * h:FF * part + 512 * h + 512], start=True, stop=False)
                    return ins

                def up(blocks):
                    if blocks == 2:
                        pe.wait_ge(y_ready, i + 1)
                    for v in range(blocks):
                        ins = up_bias(v)
                    ins.then_inc(bup_used, 1)
                    for k in range(KC):
                        pe.wait_ge(up_in[k], i * 16 + 16)
                        for v in range(blocks):
                            for part in range(2):
                                for h in range(2):
                                    at = 128 * (k % 4) + 64 * (k // 4)
                                    ins = mm(bank(2 * v + part)[64 * h:64 * h + 64], xe_t[:, v, at:at + 64],
                                             up_w[:, k, FF * part + 512 * h:FF * part + 512 * h + 512],
                                             start=False, stop=k == KC - 1)
                        ins.then_inc(up_used, 1)

                with pe.If(now_b > 0):
                    up(2)
                with pe.Else():
                    up(1)
                pe.wait_ge(sel_ready, i + 2)
                pe.wait_ge(sc_added, i * 3 + 1)
                with pe.If(next_b > 0):
                    gather(2)
                with pe.Else():
                    gather(1)

                def turn_act(v):
                    pe.wait_ge(a_ready[v], i + 1)
                    for c in range(4):
                        ins = turn(bank(2 * v, 128 * c, 128 * c + 128), act_l[:, v, 128 * c:128 * c + 128], 128)
                    ins.then_inc(at_done[v], 1)

                def add_up(tts):
                    with pe.If(last_b > 0):
                        for tt in tts:
                            scatter(tt, ((6, 7), (4, 5), (6, 7))[tt], 2).then_inc(sc_done, 1)
                    with pe.Else():
                        for tt in tts:
                            scatter(tt, ((6, 7), (4, 5), (6, 7))[tt], 1).then_inc(sc_done, 1)

                pe.wait_ge(selt_ready, i + 1)
                pe.wait_ge(y_ready, i + 1)
                add_up((0,))
                turn_act(0)
                with pe.If(now_b > 0):
                    turn_act(1)
                with pe.Else():
                    pe.sem_inc(at_done[1], 1)
                with pe.If(next_b > 0):
                    turn_gathered(2, i + 2)
                with pe.Else():
                    turn_gathered(1, i + 2)
                add_up((1,))

                def down(blocks, ms):
                    for m in ms:
                        pe.wait_ge(dn_in[m], i * 16 + 16)
                        for kk in (2 * m, 2 * m + 1):
                            for v in range(blocks):
                                for h in range(2):
                                    lhs = a_t[:, v, 128 * (kk % 4) + 64 * (kk // 4):128 * (kk % 4) + 64 * (kk // 4) + 64]
                                    ins = mm(bank(3 - v)[64 * h:64 * h + 64], lhs,
                                             dn_w[:, kk, 512 * h:512 * h + 512], start=kk == 0, stop=kk == KC - 1)
                        ins.then_inc(dn_used, 1)

                pe.wait_ge(at_ready[0], i + 1)
                pe.wait_ge(xe_ready, i + 2)
                with pe.If(now_b > 0):
                    pe.wait_ge(at_ready[1], i + 1)
                    down(2, (0,))
                with pe.Else():
                    down(1, (0,))
                pe.wait_ge(sc_added, i * 3 + 2)
                add_up((2,))
                with pe.If(now_b > 0):
                    down(2, (1, 2, 3))
                with pe.Else():
                    down(1, (1, 2, 3))
                pe.wait_ge(sc_added, i * 3 + 4)
                pe.wait_ge(selg_ready, i + 1)
                for v in range(2):
                    for tt, (a, n) in enumerate(TILES):
                        ins = turn(bank(6 + v, a, a + n), sel_g[0:n, tt, 2 * v:2 * v + 2, :], n)
                ins.then_inc(selt_done, 1)
            last_b = pe.value_load(flag_i[0:1, bass.ds(items, 1)], min_val=0, max_val=ITEMS)

            gate2(0, 0)
            pe.wait_ge(late_in, 16)
            pe.wait_ge(selt_ready, items + 1)
            pe.wait_ge(y_ready, items + 1)
            with pe.If(last_b > 0):
                last_scatter(2)
            with pe.Else():
                last_scatter(1)
            for tt in (1, 2):
                pe.wait_ge(sc_added, items * 3 + 1 + tt)
                gate2(tt, (0, 6, 4)[tt])


def layer_norm(dve, V, v_, x, n, st, gb, var_ready, sd_ready, sd_count, y):
    for h in range(2):
        ins = v_.bn_stats(st[0:n, 20 + 6 * h:26 + 6 * h], x[:, 512 * h:512 * h + 512])
    V(ins)
    V(v_.bn_aggr(st[0:n, 32:34], st[0:n, 20:32]))
    v_.tensor_scalar(st[0:n, 35:36], st[0:n, 33:34], LN_EPS, None, ALU.add).then_inc(var_ready, 1)
    dve.wait_ge(sd_ready, sd_count)
    V(v_.reciprocal(st[0:n, 37:38], st[0:n, 36:37]))
    V(v_.scalar_tensor_tensor(x, x, st[0:n, 32:33], gb[0:n, 0, :], ALU.subtract, ALU.mult))
    V(v_.scalar_tensor_tensor(y, x, st[0:n, 37:38], gb[0:n, 1, :], ALU.mult, ALU.add))


_INS = ["x_prompt", "x_sample", "cache_k", "cache_v", "state_conv", "c_prompt", "c_sample", "w_ada", "b_ada", "w_in",
        "conv_w", "norm_attn_g", "norm_conv_g", "w_o", "ln1_g", "ln1_b", "rel_bias", "router_w", "router_b", "w_up",
        "b_up", "w_down", "b_down", "ln2_g", "ln2_b"]
_OUTS = [(1, SEQ, D), (NB, NS, D), (1, 1, SEQ, HEADS, HD), (1, 1, SEQ, HEADS, HD), (1, 1, 2, DC),
         (1, NB, NS, HEADS, HD), (1, NB, NS, HEADS, HD), (1, NB, 2, DC)]
BRANCHES = ((128, 1), (512, 4), (2048, 16))


def shape_constants():
    import math
    import numpy as np

    def bucket(dist):
        df = np.maximum(dist, 16).astype(np.float32)
        large = 16 + (np.log(df / np.float32(16)) / np.float32(math.log(2048 / 16)) * np.float32(16)).astype(np.int32)
        return np.where(dist < 16, dist, np.minimum(large, 31))

    def log_count(dist):
        n = sum(((dist >= 0) & (dist <= w) & (dist % d == 0)).astype(np.int32) for w, d in BRANCHES)
        return np.where(n > 0, np.log(np.maximum(n, 1)), -1e30).astype(np.float32)

    def one_hot(dist):
        return (np.arange(32)[:, None] == bucket(np.clip(dist, 0, 2048))[None, :]).astype(np.float32)

    out = {}
    consts = np.zeros((128, NCONST), np.float32)
    p, c = np.arange(128)[:, None], np.arange(128)[None, :]
    for name, m in (("ident", p == c), ("tri", p < c), ("iota", np.broadcast_to(c, (128, 128))),
                    ("ones", np.ones((128, 128))), ("rep_p", (p % 32 == 0) & (c >= 0)),
                    ("rep_s", p % 32 == 1 + c[:, 0:64] // NS)):
        at, n = CONSTS[name]
        consts[:, at:at + n] = m
    out["consts"] = consts
    out["anti"] = (p == 127 - c).astype(np.float32)
    dist = 255 - np.arange(384)
    out["tab_hot"] = one_hot(dist)
    out["tab_log"] = log_count(dist)[None, :]
    part = np.arange(128)
    pos = [PAST - REC + 4 * part + r for r in range(4)]
    pos += [16 * (16 * r + part % 16) + part // 16 for r in range(6)]
    pos = np.concatenate(pos + [np.full(WIN, -1)])
    hot, logs = [], []
    for q in range(NS):
        dist = PAST + q - pos
        key = np.arange(WIN) - (NB * NS - NS)
        d_new = np.where((key >= 0) & (key < NS), q - key, -1)
        dist[NCACHE:] = d_new
        hot.append(one_hot(dist))
        logs.append(log_count(dist))
    out["hot_s"] = np.concatenate(hot).astype(np.float32)
    out["log_s"] = np.stack(logs)
    row = np.arange(96)[:, None]
    out["log_sel"] = (np.arange(96)[None, :] % NS == np.arange(NS)[:, None]).astype(np.float32)
    out["head_mask"] = (np.arange(256)[None, :] // HD == (row // NS) % 4).astype(np.float32)
    col = np.arange(24)[None, :]
    out["query_sum"] = ((row // 32 == col // 8) & (row % NS == col % 8)).astype(np.float32)
    return out


def kernel(**inputs):
    import numpy as _np
    import concourse.bacc as _bacc
    from concourse import mybir as _mybir
    from concourse.bass_utils import run_bass_kernel_spmd as _run

    nc = _bacc.Bacc("TRN2", target_bir_lowering=False, num_devices=1)
    arrays, t = {}, {}
    for name, a in list((n, inputs[n]) for n in _INS) + list(shape_constants().items()):
        a = _np.ascontiguousarray(a)
        arrays[f"in_{name}"] = a
        t[name] = nc.dram_tensor(f"in_{name}", a.shape, _mybir.dt.from_np(a.dtype), kind="ExternalInput").ap()
    outs = [nc.dram_tensor(f"out_{i}", shape, F32, kind="ExternalOutput").ap() for i, shape in enumerate(_OUTS)]
    scratch = nc.dram_tensor("by_distance", (HEADS, 384), F32, kind="Internal").ap()
    vectors = nc.dram_tensor("adaln_vectors", (1 + NB, 2 * 2048), F32, kind="Internal").ap()
    layer_kernel(nc, t, outs, scratch, vectors)
    r = _run(nc, [arrays], core_ids=[0])
    return tuple(r.results[0][f"out_{i}"] for i in range(len(_OUTS)))
```
